# Optimizing a Trainium2 kernel written in Bass

```python
import jax, jax.numpy as jnp
from jax import lax
import numpy as np

D_MODEL = 1024
BATCH = 1
SEQ = 512
DEPTH = 2

N_A = DEPTH // 2
N_B = DEPTH - N_A
N_HEADS = 16
HEAD_DIM = D_MODEL // N_HEADS
CONV_W = 3
D_FF = 2816
Q_BLOCK = 128
EPS = 1e-6


def rmsnorm(x, g):
    xf = x.astype(jnp.float32)
    y = xf * lax.rsqrt(jnp.mean(xf * xf, axis=-1, keepdims=True) + EPS)
    return (y * g).astype(x.dtype)

def causal_dwconv(u, w):
    width = w.shape[0]
    s = u.shape[1]
    up = jnp.pad(u, ((0, 0), (width - 1, 0), (0, 0)))
    return sum(up[:, i:i + s] * w[i] for i in range(width))

def short_conv_mixer(xn, w_in, conv_w, w_out):
    proj = xn @ w_in
    b, c, h = jnp.split(proj, 3, axis=-1)
    u = causal_dwconv(c * h, conv_w)
    return (b * u) @ w_out

def conv_ffn(xn, w_up, conv_w, w_down):
    up = xn @ w_up
    a, g = jnp.split(up, 2, axis=-1)
    a = causal_dwconv(a, conv_w)
    return (jax.nn.silu(a) * g) @ w_down

def forgetting_attention(q, k, v, c):
    bsz, nh, s_len, hd = q.shape
    nb = s_len // Q_BLOCK
    scale = hd ** -0.5
    qb = q.reshape(bsz, nh, nb, Q_BLOCK, hd).transpose(2, 0, 1, 3, 4)
    cb = c.reshape(bsz, nh, nb, Q_BLOCK).transpose(2, 0, 1, 3)
    kpos = jnp.arange(s_len)

    def one_block(args):
        q_i, c_i, i = args
        s = jnp.einsum('bhqd,bhkd->bhqk', q_i, k, preferred_element_type=jnp.float32) * scale
        s = s + c_i[..., None] - c[:, :, None, :]
        qpos = i * Q_BLOCK + jnp.arange(Q_BLOCK)
        s = jnp.where(kpos[None, :] <= qpos[:, None], s, -jnp.inf)
        p = jax.nn.softmax(s, axis=-1)
        return jnp.einsum('bhqk,bhkd->bhqd', p.astype(v.dtype), v)

    o = lax.map(one_block, (qb, cb, jnp.arange(nb)))
    return o.transpose(1, 0, 3, 2, 4).reshape(bsz, s_len, nh * hd)

def first_inputs(seed: int = 0) -> dict:
    key = jax.random.key(seed)
    ks = jax.random.split(key, 17)
    f32 = jnp.float32
    out_scale = (2 * DEPTH) ** -0.5

    def nrm(k, shape, scale):
        return jax.random.normal(k, shape, f32) * scale

    def gain(k, shape):
        return 1.0 + 0.02 * jax.random.normal(k, shape, f32)

    x = nrm(ks[0], (BATCH, SEQ, D_MODEL), 1.0)
    attn_norm = gain(ks[1], (DEPTH, D_MODEL))
    ffn_norm = gain(ks[2], (DEPTH, D_MODEL))
    a_w_in = nrm(ks[3], (N_A, D_MODEL, 3 * D_MODEL), D_MODEL ** -0.5)
    a_conv = nrm(ks[4], (N_A, CONV_W, D_MODEL), CONV_W ** -0.5)
    a_w_out = nrm(ks[5], (N_A, D_MODEL, D_MODEL), out_scale * D_MODEL ** -0.5)
    kv_norm = gain(ks[6], (D_MODEL,))
    w_kvf = jnp.concatenate([
        nrm(ks[7], (D_MODEL, 2 * D_MODEL), D_MODEL ** -0.5),
        nrm(ks[8], (D_MODEL, N_HEADS), 0.1 * D_MODEL ** -0.5),
    ], axis=1)
    b_f = jax.random.uniform(ks[9], (N_HEADS,), f32, 1.0, 6.0)
    k_norm = gain(ks[10], (HEAD_DIM,))
    b_w_qg = nrm(ks[11], (N_B, D_MODEL, 2 * D_MODEL), D_MODEL ** -0.5)
    q_norm = gain(ks[12], (N_B, HEAD_DIM))
    b_w_out = nrm(ks[13], (N_B, D_MODEL, D_MODEL), out_scale * D_MODEL ** -0.5)
    ffn_w_up = nrm(ks[14], (DEPTH, D_MODEL, 2 * D_FF), D_MODEL ** -0.5)
    ffn_conv = nrm(ks[15], (DEPTH, CONV_W, D_FF), CONV_W ** -0.5)
    ffn_w_down = nrm(ks[16], (DEPTH, D_FF, D_MODEL), out_scale * D_FF ** -0.5)
    return {"x": x, "attn_norm": attn_norm, "ffn_norm": ffn_norm,
            "a_w_in": a_w_in, "a_conv": a_conv, "a_w_out": a_w_out,
            "kv_norm": kv_norm, "w_kvf": w_kvf, "b_f": b_f, "k_norm": k_norm,
            "b_w_qg": b_w_qg, "q_norm": q_norm, "b_w_out": b_w_out,
            "ffn_w_up": ffn_w_up, "ffn_conv": ffn_conv, "ffn_w_down": ffn_w_down}

def first_block(x, attn_norm, ffn_norm, a_w_in, a_conv, a_w_out, kv_norm, w_kvf, b_f,
              k_norm, b_w_qg, q_norm, b_w_out, ffn_w_up, ffn_conv, ffn_w_down):
    bsz, s_len, d = x.shape
    k = v = c = None
    for l in range(DEPTH):
        if l < N_A:
            xn = rmsnorm(x, attn_norm[l])
            x = x + short_conv_mixer(xn, a_w_in[l], a_conv[l], a_w_out[l])
        else:
            if l == N_A:
                h = rmsnorm(x, kv_norm)
                kvf = h @ w_kvf
                k_s = kvf[..., :d].reshape(bsz, s_len, N_HEADS, HEAD_DIM)
                v_s = kvf[..., d:2 * d].reshape(bsz, s_len, N_HEADS, HEAD_DIM)
                f_logit = (kvf[..., 2 * d:] + b_f).astype(jnp.float32)
                k = rmsnorm(k_s, k_norm).transpose(0, 2, 1, 3)
                v = v_s.transpose(0, 2, 1, 3)
                c = jnp.cumsum(jax.nn.log_sigmoid(f_logit), axis=1).transpose(0, 2, 1)
            j = l - N_A
            xn = rmsnorm(x, attn_norm[l])
            qg = xn @ b_w_qg[j]
            q = rmsnorm(qg[..., :d].reshape(bsz, s_len, N_HEADS, HEAD_DIM), q_norm[j])
            q = q.transpose(0, 2, 1, 3)
            o = forgetting_attention(q, k, v, c)
            o = o * jax.nn.sigmoid(qg[..., d:])
            x = x + o @ b_w_out[j]
        xn = rmsnorm(x, ffn_norm[l])
        x = x + conv_ffn(xn, ffn_w_up[l], ffn_conv[l], ffn_w_down[l])
    return x


DEPTH_2 = 1

GLA_HEADS = 4
GLA_DK = D_MODEL // 2 // GLA_HEADS
GLA_DV = D_MODEL // GLA_HEADS
GLA_QK_W = GLA_HEADS * GLA_DK
GLA_V_W = GLA_HEADS * GLA_DV
GLA_GATE_RANK = 16
GLA_GATE_NORMALIZER = 16.0
GLA_LOG_GATE_MIN = -0.5
GLA_CHUNK = 64
SWA_HEADS = 8
SWA_KV_HEADS = 2
SWA_HEAD_DIM = 128
SWA_Q_W = SWA_HEADS * SWA_HEAD_DIM
SWA_KV_W = SWA_KV_HEADS * SWA_HEAD_DIM
SWA_WINDOW = 128
SWA_BLOCK = 128
ROPE_THETA = 10000.0
D_FF_2 = -(-8 * D_MODEL // (3 * 256)) * 256
NORM_EPS = 1e-6
IN_SPLITS = (GLA_QK_W, GLA_QK_W, GLA_V_W, GLA_V_W, GLA_GATE_RANK, GLA_GATE_RANK,
             SWA_Q_W, SWA_KV_W, SWA_KV_W, D_MODEL, D_MODEL)
D_IN = sum(IN_SPLITS)


def _rms_norm(x, g):
    xf = x.astype(jnp.float32)
    y = xf * lax.rsqrt(jnp.mean(xf * xf, axis=-1, keepdims=True) + NORM_EPS)
    return (y * g.astype(jnp.float32)).astype(x.dtype)

def _rope(x, pos):
    half = x.shape[-1] // 2
    inv_freq = ROPE_THETA ** (-jnp.arange(half, dtype=jnp.float32) / half)
    ang = pos.astype(jnp.float32)[:, None] * inv_freq[None, :]
    cos = jnp.cos(ang)[None, :, None, :]
    sin = jnp.sin(ang)[None, :, None, :]
    x1, x2 = x[..., :half], x[..., half:]
    return jnp.concatenate([x1 * cos - x2 * sin, x2 * cos + x1 * sin], axis=-1)

def _gla_direction(q, k, v, log_g, include_diag):
    bsz, nh, s, dk = q.shape
    dv = v.shape[-1]
    c = GLA_CHUNK
    n = s // c
    q = q.reshape(bsz, nh, n, c, dk)
    k = k.reshape(bsz, nh, n, c, dk)
    log_g = log_g.reshape(bsz, nh, n, c, dk)
    v = v.reshape(bsz, nh, n, c, dv)
    b = jnp.cumsum(log_g, axis=3)
    b_last = b[:, :, :, -1:, :]
    q_dec = q * jnp.exp(b)
    k_inv = k * jnp.exp(-b)
    k_tail = k * jnp.exp(b_last - b)
    mask = jnp.tril(jnp.ones((c, c), dtype=bool), k=0 if include_diag else -1)
    scores = jnp.where(mask, jnp.einsum("bhncd,bhnmd->bhncm", q_dec, k_inv), 0.0)
    o_intra = jnp.einsum("bhncm,bhnme->bhnce", scores, v)
    chunk_kv = jnp.einsum("bhnmd,bhnme->nbhde", k_tail, v)
    chunk_decay = jnp.exp(jnp.moveaxis(b_last[:, :, :, 0, :], 2, 0))

    def step(state, inp):
        kv_n, dec_n = inp
        return dec_n[..., None] * state + kv_n, state

    _, states = lax.scan(step, jnp.zeros((bsz, nh, dk, dv), q.dtype), (chunk_kv, chunk_decay))
    o_inter = jnp.einsum("bhncd,nbhde->bhnce", q_dec, states)
    return (o_intra + o_inter).reshape(bsz, nh, s, dv)

def _gla_branch(q, k, v, r, lr_f, lr_b, up_f, bias_f, up_b, bias_b, out_g):
    bsz, s, _ = q.shape
    f32 = jnp.float32

    def heads(t, d):
        return t.astype(f32).reshape(bsz, s, GLA_HEADS, d).transpose(0, 2, 1, 3)

    def log_gate(lr, up, bias):
        z = lr.astype(f32) @ up.astype(f32) + bias.astype(f32)
        lg = jnp.maximum(jax.nn.log_sigmoid(z) / GLA_GATE_NORMALIZER, GLA_LOG_GATE_MIN)
        return heads(lg, GLA_DK)

    qh = heads(q, GLA_DK) * (GLA_DK ** -0.5)
    kh = heads(k, GLA_DK)
    vh = heads(v, GLA_DV)
    o_fwd = _gla_direction(qh, kh, vh, log_gate(lr_f, up_f, bias_f), True)
    flip = lambda t: jnp.flip(t, axis=2)
    o_bwd = flip(_gla_direction(flip(qh), flip(kh), flip(vh),
                                flip(log_gate(lr_b, up_b, bias_b)), False))
    o = _rms_norm(o_fwd + o_bwd, out_g)
    o = o.transpose(0, 2, 1, 3).reshape(bsz, s, GLA_V_W)
    return (o * jax.nn.silu(r.astype(f32))).astype(q.dtype)

def _swa_branch(q, k, v, q_g, k_g, sinks):
    bsz, s, _ = q.shape
    f32 = jnp.float32
    hd, hkv, blk = SWA_HEAD_DIM, SWA_KV_HEADS, SWA_BLOCK
    grp = SWA_HEADS // SWA_KV_HEADS
    n = s // blk
    pos = jnp.arange(s)
    q = _rope(_rms_norm(q.astype(f32).reshape(bsz, s, SWA_HEADS, hd), q_g), pos)
    k = _rope(_rms_norm(k.astype(f32).reshape(bsz, s, hkv, hd), k_g), pos)
    v = v.astype(f32).reshape(bsz, s, hkv, hd)

    def context(t):
        tp = jnp.pad(t, ((0, 0), (blk, blk), (0, 0), (0, 0)))
        return jnp.concatenate(
            [tp[:, o * blk:o * blk + s].reshape(bsz, n, blk, hkv, hd) for o in range(3)], axis=2)

    kc, vc = context(k), context(v)
    qb = q.reshape(bsz, n, blk, hkv, grp, hd)
    scores = jnp.einsum("bnqhgd,bnkhd->bnhgqk", qb, kc) * (hd ** -0.5)
    q_off = jnp.arange(blk)
    k_off = jnp.arange(3 * blk) - blk
    in_window = jnp.abs(k_off[None, :] - q_off[:, None]) <= SWA_WINDOW
    k_abs = jnp.arange(n)[:, None] * blk + k_off[None, :]
    in_seq = (k_abs >= 0) & (k_abs < s)
    mask = in_window[None, :, :] & in_seq[:, None, :]
    scores = jnp.where(mask[None, :, None, None], scores, -jnp.inf)
    sink = sinks.astype(f32).reshape(1, 1, hkv, grp, 1, 1)
    m = jnp.maximum(scores.max(axis=-1, keepdims=True), sink)
    p = jnp.exp(scores - m)
    denom = p.sum(axis=-1, keepdims=True) + jnp.exp(sink - m)
    o = jnp.einsum("bnhgqk,bnkhd->bnqhgd", p / denom, vc)
    return o.reshape(bsz, s, SWA_Q_W)

def second_inputs(seed: int = 0) -> dict:
    key = jax.random.key(seed)
    ks = jax.random.split(key, 20)
    f32 = jnp.float32
    nrm = lambda k, shape, scale: jax.random.normal(k, shape, f32) * scale
    gain = lambda k, d: 1.0 + 0.02 * jax.random.normal(k, (DEPTH_2, d), f32)
    return {
        "x": nrm(ks[0], (BATCH, SEQ, D_MODEL), 1.0),
        "norm_mix_g": gain(ks[1], D_MODEL),
        "w_in": nrm(ks[2], (DEPTH_2, D_MODEL, D_IN), D_MODEL ** -0.5),
        "gla_gate_up_fwd": nrm(ks[3], (DEPTH_2, GLA_GATE_RANK, GLA_QK_W), GLA_GATE_RANK ** -0.5),
        "gla_gate_bias_fwd": nrm(ks[4], (DEPTH_2, GLA_QK_W), 0.02),
        "gla_gate_up_bwd": nrm(ks[5], (DEPTH_2, GLA_GATE_RANK, GLA_QK_W), GLA_GATE_RANK ** -0.5),
        "gla_gate_bias_bwd": nrm(ks[6], (DEPTH_2, GLA_QK_W), 0.02),
        "gla_out_norm_g": gain(ks[7], GLA_DV),
        "w_o_gla": nrm(ks[8], (DEPTH_2, GLA_V_W, D_MODEL), GLA_V_W ** -0.5),
        "swa_q_norm_g": gain(ks[9], SWA_HEAD_DIM),
        "swa_k_norm_g": gain(ks[10], SWA_HEAD_DIM),
        "swa_sinks": nrm(ks[11], (DEPTH_2, SWA_HEADS), 0.5),
        "w_o_swa": nrm(ks[12], (DEPTH_2, SWA_Q_W, D_MODEL), SWA_Q_W ** -0.5),
        "w_out": nrm(ks[13], (DEPTH_2, D_MODEL, D_MODEL), D_MODEL ** -0.5),
        "norm_ffn_g": gain(ks[14], D_MODEL),
        "w_ffn_in": nrm(ks[15], (DEPTH_2, D_MODEL, 2 * D_FF_2), D_MODEL ** -0.5),
        "w_ffn_out": nrm(ks[16], (DEPTH_2, D_FF_2, D_MODEL), D_FF_2 ** -0.5),
    }

def second_block(x, norm_mix_g, w_in, gla_gate_up_fwd, gla_gate_bias_fwd, gla_gate_up_bwd,
              gla_gate_bias_bwd, gla_out_norm_g, w_o_gla, swa_q_norm_g, swa_k_norm_g,
              swa_sinks, w_o_swa, w_out, norm_ffn_g, w_ffn_in, w_ffn_out):
    split_at = tuple(int(i) for i in np.cumsum(IN_SPLITS)[:-1])
    for l in range(DEPTH_2):
        h = _rms_norm(x, norm_mix_g[l])
        proj = h @ w_in[l]
        (g_q, g_k, g_v, g_r, g_lr_f, g_lr_b,
         s_q, s_k, s_v, gate_a, gate_b) = jnp.split(proj, split_at, axis=-1)
        y_gla = _gla_branch(g_q, g_k, g_v, g_r, g_lr_f, g_lr_b,
                            gla_gate_up_fwd[l], gla_gate_bias_fwd[l],
                            gla_gate_up_bwd[l], gla_gate_bias_bwd[l],
                            gla_out_norm_g[l]) @ w_o_gla[l]
        y_swa = _swa_branch(s_q, s_k, s_v, swa_q_norm_g[l], swa_k_norm_g[l],
                            swa_sinks[l]).astype(x.dtype) @ w_o_swa[l]
        merged = jax.nn.sigmoid(gate_a) * y_gla + jax.nn.sigmoid(gate_b) * y_swa
        x = x + merged @ w_out[l]
        h2 = _rms_norm(x, norm_ffn_g[l])
        gu = h2 @ w_ffn_in[l]
        ff_gate, ff_up = gu[..., :D_FF_2], gu[..., D_FF_2:]
        x = x + (jax.nn.silu(ff_gate) * ff_up) @ w_ffn_out[l]
    return x


def setup_inputs(seed=0):
    out = dict(first_inputs(seed))
    for name, value in second_inputs(seed + 1).items():
        if name != "x":
            out[name + "_2"] = value
    return out


def reference(
    x, attn_norm, ffn_norm, a_w_in, a_conv, a_w_out, kv_norm, w_kvf, b_f, k_norm, b_w_qg,
    q_norm, b_w_out, ffn_w_up, ffn_conv, ffn_w_down, norm_mix_g_2, w_in_2, gla_gate_up_fwd_2,
    gla_gate_bias_fwd_2, gla_gate_up_bwd_2, gla_gate_bias_bwd_2, gla_out_norm_g_2, w_o_gla_2,
    swa_q_norm_g_2, swa_k_norm_g_2, swa_sinks_2, w_o_swa_2, w_out_2, norm_ffn_g_2, w_ffn_in_2,
    w_ffn_out_2,
):
    x = first_block(
        x, attn_norm, ffn_norm, a_w_in, a_conv, a_w_out, kv_norm, w_kvf, b_f, k_norm, b_w_qg,
        q_norm, b_w_out, ffn_w_up, ffn_conv, ffn_w_down,
    )
    return second_block(
        x, norm_mix_g_2, w_in_2, gla_gate_up_fwd_2, gla_gate_bias_fwd_2, gla_gate_up_bwd_2,
        gla_gate_bias_bwd_2, gla_out_norm_g_2, w_o_gla_2, swa_q_norm_g_2, swa_k_norm_g_2,
        swa_sinks_2, w_o_swa_2, w_out_2, norm_ffn_g_2, w_ffn_in_2, w_ffn_out_2,
    )


_drawn_inputs = setup_inputs


def setup_inputs(seed=0):
    import zlib

    import numpy as np

    out = dict(_drawn_inputs(seed))
    spreads = {}
    factors = {'attn_norm': 2.751,
     'ffn_norm': 4.208,
     'kv_norm': 8.0,
     'k_norm': 8.0,
     'q_norm': 8.0,
     'norm_mix_g_2': 4.615,
     'gla_gate_bias_fwd_2': 8.0,
     'gla_gate_up_bwd_2': 2.685,
     'gla_gate_bias_bwd_2': 64.0,
     'gla_out_norm_g_2': 27.096,
     'swa_q_norm_g_2': 23.423,
     'swa_k_norm_g_2': 23.124,
     'swa_sinks_2': 8.0,
     'norm_ffn_g_2': 16.435}
    for name, (base, spread) in spreads.items():
        noise = np.random.default_rng([zlib.crc32(name.encode()), seed]).standard_normal(out[name].shape)
        drawn = base * np.exp(spread * noise) if base else spread * noise
        out[name] = __import__('jax').numpy.asarray(drawn.astype(out[name].dtype))
    for name, factor in factors.items():
        out[name] = (out[name] * factor).astype(out[name].dtype)
    return out
```

```python
from contextlib import ExitStack

import numpy as np

import concourse.bass as bass
from concourse import mybir

F32 = mybir.dt.float32
F32R = mybir.dt.float32r
BF16 = mybir.dt.bfloat16
ACT = mybir.ActivationFunctionType
ALU = mybir.AluOpType
AX = mybir.AxisListType

P = 128
S = 512
D = 1024
KT = D // P
TB = S // P
FF = 2816
FT = FF // P
EPS = 1e-6
NEG = -1e30

HEADS = 16
HD = D // HEADS
PAIRS = HEADS // 2

GH = 4
GDK = 128
CH = 64
NCH = S // CH
GATE_RANK = 16
SWA_GROUPS = 2
SWA_Q = 4
G_Q, G_K, G_V, G_R, G_LR = 0, 512, 1024, 2048, 3072
S_Q, S_K, S_V, GA, GB = 3104, 4128, 4384, 4640, 5664

(R_ATTN, R_FFN, R_KV, R_MIX, R_FFN2, R_ACONV, R_GBF, R_GBB, R_OUTG, R_SQG, R_SKG, R_QN, R_KN,
 R_BF) = (0, 16, 32, 40, 48, 56, 80, 84, 88, 90, 91, 92, 93, 94)
N_PRM = 96
N_FC = 3 * FT
C_ID, C_ONE, C_ONE64, C_CAUSAL, C_UPPER, C_GF, C_GB, C_COS = 0, 128, 256, 384, 512, 640, 768, 896
C_SIN = C_COS + S
N_CONST = C_SIN + S


class WeightPhase:

    def __init__(self, stream, ring, iters, units):
        self.ring, self.iters, self.units, self.U = ring, iters, units, len(units)
        assert iters == 1 or self.U % ring == 0
        self.base = stream["units"]
        self.owner = list(stream["owner"])
        self.loads0 = list(stream["loads"])
        stream["units"] += self.U * iters
        for n in range(self.U * iters):
            s = (n % self.U) % ring
            stream["owner"][s] = self.base + n
            stream["loads"][s] += 1

    def unit(self, i, j):
        return i * self.U + (self.base + j)

    def slot(self, j):
        return j % self.ring

    def load_count(self, i, j):
        return i * (self.U // self.ring if self.iters > 1 else 0) + (self.loads0[self.slot(j)] + j // self.ring + 1)

    def before(self, i, j):
        if j >= self.ring or not isinstance(i, int) or i > 0:
            return i * self.U + (self.base + j - self.ring + 1)
        last = self.owner[self.slot(j)]
        return None if last is None else last + 1


class Steps:

    def __init__(self, engine, sem):
        self.engine, self.sem = engine, sem
        self.base, self.n, self.i, self.stride, self.start = 0, 0, 0, None, 0

    def enter_loop(self, start):
        self.base, self.n, self.i, self.stride, self.start = self.base + self.n, 0, 0, None, start

    def enter(self, i):
        self.i, self.n = i, 0

    def leave_iteration(self):
        if self.stride is None:
            self.stride = self.n
        assert self.stride == self.n

    def leave_loop(self, iters):
        self.base += (self.stride or 0) * iters
        self.i, self.n, self.stride, self.start = 0, 0, None, 0

    def value(self):
        if isinstance(self.i, int):
            return self.base + self.n + (self.i - self.start) * (self.stride or 0)
        return self.i * self.stride + (self.base + self.n - self.start * self.stride)

    def link(self, ins):
        self.n += 1
        ins.then_inc(self.sem, 1)
        self.engine.wait_ge(self.sem, self.value())


def loop(engine, iters, body, steps=None, start=0):
    def one(i):
        if steps:
            steps.enter(i)
        body(i)
        if steps:
            steps.leave_iteration()
    if steps:
        steps.enter_loop(start)
    one(start)
    if iters > start + 1:
        with engine.Fori(start + 1, iters) as i:
            one(i)
    if steps:
        steps.leave_loop(iters - start)


def build(nc, T, out, stop=99):
    with ExitStack() as ctx:
        sems = {}

        def sem(name):
            if name not in sems:
                sems[name] = ctx.enter_context(nc.semaphore(name))
            return sems[name]

        pos = [(nc.sbuf_base + 31) // 32 * 32]

        def at(name, shape, dt, offset=None):
            size = int(np.prod(shape[1:])) * (2 if dt == BF16 else 4)
            if offset is None:
                offset = pos[0]
                pos[0] += (size + 31) // 32 * 32
            return nc.alloc_sbuf_tensor_at(name, shape, dt, offset=offset)

        XT = at("XT", [P, KT, S], F32)
        XH = at("XH", [P, KT, S], F32R)
        XL = at("XL", [P, KT, S], F32R)
        RAW = [at(f"RAW{s}", [P, KT, P], F32) for s in range(4)]
        ring_at = []
        WH, WL = [], []
        for s in range(4):
            ring_at.append(pos[0])
            WH.append(at(f"WH{s}", [P, KT, P], F32R))
            WL.append(at(f"WL{s}", [P, KT, P], F32R))
        W_at = []
        W = []
        for s in range(10):
            W_at.append(pos[0])
            W.append(at(f"W{s}", [P, S + 8], F32))
        IDF = at("IDF", [P, P], F32)
        ONE = at("ONE", [P, P], F32)
        ONE64 = at("ONE64", [P, P], F32)
        IDB = at("IDB", [P, P], BF16)
        MCAUSAL = at("MCAUSAL", [P, P], BF16)
        MUPPER = at("MUPPER", [P, P], BF16)
        PRM = at("PRM", [P, N_PRM], F32)
        FC = at("FC", [P, 2 * N_FC], F32)
        SINK = at("SINK", [P, 8], F32)
        COL = at("COL", [P, 32], F32)
        EPSC, ONEC, TICK = COL[:, 0:1], COL[:, 1:2], COL[:, 2:3]
        NEGM, RS, RINV, ESK = COL[:, 4:8], COL[:, 8:12], COL[:, 12:16], COL[:, 16:20]
        BIG = pos[0]
        assert BIG + 2 * FT * S * 4 <= nc.sbuf_usable_end, (BIG, nc.sbuf_usable_end)
        KB = 1024
        XIN = at("XIN", [P, TB, D], F32, BIG)
        PROW = at("PROW", [P, 3, P], F32, BIG + 16 * KB)
        CST = at("CST", [P, C_GF], F32, BIG + 18 * KB)
        BUH = at("BUH", [P, KT, S], F32R, BIG + 32 * KB)
        BUL = at("BUL", [P, KT, S], F32R, BIG + 48 * KB)
        HH = at("HH", [P, FT, S], F32R, BIG)
        HL = at("HL", [P, FT, S], F32R, BIG + 44 * KB)
        X2H = at("X2H", [P, KT, S], F32R, BIG)
        X2L = at("X2L", [P, KT, S], F32R, BIG + 16 * KB)
        OH = at("OH", [P, KT, S], F32R, BIG + 32 * KB)
        OL = at("OL", [P, KT, S], F32R, BIG + 48 * KB)
        KH, KL, QH, QL = [at(n, [P, S], F32R, BIG + (64 + 2 * k) * KB) for k, n in enumerate(("KH", "KL", "QH", "QL"))]
        VH = at("VH", [P, TB, P], F32R, BIG + 72 * KB)
        VL = at("VL", [P, TB, P], F32R, BIG + 74 * KB)
        PTH = [at(f"PTH{k}", [P, S], F32R, BIG + (76 + 2 * k) * KB) for k in range(2)]
        PTL = [at(f"PTL{k}", [P, S], F32R, BIG + (80 + 2 * k) * KB) for k in range(2)]
        PQ = at("PQ", [P, 6 * P], F32, BIG + 84 * KB)
        CT = at("CT", [P, TB, HEADS], F32, BIG + 87 * KB)
        PROB = [PQ[:, 0:128], PQ[:, 128:384], PQ[:, 384:768], W[7][:, 0:S]]

        YGH = at("YGH", [P, KT, S], F32R, BIG)
        YGL = at("YGL", [P, KT, S], F32R, BIG + 16 * KB)
        BC = at("BC", [P, 2 * GH, S], F32, BIG + 32 * KB)
        QDH, QDL, KIH, KIL, KTH, KTL = [at(n, [P, S], F32R, BIG + (48 + 2 * k) * KB)
                                        for k, n in enumerate(("QDH", "QDL", "KIH", "KIL", "KTH", "KTL"))]
        VGH = at("VGH", [P, TB, 2 * P], F32R, BIG + 60 * KB)
        VGL = at("VGL", [P, TB, 2 * P], F32R, BIG + 64 * KB)
        SH = at("SH", [P, NCH - 1, 2 * P], F32R, BIG + 68 * KB)
        SL = at("SL", [P, NCH - 1, 2 * P], F32R, BIG + 75 * KB)
        ST = [at(f"ST{k}", [P, 2 * P], F32, BIG + (82 + k) * KB) for k in range(2)]
        SCH = at("SCH", [P, S], F32R, BIG + 84 * KB)
        SCL = at("SCL", [P, S], F32R, BIG + 86 * KB)
        UP = at("UP", [2 * GATE_RANK, 2 * GH * GDK], F32, BIG + 68 * KB)
        GMASK = [W[9][:, 0:P], W[9][:, P:2 * P]]
        EBL = W[9][:, 2 * P:2 * P + NCH]
        YSH = at("YSH", [P, KT, S], F32R, BIG + 32 * KB)
        YSL = at("YSL", [P, KT, S], F32R, BIG + 48 * KB)
        SKH, SKL = [at(n, [P, S], F32R, BIG + (64 + 2 * k) * KB) for k, n in enumerate(("SKH", "SKL"))]
        SVH, SVL = [at(n, [P, TB, P], F32R, BIG + (68 + 2 * k) * KB) for k, n in enumerate(("SVH", "SVL"))]
        SQH = [at(f"SQH{t}", [P, S], F32R, BIG + (72 + 4 * t) * KB) for t in range(SWA_Q)]
        SQL = [at(f"SQL{t}", [P, S], F32R, BIG + (74 + 4 * t) * KB) for t in range(SWA_Q)]
        SPH = at("SPH", [P, S], F32R, W_at[1])
        SPL = at("SPL", [P, S], F32R, W_at[5])
        SPROB = [W[k][:, 0:3 * P] for k in (2, 3, 4, 6)]
        MGH = at("MGH", [P, KT, S], F32R, BIG + 64 * KB)
        MGL = at("MGL", [P, KT, S], F32R, ring_at[2])

        WIN = [list(range(max(0, q - 1), min(TB - 1, q + 1) + 1)) for q in range(TB)]
        SEEN = [sum(len(w) for w in WIN[:q]) for q in range(TB + 1)]

        def chunk_order(d):
            return [n if d == 0 else NCH - 1 - n for n in range(NCH - 1)]

        def kv_place(n):
            bank = (0, 1)[n % 2] if n // 2 < 2 else (4, 5)[n % 2]
            return bank, slice(n // 2 % 2 * 2 * P, (n // 2 % 2 + 1) * 2 * P)

        PS = ctx.enter_context(nc.psum_tensor("PS", [P, 8, S], F32))
        cums = nc.dram_tensor("cums", (HEADS, S), F32, kind="Internal").ap()

        stream = {"units": 0, "owner": [None] * 4, "loads": [0] * 4}

        def rows(w):
            return w.rearrange("(k p) n -> p k n", p=P)

        def wphase(ring, iters, units):
            return WeightPhase(stream, ring, iters, units)

        def col(base, step=P):
            return lambda i: i * step + base

        a_in, a_out = rows(T["a_w_in"][0]), rows(T["a_w_out"][0])
        up = [rows(T["ffn_w_up"][l]) for l in range(2)] + [rows(T["w_ffn_in_2"][0])]
        down = [rows(T["ffn_w_down"][l]) for l in range(2)] + [rows(T["w_ffn_out_2"][0])]
        kvf, qg, b_out = rows(T["w_kvf"]), rows(T["b_w_qg"][0]), rows(T["b_w_out"][0])
        w_in, w_og, w_os, w_out = [rows(T[n][0]) for n in ("w_in_2", "w_o_gla_2", "w_o_swa_2", "w_out_2")]

        def square_units(w, n=4):
            return [(w, 0, KT, col(j * P, n * P)) for j in range(n)]

        def ffn_phases(l):
            u = []
            for p in range(2):
                u += [(up[l], 0, KT, col(p * P, 2 * P)), (up[l], 0, KT, col(FF + p * P, 2 * P))]
            d = []
            for p in range(2):
                d += [(down[l], k0, min(KT, FT - k0), col(p * P, 2 * P)) for k0 in (0, 8, 16)]
            return wphase(4, FT // 2, u), wphase(3, KT // 2, d)

        ph = {}
        ph["mix"] = wphase(3, KT, [(a_in, 0, KT, col(D)), (a_in, 0, KT, col(2 * D)), (a_in, 0, KT, col(0))])
        ph["mix_out"] = wphase(4, 2, square_units(a_out))
        if stop > 1:
            ph["up0"], ph["down0"] = ffn_phases(0)
        if stop > 2:
            ph["forget"] = wphase(4, 1, [(kvf, 0, KT, lambda i: 2 * D + HEADS - P)])
            ph["attn"] = wphase(4, PAIRS, [(kvf, 0, KT, col(0)), (kvf, 0, KT, col(D)),
                                           (qg, 0, KT, col(0)), (qg, 0, KT, col(D))])
            ph["attn_out"] = wphase(4, 2, square_units(b_out))
        if stop > 3:
            ph["up1"], ph["down1"] = ffn_phases(1)
        if stop > 4:
            ph["lr"] = wphase(4, 1, [(w_in, 0, KT, lambda i: G_LR)])
            ph["gla"] = wphase(3, GH, [(w_in, 0, KT, col(G_Q)), (w_in, 0, KT, col(G_K)),
                                       (w_in, 0, KT, col(G_V, 256)), (w_in, 0, KT, col(G_V + P, 256)),
                                       (w_in, 0, KT, col(G_R, 256)), (w_in, 0, KT, col(G_R + P, 256))])
            ph["swa"] = wphase(3, SWA_GROUPS, [(w_in, 0, KT, col(S_K)), (w_in, 0, KT, col(S_V))] +
                               [(w_in, 0, KT, col(S_Q + t * P, SWA_Q * P)) for t in range(SWA_Q)])
            ph["merge"] = wphase(2, KT, [(w_in, 0, KT, col(GA)), (w_in, 0, KT, col(GB)),
                                         (w_og, 0, KT, col(0)), (w_os, 0, KT, col(0))])
            ph["out2"] = wphase(2, 2, square_units(w_out))
            stream["owner"][2] = stream["owner"][3] = stream["units"] - 1
        if stop > 5:
            ph["up2"], ph["down2"] = ffn_phases(2)

        loaded = [sem(f"weights_loaded{s}") for s in range(4)]
        high_done, split_done, unit_done = sem("weights_high"), sem("weights_split"), sem("unit_done")

        def tile(t, m):
            return t[:, m, :] if isinstance(m, int) else t[:, bass.ds(m, 1), :].rearrange("p a n -> p (a n)")

        def window_out(t, i, q):
            c = slice(q * P, (q + 1) * P)
            return t[:, i * SWA_Q:(i + 1) * SWA_Q, c] if isinstance(i, int) else t[:, bass.ds(i * SWA_Q, SWA_Q), c]

        def column(t, m):
            return t[:, m:m + 1] if isinstance(m, int) else t[:, bass.ds(m, 1)]

        ORDER = {"_x": 0, 0: 1, 1: 2, 2: 3, 3: 4, 4: 5, 5: 6}

        def tiles(n):
            return ORDER[n] * KT

        last_resid = min(stop, 6) - 1

        block = ctx.enter_context(nc.Block())

        @block.sync
        def _(sp):
            for t in range(TB):
                sp.dma_start(XIN[:, t, :], T["x"][0, t * P:(t + 1) * P, :]).then_inc(sem("x_loaded"), 16)
            for p in ph.values():
                def body(i, p=p):
                    for j, (w, k0, nk, c) in enumerate(p.units):
                        free = p.before(i, j)
                        if free is not None:
                            sp.wait_ge(split_done, free)
                            if not isinstance(i, int):
                                sp.sem_inc(sem("sync_step"), 1)
                        sp.dma_start(RAW[p.slot(j)][:, 0:nk, :], w[:, k0:k0 + nk, bass.ds(c(i), P)]).then_inc(
                            loaded[p.slot(j)], 16)
                loop(sp, p.iters, body)
            for t in range(TB):
                sp.wait_ge(sem("out_rows"), 2 * (t + 1))
                sp.dma_start(out[0, t * P:(t + 1) * P, :], XIN[:, t, :]).then_inc(sem("stored"), 16)
            sp.wait_ge(sem("stored"), 16 * TB)

        @block.gpsimd
        def _(pool):
            pool.wait_ge(sem("zeroed"), 1)
            for p in ph.values():
                def body(i, p=p):
                    for j, (w, k0, nk, c) in enumerate(p.units):
                        s = p.slot(j)
                        free = p.before(i, j)
                        if free is not None:
                            pool.wait_ge(unit_done, free)
                        pool.wait_ge(loaded[s], p.load_count(i, j) * 16)
                        if not isinstance(i, int):
                            pool.tensor_tensor(TICK, ONEC, ONEC, ALU.mult)
                        pool.tensor_scalar(WH[s][:, 0:nk, :], RAW[s][:, 0:nk, :], 1.0, 1.0, ALU.mult, ALU.mult).then_inc(high_done, 1)
                        pool.wait_ge(high_done, p.unit(i, j) + 1)
                        pool.tensor_tensor(WL[s][:, 0:nk, :], RAW[s][:, 0:nk, :], WH[s][:, 0:nk, :].bitcast(F32),
                                           ALU.subtract).then_inc(split_done, 1)
                loop(pool, p.iters, body)

        @block.tensor
        def _(pe):
            def unit(p, i, j, bank, xh, xl, first=True, last=True, ready=None):
                pe.wait_ge(split_done, p.unit(i, j) + 1)
                s, (_, k0, nk, _) = p.slot(j), p.units[j]
                for k in range(nk):
                    if ready:
                        pe.wait_ge(ready[0], ready[2] + ready[1] * (k0 + k + 1))
                    o = PS[:, bank, :]
                    pe.matmul(o, WH[s][:, k, :], xh[:, k0 + k, :], start=first and k == 0, stop=False)
                    pe.matmul(o, WH[s][:, k, :], xl[:, k0 + k, :], start=False, stop=False)
                    mm = pe.matmul(o, WL[s][:, k, :], xh[:, k0 + k, :], start=False, stop=last and k == nk - 1)
                mm.then_inc(unit_done, 1)

            def product(o, ah, al, bh, bl, start=True, stop=True, loose=False):
                pe.matmul(o, ah, bh, start=start, stop=False, skip_group_check=loose)
                pe.matmul(o, ah, bl, start=False, stop=False, skip_group_check=loose)
                return pe.matmul(o, al, bh, start=False, stop=stop, skip_group_check=loose)

            def row_sums(n):
                pe.wait_ge(sem("acc"), tiles(n) + KT)
                pe.matmul(PS[:, 7, :], ONE[:, :], W[1][:, 0:S], start=True, stop=True).then_inc(sem("nsum"), 1)

            def residual(p, n, groups, xh, xl, ready, banks_read):
                tpi = p.U // groups
                def body(i):
                    for t in range(tpi):
                        m = i * tpi + t
                        if t >= 2 or not isinstance(i, int) or i > 0:
                            pe.wait_ge(sem("resid"), tiles(n) + m - 1)
                        else:
                            pe.wait_ge(*banks_read[t])
                        for g in range(groups):
                            unit(p, i, t * groups + g, t % 2, xh, xl, g == 0, g == groups - 1,
                                 ready if isinstance(i, int) and i == 0 and t == 0 else None)
                loop(pe, p.iters, body)

            def ffn(l, n):
                pu, pd = ph[f"up{l}"], ph[f"down{l}"]
                def body(i):
                    for q in range(2):
                        m = 2 * i + q
                        for k in range(2):
                            if not isinstance(i, int) or i > 0:
                                pe.wait_ge(sem(f"ffn_{'ag'[k]}"), m + (l * FT - 1))
                            elif q == 0:
                                pe.wait_ge(sem("resid"), tiles(n) + KT - 1 + k)
                            unit(pu, i, 2 * q + k, 2 * q + k, XH, XL,
                                 ready=(sem("xld"), 1, tiles(n)) if isinstance(i, int) and i == 0 and q == k == 0 else None)
                            if isinstance(i, int) and i == 0 and q == k == 0:
                                row_sums(n)
                loop(pe, pu.iters, body)
                residual(pd, n + 1, 3, HH, HL, (sem("ffn_low"), 1, l * FT),
                         [(sem("ffn_a"), (l + 1) * FT), (sem("ffn_g"), (l + 1) * FT)])

            def scores(b, h):
                H, r = 2 * b + h, slice(HD * h, HD * h + HD)
                if h == 0:
                    pe.wait_ge(sem("hn_low"), 2 * b + 2)
                if not isinstance(b, int) or H > 0:
                    pe.wait_ge(sem("pt_low"), H * TB)
                for q in range(TB):
                    n = (q + 1) * P
                    product(PS[:, 4 + q, 0:n], QH[r, q * P:n], QL[r, q * P:n], KH[r, 0:n], KL[r, 0:n],
                            stop=False, loose=True)
                    pe.matmul(PS[:, 4 + q, q * P:n], IDB[:, :], MCAUSAL[:, :], start=False, stop=True,
                              skip_group_check=True).then_inc(sem("scores"), 1)

            def weigh(b, h):
                H = 2 * b + h
                pe.wait_ge(sem("prob"), H * TB + TB)
                for j in range(TB):
                    for q in range(j, TB):
                        tr = pe.transpose(PS[:, 4 + j, (q - j) * P:(q - j + 1) * P],
                                          PROB[q][:, j * P:(j + 1) * P], IDF[:, :])
                    tr.then_inc(sem("prob_t"), 1)
                if h == 0:
                    pe.wait_ge(sem("v_low"), b + 1)
                if not isinstance(b, int) or H > 0:
                    pe.wait_ge(sem("o_read"), H * 1)
                for j in range(TB):
                    pe.wait_ge(sem("pt_low"), H * TB + (j + 1))
                    n = (TB - j) * P
                    product(PS[:, 2, j * P:S], VH[:, j, :], VL[:, j, :], PTH[j % 2][:, 0:n], PTL[j % 2][:, 0:n],
                            start=j == 0, stop=j == TB - 1, loose=True).then_inc(sem("weighed"), 1)

            def head_sums(n):
                pe.wait_ge(sem("hn_sq"), n + 1)
                pe.matmul(PS[:, 3, :], ONE64[:, :], W[2][:, 0:S], start=True, stop=True).then_inc(sem("hn_sum"), 1)

            def attention():
                pe.wait_ge(sem("resid"), tiles(1) + KT)
                pe.wait_ge(sem("xld"), tiles(1) + KT)
                unit(ph["forget"], 0, 0, 0, X2H, X2L, ready=(sem("x2_low"), 1, 0))
                row_sums(1)
                pe.wait_ge(sem("fg_c"), 1)
                for t in range(TB):
                    tr = pe.transpose(PS[:, 1, t * P:(t + 1) * P], W[4][:, t * P:(t + 1) * P], IDF[:, :])
                tr.then_inc(sem("fg_t"), 1)
                p = ph["attn"]
                def body(i):
                    first = isinstance(i, int) and i == 0
                    if first:
                        pe.wait_ge(sem("fg_z"), 1)
                    else:
                        pe.wait_ge(sem("kq_read"), i * 2)
                    unit(p, i, 0, 0, X2H, X2L)
                    if not first:
                        scores(i - 1, 0)
                    if first:
                        pe.wait_ge(sem("fg_ct"), 1)
                    else:
                        pe.wait_ge(sem("vg_read"), i * 2)
                    unit(p, i, 1, 1, X2H, X2L)
                    if not first:
                        weigh(i - 1, 0)
                        scores(i - 1, 1)
                        pe.wait_ge(sem("v_low"), i * 1)
                    head_sums(i * 2)
                    pe.wait_ge(sem("kq_read"), i * 2 + 1)
                    unit(p, i, 2, 0, XH, XL)
                    if not first:
                        weigh(i - 1, 1)
                    pe.wait_ge(sem("hn_v"), i * 2 + 1)
                    head_sums(i * 2 + 1)
                    pe.wait_ge(sem("vg_read"), i * 2 + 1)
                    unit(p, i, 3, 1, XH, XL)
                    pe.wait_ge(sem("hn_v"), i * 2 + 2)
                    for t in range(TB):
                        tr = pe.transpose(PS[:, 3, t * P:(t + 1) * P], W[5][:, t * P:(t + 1) * P], IDF[:, :])
                    tr.then_inc(sem("v_t"), 1)
                body(0)
                loop(pe, PAIRS, body, start=1)
                for h in range(2):
                    scores(PAIRS - 1, h)
                    weigh(PAIRS - 1, h)
                residual(ph["attn_out"], 2, 1, OH, OL, (sem("o_low"), 1, 0),
                         [(sem("kq_read"), 2 * PAIRS), (sem("vg_read"), 2 * PAIRS)])

            def gates():
                pe.wait_ge(sem("resid"), tiles(3) + KT)
                unit(ph["lr"], 0, 0, 0, XH, XL, ready=(sem("xld"), 1, tiles(3)))
                row_sums(3)
                pe.wait_ge(sem("up_loaded"), 32)
                pe.wait_ge(sem("lr"), 1)
                for t in range(2 * GH):
                    if t >= 2:
                        pe.wait_ge(sem("z_read"), t - 1)
                    pe.matmul(PS[:, 1 + t % 2, :], UP[:, t * P:(t + 1) * P], W[1][0:2 * GATE_RANK, 0:S],
                              start=True, stop=True).then_inc(sem("z"), 1)

            def gla(i):
                p = ph["gla"]
                if isinstance(i, int) and i == 0:
                    pe.wait_ge(sem("z_read"), 2 * GH)
                else:
                    pe.wait_ge(sem("g_nv"), i * 1)
                for j in range(6):
                    unit(p, i, j, j, XH, XL)
                pe.wait_ge(sem("g_read"), i * 6 + 4)
                for t in range(TB):
                    for u in range(2):
                        tr = pe.transpose(PS[:, t // 2, (t % 2 * 2 + u) * P:(t % 2 * 2 + u + 1) * P],
                                          W[3 + u][:, t * P:(t + 1) * P], IDF[:, :])
                tr.then_inc(sem("gv_t"), 1)
                for d in range(2):
                    n = 2 * i + d
                    pe.wait_ge(sem("gd_low"), n * 3 + 2)
                    for b in range(TB):
                        c = slice(b * P, (b + 1) * P)
                        mm = product(PS[:, 2 + d, c], KIH[:, c], KIL[:, c], QDH[:, c], QDL[:, c])
                    mm.then_inc(sem("g_scores"), 1)
                    pe.wait_ge(sem("g_kt"), n + 1)
                    if d == 1:
                        pe.wait_ge(sem("g_st"), n * (NCH - 1))
                    else:
                        pe.wait_ge(sem("g_read"), i * 6 + 6)
                    for t in range(TB):
                        tr = pe.transpose(PS[:, 4, t * P:(t + 1) * P], W[8][:, t * P:(t + 1) * P], IDF[:, :])
                    tr.then_inc(sem("g_kt_t"), 1)
                    pe.wait_ge(sem("gv_low"), i * 2 + 2)
                    pe.wait_ge(sem("gd_low"), n * 3 + 3)
                    for c in chunk_order(d):
                        r, b = slice(c % 2 * CH, c % 2 * CH + CH), c // 2
                        bank, cols = kv_place(c)
                        product(PS[:, bank, cols], KTH[r, b * P:(b + 1) * P], KTL[r, b * P:(b + 1) * P],
                                VGH[r, b, :], VGL[r, b, :]).then_inc(sem("g_kv"), 1)
                    if d == 0 and not (isinstance(i, int) and i == 0):
                        pe.wait_ge(sem("g_y"), i * 2)
                    for s, c in enumerate(chunk_order(d)):
                        to = c + 1 if d == 0 else c - 1
                        t = slice(to * CH, (to + 1) * CH)
                        pe.wait_ge(sem("g_state_low"), n * (NCH - 1) + (s + 1))
                        for u in range(2):
                            v = slice(u * P, (u + 1) * P)
                            mm = product(PS[:, 6 + u, t], SH[:, s, v], SL[:, s, v], QDH[:, t], QDL[:, t],
                                         start=d == 0 and s == 0, stop=False, loose=True)
                    mm.then_inc(sem("g_inter"), 1)
                pe.wait_ge(sem("g_sc_low"), i + 1)
                for u in range(2):
                    for b in range(TB):
                        c = slice(b * P, (b + 1) * P)
                        mm = product(PS[:, 6 + u, c], VGH[:, b, u * P:(u + 1) * P], VGL[:, b, u * P:(u + 1) * P],
                                     SCH[:, c], SCL[:, c], start=False, stop=b == TB - 1, loose=True)
                mm.then_inc(sem("g_o"), 1)
                pe.wait_ge(sem("g_sq"), i * 2 + 2)
                pe.matmul(PS[:, 0, :], ONE[:, :], W[7][:, 0:S], start=True, stop=False)
                pe.matmul(PS[:, 0, :], ONE[:, :], W[8][:, 0:S], start=False, stop=True).then_inc(sem("g_sum"), 1)

            def swa(i):
                p = ph["swa"]
                def head_sum(n):
                    pe.wait_ge(sem("sw_sq"), i * 5 + (n + 1))
                    if n > 0 or not isinstance(i, int) or i > 0:
                        pe.wait_ge(sem("sw_v"), i * 5 + n)
                    pe.matmul(PS[:, 4, :], ONE[:, :], W[2][:, 0:S], start=True, stop=True).then_inc(sem("sw_sum"), 1)
                if isinstance(i, int) and i == 0:
                    pe.wait_ge(sem("g_ylow"), 2 * GH)
                else:
                    pe.wait_ge(sem("sw_out"), i * TB)
                unit(p, i, 0, 0, XH, XL)
                unit(p, i, 1, 1, XH, XL)
                head_sum(0)
                unit(p, i, 2, 2, XH, XL)
                pe.wait_ge(sem("sw_read"), i * 6 + 2)
                for t in range(TB):
                    tr = pe.transpose(PS[:, 5, t * P:(t + 1) * P], W[9][:, t * P:(t + 1) * P], IDF[:, :])
                tr.then_inc(sem("sv_t"), 1)
                unit(p, i, 3, 3, XH, XL)
                head_sum(1)
                unit(p, i, 4, 0, XH, XL)
                head_sum(2)
                unit(p, i, 5, 1, XH, XL)
                head_sum(3)
                head_sum(4)
                pe.wait_ge(sem("sv_low"), i + 1)
                pe.wait_ge(sem("sw_low"), i * 5 + 5)
                for q in range(TB):
                    win, n = WIN[q], i * 4 * TB + 4 * q
                    if q > 0:
                        pe.wait_ge(sem("sw_exp"), n)
                    for t in range(SWA_Q):
                        c = slice(q * P, (q + 1) * P)
                        k = slice(win[0] * P, (win[-1] + 1) * P)
                        product(PS[:, 4 + t, 0:len(win) * P], SQH[t][:, c], SQL[t][:, c], SKH[:, k], SKL[:, k],
                                stop=False, loose=True)
                        if q > 0:
                            mm = pe.matmul(PS[:, 4 + t, 0:P], IDB[:, :], MUPPER[:, :], start=False,
                                           stop=q == TB - 1, skip_group_check=True)
                        if q < TB - 1:
                            mm = pe.matmul(PS[:, 4 + t, (len(win) - 1) * P:len(win) * P], IDB[:, :], MCAUSAL[:, :],
                                           start=False, stop=True, skip_group_check=True)
                        mm.then_inc(sem("sw_scores"), 1)
                    pe.wait_ge(sem("sw_prob"), n + 4)
                    for jj in range(len(win)):
                        if q > 0 or not isinstance(i, int) or i > 0:
                            if jj == 0:
                                pe.wait_ge(sem("sw_plow"), i * SEEN[TB] + SEEN[q])
                        for t in range(SWA_Q):
                            tr = pe.transpose(PS[:, jj, t * P:(t + 1) * P], SPROB[t][:, jj * P:(jj + 1) * P], IDF[:, :])
                        tr.then_inc(sem("sw_pt"), 1)
                    if q > 0:
                        pe.wait_ge(sem("sw_out"), i * TB + q)
                    for jj, j in enumerate(win):
                        pe.wait_ge(sem("sw_plow"), i * SEEN[TB] + (SEEN[q] + jj + 1))
                        product(PS[:, 3, :], SVH[:, j, :], SVL[:, j, :], SPH[:, :], SPL[:, :], start=jj == 0,
                                stop=jj == len(win) - 1).then_inc(sem("sw_pv"), 1)

            def merge(i):
                p = ph["merge"]
                for j, (xh, xl) in enumerate(((XH, XL), (XH, XL), (YGH, YGL), (YSH, YSL))):
                    if isinstance(i, int) and i == 0:
                        if j == 0:
                            pe.wait_ge(sem("sw_out"), SWA_GROUPS * TB)
                    else:
                        pe.wait_ge(sem("mg_read"), i * 4 + (j - 3))
                    unit(p, i, j, j, xh, xl)

            pe.wait_ge(sem("consts"), 16)
            pe.wait_ge(sem("params"), 16 * N_PARAM_DMAS)
            pe.wait_ge(sem("zeroed"), 1)
            pe.transpose(PS[:, 2, 0:P], PROW[:, 0, :], CST[:, C_ID:C_ID + P])
            for l in range(2):
                tr = pe.transpose(PS[:, 2, P * (l + 1):P * (l + 1) + P], PROW[:, 1 + l, :], CST[:, C_ID:C_ID + P])
            tr.then_inc(sem("prm_t"), 1)
            pe.wait_ge(sem("x_loaded"), 16 * TB)
            for m in range(KT):
                if m >= 2:
                    pe.wait_ge(sem("resid"), tiles("_x") + m - 1)
                for t in range(TB):
                    tr = pe.transpose(PS[:, m % 2, t * P:(t + 1) * P], XIN[:, t, m * P:(m + 1) * P], CST[:, C_ID:C_ID + P])
                tr.then_inc(sem("xt"), 1)
            p = ph["mix"]
            pe.wait_ge(sem("resid"), tiles("_x") + KT)
            def mix(i):
                for j in range(3):
                    if not isinstance(i, int) or i > 0:
                        pe.wait_ge(sem(f"mix_{'chb'[j]}"), i * 1)
                    unit(p, i, j, j, XH, XL, ready=(sem("xld"), 1, tiles("_x")) if isinstance(i, int) and i == 0 and j == 0 else None)
                    if isinstance(i, int) and i == 0 and j == 0:
                        row_sums("_x")
            loop(pe, KT, mix)
            residual(ph["mix_out"], 0, 1, BUH, BUL, (sem("mix_low"), 1, 0),
                     [(sem("mix_c"), KT), (sem("mix_h"), KT)])
            if stop > 1:
                ffn(0, 0)
            if stop > 2:
                attention()
            if stop > 3:
                ffn(1, 2)
            if stop > 4:
                gates()
                loop(pe, GH, gla)
                loop(pe, SWA_GROUPS, swa)
                loop(pe, KT, merge)
                residual(ph["out2"], 4, 1, MGH, MGL, (sem("mg_low"), 1, 0),
                         [(sem("mg_read"), 4 * KT), (sem("mg_read"), 4 * KT)])
            if stop > 5:
                ffn(2, 4)
            pe.wait_ge(sem("resid"), tiles(last_resid) + KT)
            for t in range(TB):
                for h in range(2):
                    n = 2 * t + h
                    if n >= 2:
                        pe.wait_ge(sem("out_rows"), n - 1)
                    for m in range(4):
                        tr = pe.transpose(PS[:, 2 + n % 2, m * P:(m + 1) * P],
                                          XT[:, 4 * h + m, t * P:(t + 1) * P], IDF[:, :])
                    tr.then_inc(sem("out_t"), 1)

        @block.scalar
        def _(act):
            steps = Steps(act, sem("act_step"))
            link = steps.link

            def rsqrt(v, r, rr, ready, value, done):
                act.wait_ge(ready, value)
                link(act.activation(r, v, ACT.Ln))
                link(act.activation(r, r, ACT.Exp, scale=-0.5))
                act.activation(rr, r, ACT.Square).then_inc(done, 1)

            def norm(n):
                rsqrt(W[4][:, 0:S], W[5][:, 0:S], W[6][:, 0:S], sem("nv"), ORDER[n] + 1, sem("nrr"))

            def residual(n, iters, tpi, gains):
                def body(i):
                    for t in range(tpi):
                        m = i * tpi + t
                        if gains and (t >= 2 or not isinstance(i, int) or i > 0):
                            act.wait_ge(sem("acc"), tiles(n) + m - 1)
                        act.wait_ge(sem("resid"), tiles(n) + m + 1)
                        if not gains:
                            continue
                        act.wait_ge(sem("prm_ready"), 3)
                        act.activation(W[2 + t % 2][:, 0:S], tile(XT, m), ACT.Square).then_inc(sem("sq"), 1)
                        for xh, _, row in gains:
                            act.activation(tile(xh, m), tile(XT, m), ACT.Copy,
                                           scale=column(PRM, m + row)).then_inc(sem("xhd"), 1)
                if gains:
                    loop(act, iters, body, steps)

            def ffn(l, n, conv, gains):
                norm(n)
                def body(i):
                    for q in range(2):
                        m = 2 * i + q
                        u, g = W[3 + q][:, 0:S], W[5 + q]
                        act.wait_ge(sem("ffn_u" if conv else "ffn_a"), m + (l * FT + 1))
                        act.activation(u, u, ACT.Silu).then_inc(sem("ffn_silu"), 1)
                        act.wait_ge(sem("ffn_h"), m + l * FT + 1)
                        act.wait_ge(sem("prm_ready"), 3)
                        act.copy(tile(HH, m), g[:, 0:S]).then_inc(sem("ffn_high"), 1)
                loop(act, FT // 2, body, steps)
                residual(n + 1, KT // 2, 2, gains)

            def softmax(b, h):
                H = 2 * b + h
                for q in range(TB):
                    act.wait_ge(sem("score_max"), H * TB + (q + 1))
                    pr = PROB[q][:, 0:(q + 1) * P]
                    act.activation(pr, pr, ACT.Exp, bias=NEGM[:, q:q + 1],
                                   accum_out=RS[:, q:q + 1]).then_inc(sem("exp"), 1)
                for q in range(TB):
                    act.wait_ge(sem("rinv"), H * TB + (q + 1))
                    pr = PROB[q][:, 0:(q + 1) * P]
                    act.activation(pr, pr, ACT.Copy, scale=RINV[:, q:q + 1]).then_inc(sem("prob"), 1)

            def high_probs(b, h):
                H = 2 * b + h
                for j in range(TB):
                    act.wait_ge(sem("prob_t"), H * TB + (j + 1))
                    if not isinstance(b, int) or H > 0 or j >= 2:
                        act.wait_ge(sem("weighed"), H * TB + (j - 1))
                    act.copy(PTH[j % 2][:, 0:(TB - j) * P], PS[:, 4 + j, 0:(TB - j) * P]).then_inc(sem("pt_high"), 1)

            def high_out(b):
                act.wait_ge(sem("o_read"), 2 * b + 2)
                act.wait_ge(sem("prm_ready"), 3)
                act.copy(tile(OH, b), W[6][:, 0:S]).then_inc(sem("o_high"), 1)

            def load_cums(b):
                for h in range(2):
                    row = cums[2 * b + h, :] if isinstance(b, int) else \
                        cums[bass.ds(2 * b + h, 1), :].rearrange("a n -> (a n)")
                    act.dma_start(W[8 + h][:, 0:S], row.partition_broadcast(P)).then_inc(sem("cums_loaded"), 16)

            def head_norm(n, to):
                rsqrt(W[3][:, 0:S], W[2][:, 0:S], W[4][:, 0:S], sem("hn_v"), n + 1, sem("hn_rr"))
                act.wait_ge(sem("hn_x"), n + 1)
                act.copy(to[:, :], W[1][:, 0:S]).then_inc(sem("hn_high"), 1)

            def square(n):
                act.wait_ge(sem("kq_read"), n + 1)
                act.activation(W[2][:, 0:S], W[1][:, 0:S], ACT.Square).then_inc(sem("hn_sq"), 1)

            def attention():
                act.wait_ge(sem("resid"), tiles(1) + KT)
                for m in range(KT):
                    act.activation(X2H[:, m, :], XT[:, m, :], ACT.Copy,
                                   scale=PRM[:, R_KV + m:R_KV + m + 1]).then_inc(sem("x2_high"), 1)
                norm(1)
                act.wait_ge(sem("fg_z"), 1)
                link(act.activation(W[2][:, 0:S], W[1][:, 0:S], ACT.Abs))
                link(act.activation(W[2][:, 0:S], W[2][:, 0:S], ACT.Exp, scale=-1.0))
                act.activation(W[2][:, 0:S], W[2][:, 0:S], ACT.Ln, bias=ONEC).then_inc(sem("fg_sp"), 1)
                act.wait_ge(sem("fg_c"), 1)
                act.dma_start(cums[:, :], W[4][P - HEADS:P, 0:S]).then_inc(sem("cums_stored"), 16)
                act.wait_ge(sem("cums_stored"), 16)
                def body(i):
                    first = isinstance(i, int) and i == 0
                    square(i * 2)
                    if not first:
                        softmax(i - 1, 0)
                        high_probs(i - 1, 0)
                        softmax(i - 1, 1)
                    load_cums(i)
                    if not first:
                        act.wait_ge(sem("scores"), i * 2 * TB)
                    head_norm(i * 2, KH)
                    square(i * 2 + 1)
                    if not first:
                        high_probs(i - 1, 1)
                        high_out(i - 1)
                    head_norm(i * 2 + 1, QH)
                    act.wait_ge(sem("vg_read"), i * 2 + 2)
                    act.activation(W[6][:, 0:S], W[6][:, 0:S], ACT.Exp, scale=-1.0).then_inc(sem("g_exp"), 1)
                    act.wait_ge(sem("v_t"), i + 1)
                    act.copy(VH[:, :, :], PS[:, 3, :].rearrange("p (t c) -> p t c", t=TB)).then_inc(sem("v_high"), 1)
                body(0)
                loop(act, PAIRS, body, steps, start=1)
                for h in range(2):
                    softmax(PAIRS - 1, h)
                    high_probs(PAIRS - 1, h)
                high_out(PAIRS - 1)

            def gates():
                act.wait_ge(sem("up_zeroed"), 1)
                for d, name in enumerate(("gla_gate_up_fwd_2", "gla_gate_up_bwd_2")):
                    act.dma_start(UP[d * GATE_RANK:(d + 1) * GATE_RANK, d * GH * GDK:(d + 1) * GH * GDK],
                                  T[name][0]).then_inc(sem("up_loaded"), 16)
                norm(3)
                act.dma_start(W[9][:, 0:2 * P], T["consts"][:, C_GF:C_GF + 2 * P]).then_inc(sem("g_masks"), 16)
                for t in range(2 * GH):
                    z, sp = W[2 + t % 2][:, 0:S], W[4 + t % 2][:, 0:S]
                    act.wait_ge(sem("z_read"), t + 1)
                    link(act.activation(sp, z, ACT.Abs))
                    link(act.activation(sp, sp, ACT.Exp, scale=-1.0))
                    act.activation(sp, sp, ACT.Ln, bias=ONEC).then_inc(sem("z_sp"), 1)

            def gla(i):
                for u in range(2):
                    act.wait_ge(sem("g_read"), i * 6 + (5 + u))
                    act.activation(W[7 + u][:, 0:S], W[5 + u][:, 0:S], ACT.Exp, scale=-1.0).then_inc(sem("g_rexp"), 1)
                act.wait_ge(sem("gv_t"), i + 1)
                for b in range(2):
                    act.copy(VGH[:, 2 * b:2 * b + 2, :], PS[:, b, :].rearrange("p (t c) -> p t c", t=2)).then_inc(sem("gv_high"), 1)
                for d in range(2):
                    n = 2 * i + d
                    if d == 0:
                        act.wait_ge(sem("g_silu"), i + 1)
                    else:
                        act.wait_ge(sem("gd_low"), n * 3)
                    act.wait_ge(sem("prm_ready"), 3)
                    act.activation(W[7][:, 0:S], tile(BC, i + GH * d), ACT.Exp).then_inc(sem("g_e"), 1)
                    act.activation(W[8][:, 0:S], tile(BC, i + GH * d), ACT.Exp, scale=-1.0).then_inc(sem("g_e"), 1)
                    if d == 1 or not isinstance(i, int) or i > 0:
                        act.wait_ge(sem("g_inter"), n * 1)
                    act.wait_ge(sem("g_qk"), n * 2 + 1)
                    act.copy(QDH[:, :], W[7][:, 0:S]).then_inc(sem("gd_high"), 1)
                    act.wait_ge(sem("g_qk"), n * 2 + 2)
                    act.copy(KIH[:, :], W[8][:, 0:S]).then_inc(sem("gd_high"), 1)
                    act.wait_ge(sem("g_kt_t"), n + 1)
                    act.copy(KTH[:, :], PS[:, 4, :]).then_inc(sem("gd_high"), 1)
                    if d == 1:
                        act.wait_ge(sem("g_sc"), i + 1)
                        act.copy(SCH[:, :], W[7][:, 0:S]).then_inc(sem("g_sc_high"), 1)
                    for s in range(NCH - 1):
                        act.wait_ge(sem("g_st"), n * (NCH - 1) + (s + 1))
                        act.copy(SH[:, s, :], ST[s % 2][:, :]).then_inc(sem("g_state_high"), 1)
                act.wait_ge(sem("g_o"), i + 1)
                for u in range(2):
                    act.activation(W[7 + u][:, 0:S], PS[:, 6 + u, :], ACT.Square).then_inc(sem("g_sq"), 1)
                rsqrt(W[1][:, 0:S], W[2][:, 0:S], W[7][:, 0:S], sem("g_nv"), i + 1, sem("g_nrr"))
                for u in range(2):
                    act.wait_ge(sem("g_y"), i * 2 + (u + 1))
                    act.wait_ge(sem("prm_ready"), 3)
                    act.copy(tile(YGH, i * 2 + u), W[3 + u][:, 0:S]).then_inc(sem("g_yhigh"), 1)

            def swa(i):
                if isinstance(i, int) and i == 0:
                    act.wait_ge(sem("g_ylow"), 2 * GH)
                    for k in range(2):
                        act.dma_start(W[7 + k][:, 0:S], T["consts"][:, C_COS + k * S:C_COS + (k + 1) * S]).then_inc(sem("rope"), 16)
                def square(n):
                    act.wait_ge(sem("sw_read"), i * 6 + (n + 1 if n == 0 else n + 2))
                    act.activation(W[2][:, 0:S], W[1][:, 0:S], ACT.Square).then_inc(sem("sw_sq"), 1)
                def finish(n, to):
                    rsqrt(W[3][:, 0:S], W[2][:, 0:S], W[4][:, 0:S], sem("sw_v"), i * 5 + (n + 1), sem("sw_rr"))
                    act.wait_ge(sem("sw_x"), i * 5 + (n + 1))
                    act.copy(to[:, :], W[1][:, 0:S]).then_inc(sem("sw_high"), 1)
                square(0)
                finish(0, SKH)
                square(1)
                act.wait_ge(sem("sv_t"), i + 1)
                act.copy(SVH[:, :, :], PS[:, 5, :].rearrange("p (t c) -> p t c", t=TB)).then_inc(sem("sv_high"), 1)
                for t in range(SWA_Q):
                    finish(t + 1, SQH[t])
                    if t < SWA_Q - 1:
                        square(t + 2)
                for q in range(TB):
                    win, n = WIN[q], i * 4 * TB + 4 * q
                    if q > 0 or not isinstance(i, int) or i > 0:
                        act.wait_ge(sem("sw_pt"), i * SEEN[TB] + SEEN[q])
                    for t in range(SWA_Q):
                        act.wait_ge(sem("sw_max"), n + (t + 1))
                        act.wait_ge(sem("prm_ready"), 3)
                        act.activation(ESK[:, t:t + 1], column(SINK, i * SWA_Q + t), ACT.Exp,
                                       bias=NEGM[:, t:t + 1]).then_inc(sem("sw_sink"), 1)
                        act.activation(SPROB[t][:, 0:len(win) * P], PS[:, 4 + t, 0:len(win) * P], ACT.Exp,
                                       bias=NEGM[:, t:t + 1], accum_out=RS[:, t:t + 1]).then_inc(sem("sw_exp"), 1)
                    act.wait_ge(sem("sw_rinv"), i * TB + (q + 1))
                    for t in range(SWA_Q):
                        pr = SPROB[t][:, 0:len(win) * P]
                        act.activation(pr, pr, ACT.Copy, scale=RINV[:, t:t + 1]).then_inc(sem("sw_prob"), 1)
                    for jj in range(len(win)):
                        act.wait_ge(sem("sw_pt"), i * SEEN[TB] + (SEEN[q] + jj + 1))
                        if jj > 0:
                            act.wait_ge(sem("sw_pv"), i * SEEN[TB] + (SEEN[q] + jj))
                        act.copy(SPH[:, :], PS[:, jj, :]).then_inc(sem("sw_phigh"), 1)
                    act.wait_ge(sem("sw_pv"), i * SEEN[TB] + SEEN[q + 1])
                    act.wait_ge(sem("prm_ready"), 3)
                    act.copy(window_out(YSH, i, q), PS[:, 3, :].rearrange("p (t c) -> p t c", t=SWA_Q)).then_inc(sem("sw_ohigh"), 1)

            def merge(i):
                for k in range(2):
                    act.wait_ge(sem("mg_read"), i * 4 + (k + 1))
                    act.activation(W[1 + k][:, 0:S], W[1 + k][:, 0:S], ACT.Sigmoid).then_inc(sem("mg_sig"), 1)
                act.wait_ge(sem("mg"), i + 1)
                act.wait_ge(sem("prm_ready"), 3)
                act.copy(tile(MGH, i), W[3][:, 0:S]).then_inc(sem("mg_high"), 1)

            act.dma_start(CST[:, :], T["consts"][:, 0:C_GF]).then_inc(sem("consts"), 16)
            act.wait_ge(sem("zeroed"), 1)
            for to, src in PARAM_DMAS(PROW, T):
                act.dma_start(to, src).then_inc(sem("params"), 16)
            if stop > 4:
              act.dma_start(SINK[:, :], T["swa_sinks_2"][0].partition_broadcast(P)).then_inc(sem("sinks"), 16)
            residual("_x", 1, KT, [(XH, XL, R_ATTN)])
            norm("_x")
            def mix(i):
                act.wait_ge(sem("mix_bu"), i + 1)
                act.wait_ge(sem("prm_ready"), 3)
                act.copy(tile(BUH, i), W[4][:, 0:S]).then_inc(sem("mix_high"), 1)
            loop(act, KT, mix, steps)
            residual(0, 2, 4, [(XH, XL, R_FFN)] if stop > 1 else [])
            if stop > 1:
                ffn(0, 0, True, [(XH, XL, R_ATTN + KT)] if stop > 2 else [])
            if stop > 2:
                attention()
                residual(2, 2, 4, [(XH, XL, R_FFN + KT)] if stop > 3 else [])
            if stop > 3:
                ffn(1, 2, True, [(XH, XL, R_MIX)] if stop > 4 else [])
            if stop > 4:
                gates()
                loop(act, GH, gla, steps)
                loop(act, SWA_GROUPS, swa, steps)
                loop(act, KT, merge, steps)
                residual(4, 2, 4, [(XH, XL, R_FFN2)] if stop > 5 else [])
            if stop > 5:
                ffn(2, 4, False, [])

        @block.vector
        def _(dve):
            steps = Steps(dve, sem("dve_step"))
            link = steps.link

            def newton(v, r, rr, ready, value, out_, signal=None):
                dve.wait_ge(ready, value)
                link(dve.tensor_tensor(v, v, rr, ALU.mult))
                link(dve.tensor_scalar(v, v, -0.5, 1.5, ALU.mult, ALU.add))
                ins = dve.tensor_tensor(out_, r, v, ALU.mult)
                if signal is None:
                    link(ins)
                else:
                    ins.then_inc(signal, 1)

            def norm(n):
                dve.wait_ge(sem("nsum"), ORDER[n] + 1)
                dve.tensor_scalar(W[4][:, 0:S], PS[:, 7, :], 1.0 / D, EPS, ALU.mult, ALU.add).then_inc(sem("nv"), 1)
                newton(W[4][:, 0:S], W[5][:, 0:S], W[6][:, 0:S], sem("nrr"), ORDER[n] + 1, W[0][:, 0:S])

            def residual(n, iters, tpi, gains, take):
                def body(i):
                    for t in range(tpi):
                        m = i * tpi + t
                        take(i, t, m).then_inc(sem("resid"), 1)
                        if not gains:
                            continue
                        dve.wait_ge(sem("sq"), tiles(n) + m + 1)
                        sq, acc = W[2 + t % 2][:, 0:S], W[1][:, 0:S]
                        if isinstance(m, int) and m == 0:
                            dve.tensor_copy(acc, sq).then_inc(sem("acc"), 1)
                        else:
                            dve.wait_ge(sem("acc"), tiles(n) + m)
                            dve.tensor_tensor(acc, acc, sq, ALU.add).then_inc(sem("acc"), 1)
                        for g, (xh, xl, row) in enumerate(gains):
                            dve.wait_ge(sem("xhd"), tiles(n) + m + 1)
                            dve.scalar_tensor_tensor(tile(xl, m), tile(XT, m), column(PRM, m + row),
                                                     tile(xh, m).bitcast(F32), ALU.mult,
                                                     ALU.subtract).then_inc(sem("xld"), 1)
                loop(dve, iters, body, steps)

            def add_products(p, groups):
                def take(i, t, m):
                    dve.wait_ge(unit_done, p.unit(i, t * groups + groups - 1) + 1)
                    return dve.tensor_tensor(tile(XT, m), PS[:, t % 2, :], tile(XT, m), ALU.add)
                return take

            def conv(x, o, w):
                link(dve.tensor_scalar(o, x[:, 0:S], w[0], None, ALU.mult))
                link(dve.scalar_tensor_tensor(o, x[:, 1:S + 1], w[1], o, ALU.mult, ALU.add))
                return dve.scalar_tensor_tensor(o, x[:, 2:S + 2], w[2], o, ALU.mult, ALU.add)

            def ffn(l, n, with_conv, gains):
                pu, pd = ph[f"up{l}"], ph[f"down{l}"]
                norm(n)
                for q in range(2):
                    dve.memset(W[1 + q][:, 0:2], 0.0)
                link(dve.memset(W[7][:, 0:2], 0.0))
                def body(i):
                    for q in range(2):
                        m = 2 * i + q
                        a, u, g = W[1 + q], W[3 + q][:, 0:S], W[5 + q][:, 0:S]
                        dve.wait_ge(unit_done, pu.unit(i, 2 * q) + 1)
                        dve.tensor_tensor(a[:, 2:S + 2] if with_conv else u, PS[:, 2 * q, :], W[0][:, 0:S],
                                          ALU.mult).then_inc(sem("ffn_a"), 1)
                        if with_conv:
                            dve.wait_ge(sem("ffn_a"), m + l * FT + 1)
                            conv(a, u, [column(FC, m + (l * 3 + k) * FT) for k in range(3)]).then_inc(sem("ffn_u"), 1)
                        dve.wait_ge(unit_done, pu.unit(i, 2 * q + 1) + 1)
                        dve.tensor_tensor(g, PS[:, 2 * q + 1, :], W[0][:, 0:S], ALU.mult).then_inc(sem("ffn_g"), 1)
                        dve.wait_ge(sem("ffn_g"), m + l * FT + 1)
                        dve.wait_ge(sem("ffn_silu"), m + l * FT + 1)
                        dve.tensor_tensor(g, g, u, ALU.mult).then_inc(sem("ffn_h"), 1)
                        dve.wait_ge(sem("ffn_high"), m + l * FT + 1)
                        dve.tensor_tensor(tile(HL, m), g, tile(HH, m).bitcast(F32), ALU.subtract).then_inc(sem("ffn_low"), 1)
                loop(dve, FT // 2, body, steps)
                residual(n + 1, KT // 2, 2, gains, add_products(pd, 3))

            def softmax(b, h):
                H = 2 * b + h
                if h == 0:
                    dve.wait_ge(sem("cums_loaded"), 32 * b + 32)
                if not isinstance(b, int) or H > 0:
                    dve.wait_ge(sem("prob_t"), H * TB)
                for q in range(TB):
                    n = (q + 1) * P
                    pr = PROB[q][:, 0:n]
                    dve.wait_ge(sem("scores"), H * TB + (q + 1))
                    ci = CT[:, q, H:H + 1] if isinstance(b, int) else CT[:, q, bass.ds(H, 1)]
                    dve.scalar_tensor_tensor(pr, PS[:, 4 + q, 0:n], ci, W[8 + h][:, 0:n], ALU.add,
                                             ALU.subtract).then_inc(sem("scores_read"), 1)
                    dve.wait_ge(sem("scores_read"), H * TB + (q + 1))
                    dve.tensor_reduce(NEGM[:, q:q + 1], pr, AX.X, ALU.max, negate=True).then_inc(sem("score_max"), 1)
                for q in range(TB):
                    dve.wait_ge(sem("exp"), H * TB + (q + 1))
                    dve.reciprocal(RINV[:, q:q + 1], RS[:, q:q + 1]).then_inc(sem("rinv"), 1)

            def low_probs(b, h):
                H = 2 * b + h
                for j in range(TB):
                    n = (TB - j) * P
                    dve.wait_ge(sem("pt_high"), H * TB + (j + 1))
                    dve.tensor_tensor(PTL[j % 2][:, 0:n], PS[:, 4 + j, 0:n], PTH[j % 2][:, 0:n].bitcast(F32),
                                      ALU.subtract).then_inc(sem("pt_low"), 1)
                r = slice(HD * h, HD * h + HD)
                dve.wait_ge(sem("weighed"), H * TB + TB)
                dve.tensor_tensor(W[6][r, 0:S], PS[r, 2, :], W[6][r, 0:S], ALU.mult).then_inc(sem("o_read"), 1)

            def low_out(b):
                dve.wait_ge(sem("o_high"), b + 1)
                dve.tensor_tensor(tile(OL, b), W[6][:, 0:S], tile(OH, b).bitcast(F32), ALU.subtract).then_inc(sem("o_low"), 1)

            def head_norm(n, gain, high, low):
                dve.wait_ge(sem("hn_sum"), n + 1)
                dve.tensor_scalar(W[3][:, 0:S], PS[:, 3, :], 1.0 / HD, EPS, ALU.mult, ALU.add).then_inc(sem("hn_v"), 1)
                newton(W[3][:, 0:S], W[2][:, 0:S], W[4][:, 0:S], sem("hn_rr"), n + 1, W[4][:, 0:S])
                dve.scalar_tensor_tensor(W[1][:, 0:S], W[1][:, 0:S], PRM[:, gain:gain + 1], W[4][:, 0:S],
                                         ALU.mult, ALU.mult).then_inc(sem("hn_x"), 1)
                dve.wait_ge(sem("hn_high"), n + 1)
                dve.tensor_tensor(low[:, :], W[1][:, 0:S], high[:, :].bitcast(F32), ALU.subtract).then_inc(sem("hn_low"), 1)

            def attention():
                for m in range(KT):
                    dve.wait_ge(sem("x2_high"), m + 1)
                    dve.scalar_tensor_tensor(X2L[:, m, :], XT[:, m, :], PRM[:, R_KV + m:R_KV + m + 1],
                                             X2H[:, m, :].bitcast(F32), ALU.mult, ALU.subtract).then_inc(sem("x2_low"), 1)
                norm(1)
                dve.wait_ge(unit_done, ph["forget"].unit(0, 0) + 1)
                link(dve.tensor_tensor(W[1][:, 0:S], PS[:, 0, :], W[0][:, 0:S], ALU.mult))
                dve.tensor_scalar(W[1][:, 0:S], W[1][:, 0:S], PRM[:, R_BF:R_BF + 1], None, ALU.add).then_inc(sem("fg_z"), 1)
                link(dve.memset(W[5][:, 0:S], 1.0))
                dve.wait_ge(sem("fg_sp"), 1)
                link(dve.scalar_tensor_tensor(W[3][:, 0:S], W[1][:, 0:S], 0.0, W[2][:, 0:S], ALU.min, ALU.subtract))
                dve.tensor_tensor_scan(W[4][:, 0:S], W[5][:, 0:S], W[3][:, 0:S], 0.0, ALU.mult, ALU.add).then_inc(sem("fg_c"), 1)
                dve.wait_ge(sem("fg_t"), 1)
                dve.tensor_copy(CT[:, :, :], PS[:, 1, :].rearrange("p (t c) -> p t c", t=TB)[:, :, P - HEADS:P]).then_inc(sem("fg_ct"), 1)
                dve.wait_ge(sem("fg_ct"), 1)
                p = ph["attn"]
                def read(i, j, w, name, n):
                    dve.wait_ge(unit_done, p.unit(i, j) + 1)
                    if j == 2 or (j == 0 and not (isinstance(i, int) and i == 0)):
                        dve.wait_ge(sem("hn_low"), i * 2 + j // 2)
                    if j == 3 and not (isinstance(i, int) and i == 0):
                        dve.wait_ge(sem("o_low"), i * 1)
                    dve.tensor_tensor(W[w][:, 0:S], PS[:, j % 2, :], W[0][:, 0:S], ALU.mult).then_inc(sem(name), 1)
                def body(i):
                    first = isinstance(i, int) and i == 0
                    if first:
                        dve.wait_ge(sem("cums_stored"), 16)
                    read(i, 0, 1, "kq_read", i * 2)
                    if not first:
                        softmax(i - 1, 0)
                    read(i, 1, 5, "vg_read", i * 2)
                    if not first:
                        low_probs(i - 1, 0)
                        softmax(i - 1, 1)
                    head_norm(i * 2, R_KN, KH, KL)
                    read(i, 2, 1, "kq_read", i * 2 + 1)
                    if not first:
                        low_probs(i - 1, 1)
                        low_out(i - 1)
                    head_norm(i * 2 + 1, R_QN, QH, QL)
                    read(i, 3, 6, "vg_read", i * 2 + 1)
                    dve.wait_ge(sem("g_exp"), i + 1)
                    link(dve.tensor_scalar(W[6][:, 0:S], W[6][:, 0:S], 1.0, None, ALU.add))
                    link(dve.reciprocal(W[6][:, 0:S], W[6][:, 0:S]))
                    dve.wait_ge(sem("v_high"), i + 1)
                    dve.tensor_tensor(VL[:, :, :], PS[:, 3, :].rearrange("p (t c) -> p t c", t=TB),
                                      VH[:, :, :].bitcast(F32), ALU.subtract).then_inc(sem("v_low"), 1)
                body(0)
                loop(dve, PAIRS, body, steps, start=1)
                for h in range(2):
                    softmax(PAIRS - 1, h)
                    low_probs(PAIRS - 1, h)
                low_out(PAIRS - 1)

            def gates():
                dve.memset(UP[:, :], 0.0).then_inc(sem("up_zeroed"), 1)
                norm(3)
                dve.wait_ge(unit_done, ph["lr"].unit(0, 0) + 1)
                r = slice(0, 2 * GATE_RANK)
                dve.tensor_tensor(W[1][r, 0:S], PS[r, 0, :], W[0][r, 0:S], ALU.mult).then_inc(sem("lr"), 1)
                link(dve.memset(W[7][:, 0:S], 1.0))
                link(dve.memset(W[7][:, 0:S:CH], 0.0))
                def cumulate(t):
                    z, sp, lg = W[2 + t % 2][:, 0:S], W[4 + t % 2][:, 0:S], W[6][:, 0:S]
                    dve.wait_ge(sem("z_sp"), t + 1)
                    link(dve.scalar_tensor_tensor(lg, z, 0.0, sp, ALU.min, ALU.subtract))
                    link(dve.tensor_scalar(lg, lg, 1.0 / 16.0, -0.5, ALU.mult, ALU.max))
                    o = BC[:, t, :]
                    if t >= GH:
                        lg, o = lg[:, ::-1], o[:, ::-1]
                    link(dve.tensor_tensor_scan(o, W[7][:, 0:S], lg, 0.0, ALU.mult, ALU.add))
                for t in range(2 * GH):
                    dve.wait_ge(sem("z"), t + 1)
                    dve.tensor_scalar(W[2 + t % 2][:, 0:S], PS[:, 1 + t % 2, :], PRM[:, R_GBF + t:R_GBF + t + 1], None,
                                      ALU.add).then_inc(sem("z_read"), 1)
                    if t > 0:
                        cumulate(t - 1)
                cumulate(2 * GH - 1)
                dve.wait_ge(sem("g_masks"), 16)

            def gla(i):
                p = ph["gla"]
                later = not isinstance(i, int) or i > 0
                if later:
                    dve.wait_ge(sem("g_ylow"), i * 2)
                for j in range(6):
                    dve.wait_ge(unit_done, p.unit(i, j) + 1)
                    if j == 0:
                        ins = dve.scalar_tensor_tensor(W[1][:, 0:S], PS[:, 0, :], GDK ** -0.5, W[0][:, 0:S], ALU.mult, ALU.mult)
                    else:
                        ins = dve.tensor_tensor(W[1 + j][:, 0:S], PS[:, j, :], W[0][:, 0:S], ALU.mult)
                    ins.then_inc(sem("g_read"), 1)
                for u in range(2):
                    r, e = W[5 + u][:, 0:S], W[7 + u][:, 0:S]
                    dve.wait_ge(sem("g_rexp"), i * 2 + (u + 1))
                    link(dve.tensor_scalar(e, e, 1.0, None, ALU.add))
                    link(dve.reciprocal(e, e))
                    ins = dve.tensor_tensor(r, r, e, ALU.mult)
                    if u == 0:
                        link(ins)
                    else:
                        ins.then_inc(sem("g_silu"), 1)
                for b in range(2):
                    dve.wait_ge(sem("gv_high"), i * 2 + (b + 1))
                    dve.tensor_tensor(VGL[:, 2 * b:2 * b + 2, :], PS[:, b, :].rearrange("p (t c) -> p t c", t=2),
                                      VGH[:, 2 * b:2 * b + 2, :].bitcast(F32), ALU.subtract).then_inc(sem("gv_low"), 1)
                for d in range(2):
                    n = 2 * i + d
                    w7, w8 = W[7][:, 0:S], W[8][:, 0:S]
                    dve.wait_ge(sem("g_e"), n * 2 + 2)
                    link(dve.tensor_copy(EBL, W[7][:, CH - 1:S:CH] if d == 0 else W[7][:, 0:S:CH]))
                    dve.tensor_tensor(w7, W[1][:, 0:S], w7, ALU.mult).then_inc(sem("g_qk"), 1)
                    dve.tensor_tensor(w8, W[2][:, 0:S], w8, ALU.mult).then_inc(sem("g_qk"), 1)
                    dve.wait_ge(sem("gd_high"), n * 3 + 1)
                    dve.tensor_tensor(QDL[:, :], w7, QDH[:, :].bitcast(F32), ALU.subtract).then_inc(sem("gd_low"), 1)
                    dve.wait_ge(sem("gd_high"), n * 3 + 2)
                    dve.tensor_tensor(KIL[:, :], w8, KIH[:, :].bitcast(F32), ALU.subtract).then_inc(sem("gd_low"), 1)
                    dve.wait_ge(sem("gd_low"), n * 3 + 2)
                    dve.tensor_tensor(w8.rearrange("p (n c) -> p n c", n=NCH), w8.rearrange("p (n c) -> p n c", n=NCH),
                                      EBL.unsqueeze(2).to_broadcast([P, NCH, CH]), ALU.mult).then_inc(sem("g_kt"), 1)
                    dve.wait_ge(sem("gd_high"), n * 3 + 3)
                    dve.tensor_tensor(KTL[:, :], PS[:, 4, :], KTH[:, :].bitcast(F32), ALU.subtract).then_inc(sem("gd_low"), 1)
                    if d == 1:
                        dve.wait_ge(sem("g_scores"), i * 2 + 2)
                        for k, w in ((0, w7), (1, w8)):
                            link(dve.tensor_tensor(w.rearrange("p (t c) -> p t c", t=TB),
                                                   PS[:, 2 + k, :].rearrange("p (t c) -> p t c", t=TB),
                                                   GMASK[k].unsqueeze(1).to_broadcast([P, TB, P]), ALU.mult))
                        dve.tensor_tensor(w7, w7, w8, ALU.add).then_inc(sem("g_sc"), 1)
                        dve.wait_ge(sem("g_sc_high"), i + 1)
                        dve.tensor_tensor(SCL[:, :], w7, SCH[:, :].bitcast(F32), ALU.subtract).then_inc(sem("g_sc_low"), 1)
                    def low_state(s):
                        dve.wait_ge(sem("g_state_high"), n * (NCH - 1) + (s + 1))
                        dve.tensor_tensor(SL[:, s, :], ST[s % 2][:, :], SH[:, s, :].bitcast(F32),
                                          ALU.subtract).then_inc(sem("g_state_low"), 1)
                    for s, c in enumerate(chunk_order(d)):
                        bank, cols = kv_place(c)
                        dve.wait_ge(sem("g_kv"), n * (NCH - 1) + (4 if s < 4 else NCH - 1))
                        if s >= 2:
                            dve.wait_ge(sem("g_state_low"), n * (NCH - 1) + (s - 1))
                        elif s < 2 and (d == 1 or later):
                            dve.wait_ge(sem("g_state_low"), n * (NCH - 1))
                        if s == 0:
                            ins = dve.tensor_copy(ST[0][:, :], PS[:, bank, cols])
                        else:
                            dve.wait_ge(sem("g_st"), n * (NCH - 1) + s)
                            ins = dve.scalar_tensor_tensor(ST[s % 2][:, :], ST[(s + 1) % 2][:, :], EBL[:, c:c + 1],
                                                           PS[:, bank, cols], ALU.mult, ALU.add)
                        ins.then_inc(sem("g_st"), 1)
                        if s > 0:
                            low_state(s - 1)
                    low_state(NCH - 2)
                dve.wait_ge(sem("g_sum"), i + 1)
                dve.tensor_scalar(W[1][:, 0:S], PS[:, 0, :], 1.0 / (2 * P), EPS, ALU.mult, ALU.add).then_inc(sem("g_nv"), 1)
                newton(W[1][:, 0:S], W[2][:, 0:S], W[7][:, 0:S], sem("g_nrr"), i + 1, W[7][:, 0:S])
                for u in range(2):
                    o = W[3 + u][:, 0:S]
                    link(dve.scalar_tensor_tensor(o, PS[:, 6 + u, :], PRM[:, R_OUTG + u:R_OUTG + u + 1], W[7][:, 0:S],
                                                  ALU.mult, ALU.mult))
                    dve.tensor_tensor(o, o, W[5 + u][:, 0:S], ALU.mult).then_inc(sem("g_y"), 1)
                for u in range(2):
                    dve.wait_ge(sem("g_yhigh"), i * 2 + (u + 1))
                    dve.tensor_tensor(tile(YGL, i * 2 + u), W[3 + u][:, 0:S], tile(YGH, i * 2 + u).bitcast(F32),
                                      ALU.subtract).then_inc(sem("g_ylow"), 1)

            def swa(i):
                p = ph["swa"]
                if isinstance(i, int) and i == 0:
                    dve.wait_ge(sem("rope"), 32)
                    dve.wait_ge(sem("sinks"), 16)
                later = not isinstance(i, int) or i > 0
                w = [W[k][:, 0:S] for k in range(10)]
                def read(j, to):
                    dve.wait_ge(unit_done, p.unit(i, j) + 1)
                    dve.tensor_tensor(to, PS[:, (0, 1, 2, 3, 0, 1)[j], :], w[0], ALU.mult).then_inc(sem("sw_read"), 1)
                def finish(n, gain, high, low):
                    dve.wait_ge(sem("sw_sum"), i * 5 + (n + 1))
                    dve.tensor_scalar(w[3], PS[:, 4, :], 1.0 / P, EPS, ALU.mult, ALU.add).then_inc(sem("sw_v"), 1)
                    newton(w[3], w[2], w[4], sem("sw_rr"), i * 5 + (n + 1), w[4])
                    link(dve.scalar_tensor_tensor(w[5], w[1], PRM[:, gain:gain + 1], w[4], ALU.mult, ALU.mult))
                    dve.tensor_tensor(W[6][64:128, 0:S], W[5][0:64, 0:S], W[8][0:64, 0:S], ALU.mult)
                    link(dve.tensor_tensor(W[6][0:64, 0:S], W[5][64:128, 0:S], W[8][64:128, 0:S], ALU.mult))
                    link(dve.tensor_tensor(w[5], w[5], w[7], ALU.mult))
                    dve.tensor_tensor(w[1], w[5], w[6], ALU.add).then_inc(sem("sw_x"), 1)
                    dve.wait_ge(sem("sw_high"), i * 5 + (n + 1))
                    dve.tensor_tensor(low[:, :], w[1], high[:, :].bitcast(F32), ALU.subtract).then_inc(sem("sw_low"), 1)
                read(0, w[1])
                read(1, w[9])
                finish(0, R_SKG, SKH, SKL)
                dve.wait_ge(sem("sw_low"), i * 5 + 1)
                read(2, w[1])
                dve.wait_ge(sem("sv_high"), i + 1)
                dve.tensor_tensor(SVL[:, :, :], PS[:, 5, :].rearrange("p (t c) -> p t c", t=TB),
                                  SVH[:, :, :].bitcast(F32), ALU.subtract).then_inc(sem("sv_low"), 1)
                for t in range(SWA_Q):
                    finish(t + 1, R_SQG, SQH[t], SQL[t])
                    if t < SWA_Q - 1:
                        dve.wait_ge(sem("sw_low"), i * 5 + (t + 2))
                        read(t + 3, w[1])
                for q in range(TB):
                    win, n = WIN[q], i * 4 * TB + 4 * q
                    for t in range(SWA_Q):
                        dve.wait_ge(sem("sw_scores"), n + (t + 1))
                        link(dve.tensor_reduce(COL[:, 20 + t:21 + t], PS[:, 4 + t, 0:len(win) * P], AX.X, ALU.max))
                        dve.tensor_scalar(NEGM[:, t:t + 1], COL[:, 20 + t:21 + t], column(SINK, i * SWA_Q + t), -1.0,
                                          ALU.max, ALU.mult).then_inc(sem("sw_max"), 1)
                    dve.wait_ge(sem("sw_exp"), n + 4)
                    link(dve.tensor_tensor(RINV[:, :], RS[:, :], ESK[:, :], ALU.add))
                    dve.reciprocal(RINV[:, :], RINV[:, :]).then_inc(sem("sw_rinv"), 1)
                    for jj in range(len(win)):
                        dve.wait_ge(sem("sw_phigh"), i * SEEN[TB] + (SEEN[q] + jj + 1))
                        dve.tensor_tensor(SPL[:, :], PS[:, jj, :], SPH[:, :].bitcast(F32), ALU.subtract).then_inc(sem("sw_plow"), 1)
                    dve.wait_ge(sem("sw_ohigh"), i * TB + (q + 1))
                    dve.tensor_tensor(window_out(YSL, i, q), PS[:, 3, :].rearrange("p (t c) -> p t c", t=SWA_Q),
                                      window_out(YSH, i, q).bitcast(F32), ALU.subtract).then_inc(sem("sw_out"), 1)

            def merge(i):
                p = ph["merge"]
                for k in range(2):
                    dve.wait_ge(unit_done, p.unit(i, k) + 1)
                    dve.tensor_tensor(W[1 + k][:, 0:S], PS[:, k, :], W[0][:, 0:S], ALU.mult).then_inc(sem("mg_read"), 1)
                for k in range(2):
                    dve.wait_ge(unit_done, p.unit(i, 2 + k) + 1)
                    dve.wait_ge(sem("mg_sig"), i * 2 + (k + 1))
                    dve.tensor_tensor(W[3 + k][:, 0:S], PS[:, 2 + k, :], W[1 + k][:, 0:S], ALU.mult).then_inc(sem("mg_read"), 1)
                dve.wait_ge(sem("mg_read"), i * 4 + 4)
                dve.tensor_tensor(W[3][:, 0:S], W[3][:, 0:S], W[4][:, 0:S], ALU.add).then_inc(sem("mg"), 1)
                dve.wait_ge(sem("mg_high"), i + 1)
                dve.tensor_tensor(tile(MGL, i), W[3][:, 0:S], tile(MGH, i).bitcast(F32), ALU.subtract).then_inc(sem("mg_low"), 1)

            link(dve.memset(PROW[:, :, :], 0.0))
            dve.memset(EPSC, EPS)
            dve.memset(ONEC, 1.0).then_inc(sem("zeroed"), 1)
            dve.wait_ge(sem("consts"), 16)
            for to, c in ((IDF, C_ID), (ONE, C_ONE), (ONE64, C_ONE64), (IDB, C_ID), (MCAUSAL, C_CAUSAL), (MUPPER, C_UPPER)):
                ins = dve.tensor_copy(to[:, :], CST[:, c:c + P])
            ins.then_inc(sem("prm_ready"), 1)
            dve.wait_ge(sem("prm_t"), 1)
            dve.tensor_copy(PRM[:, :], PS[:, 2, 0:N_PRM])
            link(dve.tensor_copy(FC[:, 0:N_FC], PS[:, 2, P:P + N_FC]))
            dve.tensor_copy(FC[:, N_FC:2 * N_FC], PS[:, 2, 2 * P:2 * P + N_FC]).then_inc(sem("prm_ready"), 1)
            dve.tensor_scalar(PRM[:, R_QN:R_QN + 1], PRM[:, R_QN:R_QN + 1], HD ** -0.5, None, ALU.mult)
            dve.tensor_scalar(PRM[:, R_SQG:R_SQG + 1], PRM[:, R_SQG:R_SQG + 1], 128 ** -0.5, None,
                              ALU.mult).then_inc(sem("prm_ready"), 1)
            dve.wait_ge(sem("prm_ready"), 3)

            def take_x(i, t, m):
                dve.wait_ge(sem("xt"), m + 1)
                return dve.tensor_copy(XT[:, m, :], PS[:, m % 2, :])
            residual("_x", 1, KT, [(XH, XL, R_ATTN)], take_x)
            norm("_x")
            link(dve.memset(W[1][:, 0:2], 0.0))
            p = ph["mix"]
            def mix(i):
                dve.wait_ge(unit_done, p.unit(i, 0) + 1)
                dve.tensor_tensor(W[5][:, 0:S], PS[:, 0, :], W[0][:, 0:S], ALU.mult).then_inc(sem("mix_c"), 1)
                dve.wait_ge(unit_done, p.unit(i, 1) + 1)
                dve.tensor_tensor(W[6][:, 0:S], PS[:, 1, :], W[0][:, 0:S], ALU.mult).then_inc(sem("mix_h"), 1)
                dve.wait_ge(sem("mix_h"), i + 1)
                link(dve.tensor_tensor(W[1][:, 2:S + 2], W[5][:, 0:S], W[6][:, 0:S], ALU.mult))
                link(conv(W[1], W[3][:, 0:S], [column(PRM, i + R_ACONV + k * KT) for k in range(3)]))
                dve.wait_ge(unit_done, p.unit(i, 2) + 1)
                dve.tensor_tensor(W[5][:, 0:S], PS[:, 2, :], W[0][:, 0:S], ALU.mult).then_inc(sem("mix_b"), 1)
                dve.wait_ge(sem("mix_b"), i + 1)
                dve.tensor_tensor(W[4][:, 0:S], W[5][:, 0:S], W[3][:, 0:S], ALU.mult).then_inc(sem("mix_bu"), 1)
                dve.wait_ge(sem("mix_high"), i + 1)
                dve.tensor_tensor(tile(BUL, i), W[4][:, 0:S], tile(BUH, i).bitcast(F32), ALU.subtract).then_inc(sem("mix_low"), 1)
            loop(dve, KT, mix, steps)
            residual(0, 2, 4, [(XH, XL, R_FFN)] if stop > 1 else [], add_products(ph["mix_out"], 1))
            if stop > 1:
                ffn(0, 0, True, [(XH, XL, R_ATTN + KT)] if stop > 2 else [])
            if stop > 2:
                attention()
                residual(2, 2, 4, [(XH, XL, R_FFN + KT)] if stop > 3 else [], add_products(ph["attn_out"], 1))
            if stop > 3:
                ffn(1, 2, True, [(XH, XL, R_MIX)] if stop > 4 else [])
            if stop > 4:
                gates()
                loop(dve, GH, gla, steps)
                loop(dve, SWA_GROUPS, swa, steps)
                loop(dve, KT, merge, steps)
                residual(4, 2, 4, [(XH, XL, R_FFN2)] if stop > 5 else [], add_products(ph["out2"], 1))
            if stop > 5:
                ffn(2, 4, False, [])
            for t in range(TB):
                for h in range(2):
                    n = 2 * t + h
                    dve.wait_ge(sem("out_t"), n + 1)
                    dve.tensor_copy(XIN[:, t, h * S:(h + 1) * S], PS[:, 2 + n % 2, :]).then_inc(sem("out_rows"), 1)


def PARAM_DMAS(PROW, T):
    def tall(a):
        return a.rearrange("(k p) -> k p", p=P)
    d = []
    for row, a in ((R_ATTN, T["attn_norm"][0]), (R_ATTN + KT, T["attn_norm"][1]), (R_FFN, T["ffn_norm"][0]),
                   (R_FFN + KT, T["ffn_norm"][1]), (R_KV, T["kv_norm"]), (R_MIX, T["norm_mix_g_2"][0]),
                   (R_FFN2, T["norm_ffn_g_2"][0]), (R_ACONV, T["a_conv"][0, 0]), (R_ACONV + KT, T["a_conv"][0, 1]),
                   (R_ACONV + 2 * KT, T["a_conv"][0, 2]), (R_GBF, T["gla_gate_bias_fwd_2"][0]),
                   (R_GBB, T["gla_gate_bias_bwd_2"][0]), (R_OUTG, T["gla_out_norm_g_2"][0]),
                   (R_SQG, T["swa_q_norm_g_2"][0]), (R_SKG, T["swa_k_norm_g_2"][0])):
        n = a.shape[0] // P
        d.append((PROW[row:row + n, 0, :], tall(a)))
    for row, a in ((R_QN, T["q_norm"][0]), (R_KN, T["k_norm"])):
        for h in range(2):
            d.append((PROW[row:row + 1, 0, h * HD:(h + 1) * HD], a.rearrange("(k p) -> k p", p=HD)))
    d.append((PROW[R_BF:R_BF + 1, 0, P - HEADS:P], T["b_f"].rearrange("(k p) -> k p", p=HEADS)))
    for l in range(2):
        for k in range(3):
            d.append((PROW[k * FT:(k + 1) * FT, 1 + l, :], tall(T["ffn_conv"][l, k])))
    return d


N_PARAM_DMAS = 15 + 4 + 1 + 6


def constants():
    c = np.zeros((P, N_CONST), np.float32)
    r = np.arange(P)
    row, column = r[:, None], r[None, :]
    c[:, C_ID:C_ID + P] = np.eye(P)
    c[:, C_ONE:C_ONE + P] = 1.0
    c[:, C_ONE64:C_ONE64 + P] = row // HD == column // HD
    c[:, C_CAUSAL:C_CAUSAL + P] = np.where(column <= row, 0.0, NEG)
    c[:, C_UPPER:C_UPPER + P] = np.where(column >= row, 0.0, NEG)
    same = row // CH == column // CH
    c[:, C_GF:C_GF + P] = same & (row <= column)
    c[:, C_GB:C_GB + P] = same & (row > column)
    half = P // 2
    inv = (np.float32(10000.0) ** (-np.arange(half, dtype=np.float32) / np.float32(half))).astype(np.float32)
    ang = np.concatenate([inv, inv])[:, None] * np.arange(S, dtype=np.float32)[None, :]
    c[:, C_COS:C_COS + S] = np.cos(ang)
    c[:, C_SIN:C_SIN + S] = np.where(row < half, 1.0, -1.0) * np.sin(ang)
    return c


STOP = 6


def kernel(**inputs):
    import concourse.bacc as bacc
    from concourse.bass_utils import run_bass_kernel_spmd as run

    nc = bacc.Bacc("TRN2", target_bir_lowering=False, num_devices=1)
    arrays, T = {}, {}
    for name, a in {**inputs, "consts": constants()}.items():
        a = np.ascontiguousarray(a)
        arrays[f"in_{name}"] = a
        T[name] = nc.dram_tensor(f"in_{name}", a.shape, F32, kind="ExternalInput").ap()
    out = nc.dram_tensor("out", (1, S, D), F32, kind="ExternalOutput").ap()
    build(nc, T, out, STOP)
    r = run(nc, [arrays], core_ids=[0])
    return r.results[0]["out"]
```

```python
from contextlib import ExitStack

import numpy as np

import concourse.bass as bass
from concourse import mybir

F32 = mybir.dt.float32
F32R = mybir.dt.float32r
BF16 = mybir.dt.bfloat16
ACT = mybir.ActivationFunctionType
ALU = mybir.AluOpType
AX = mybir.AxisListType

P = 128
S = 512
D = 1024
KT = D // P
TB = S // P
FF = 2816
FT = FF // P
EPS = 1e-6
NEG = -1e30

HEADS = 16
HD = D // HEADS
PAIRS = HEADS // 2

GH = 4
GDK = 128
CH = 64
NCH = S // CH
GATE_RANK = 16
SWA_GROUPS = 2
SWA_Q = 4
G_Q, G_K, G_V, G_R, G_LR = 0, 512, 1024, 2048, 3072
S_Q, S_K, S_V, GA, GB = 3104, 4128, 4384, 4640, 5664

(R_ATTN, R_FFN, R_KV, R_MIX, R_FFN2, R_ACONV, R_GBF, R_GBB, R_OUTG, R_SQG, R_SKG, R_QN, R_KN,
 R_BF) = (0, 16, 32, 40, 48, 56, 80, 84, 88, 90, 91, 92, 93, 94)
N_PRM = 96
N_FC = 3 * FT
C_ID, C_ONE, C_ONE64, C_CAUSAL, C_UPPER, C_GF, C_GB, C_COS = 0, 128, 256, 384, 512, 640, 768, 896
C_SIN = C_COS + S
N_CONST = C_SIN + S


class WeightPhase:

    def __init__(self, stream, ring, iters, units):
        self.ring, self.iters, self.units, self.U = ring, iters, units, len(units)
        assert iters == 1 or self.U % ring == 0
        self.base = stream["units"]
        self.owner = list(stream["owner"])
        self.loads0 = list(stream["loads"])
        stream["units"] += self.U * iters
        for n in range(self.U * iters):
            s = (n % self.U) % ring
            stream["owner"][s] = self.base + n
            stream["loads"][s] += 1

    def unit(self, i, j):
        return i * self.U + (self.base + j)

    def slot(self, j):
        return j % self.ring

    def load_count(self, i, j):
        return i * (self.U // self.ring if self.iters > 1 else 0) + (self.loads0[self.slot(j)] + j // self.ring + 1)

    def before(self, i, j):
        if j >= self.ring or not isinstance(i, int) or i > 0:
            return i * self.U + (self.base + j - self.ring + 1)
        last = self.owner[self.slot(j)]
        return None if last is None else last + 1


class Steps:

    def __init__(self, engine, sem):
        self.engine, self.sem = engine, sem
        self.base, self.n, self.i, self.stride, self.start = 0, 0, 0, None, 0

    def enter_loop(self, start):
        self.base, self.n, self.i, self.stride, self.start = self.base + self.n, 0, 0, None, start

    def enter(self, i):
        self.i, self.n = i, 0

    def leave_iteration(self):
        if self.stride is None:
            self.stride = self.n
        assert self.stride == self.n

    def leave_loop(self, iters):
        self.base += (self.stride or 0) * iters
        self.i, self.n, self.stride, self.start = 0, 0, None, 0

    def value(self):
        if isinstance(self.i, int):
            return self.base + self.n + (self.i - self.start) * (self.stride or 0)
        return self.i * self.stride + (self.base + self.n - self.start * self.stride)

    def link(self, ins):
        self.n += 1
        ins.then_inc(self.sem, 1)
        self.engine.wait_ge(self.sem, self.value())


def loop(engine, iters, body, steps=None, start=0):
    def one(i):
        if steps:
            steps.enter(i)
        body(i)
        if steps:
            steps.leave_iteration()
    if steps:
        steps.enter_loop(start)
    one(start)
    if iters > start + 1:
        with engine.Fori(start + 1, iters) as i:
            one(i)
    if steps:
        steps.leave_loop(iters - start)


def build(nc, T, out, stop=99):
    with ExitStack() as ctx:
        sems = {}

        def sem(name):
            if name not in sems:
                sems[name] = ctx.enter_context(nc.semaphore(name))
            return sems[name]

        pos = [(nc.sbuf_base + 31) // 32 * 32]

        def at(name, shape, dt, offset=None):
            size = int(np.prod(shape[1:])) * (2 if dt == BF16 else 4)
            if offset is None:
                offset = pos[0]
                pos[0] += (size + 31) // 32 * 32
            return nc.alloc_sbuf_tensor_at(name, shape, dt, offset=offset)

        XT = at("XT", [P, KT, S], F32)
        XH = at("XH", [P, KT, S], F32R)
        XL = at("XL", [P, KT, S], F32R)
        raw_at, RAW = [], []
        for s in range(4):
            raw_at.append(pos[0])
            RAW.append(at(f"RAW{s}", [P, KT, P], F32))
        ring_at = []
        WH, WL = [], []
        for s in range(4):
            ring_at.append(pos[0])
            WH.append(at(f"WH{s}", [P, KT, P], F32R))
            WL.append(at(f"WL{s}", [P, KT, P], F32R))
        W_at = []
        W = []
        for s in range(10):
            W_at.append(pos[0])
            W.append(at(f"W{s}", [P, S + 8], F32))
        IDF = at("IDF", [P, P], F32)
        ONE = at("ONE", [P, P], F32)
        ONE64 = at("ONE64", [P, P], F32)
        IDB = at("IDB", [P, P], BF16)
        MCAUSAL = at("MCAUSAL", [P, P], BF16)
        MUPPER = at("MUPPER", [P, P], BF16)
        PRM = at("PRM", [P, N_PRM], F32)
        FC = at("FC", [P, 2 * N_FC], F32)
        SINK = at("SINK", [P, 8], F32)
        COL = at("COL", [P, 40], F32)
        EPSC, ONEC, TICK = COL[:, 0:1], COL[:, 1:2], COL[:, 2:3]
        NEGM, RS, RINV = COL[:, 4:8], COL[:, 8:12], COL[:, 12:16]
        SNEG, SRS, SINV, SESK = [[COL[:, c + d:c + d + 4] for d in (0, 16)] for c in (4, 8, 12, 16)]
        SMAX = COL[:, 36:40]
        BIG = pos[0]
        assert BIG + 2 * FT * S * 4 <= nc.sbuf_usable_end, (BIG, nc.sbuf_usable_end)
        KB = 1024
        XIN = at("XIN", [P, TB, D], F32, BIG)
        PROW = at("PROW", [P, 3, P], F32, BIG + 16 * KB)
        CST = at("CST", [P, C_GF], F32, BIG + 18 * KB)
        BUH = at("BUH", [P, KT, S], F32R, BIG + 32 * KB)
        BUL = at("BUL", [P, KT, S], F32R, BIG + 48 * KB)
        HH = at("HH", [P, FT, S], F32R, BIG)
        HL = at("HL", [P, FT, S], F32R, BIG + 44 * KB)
        X2H = at("X2H", [P, KT, S], F32R, BIG)
        X2L = at("X2L", [P, KT, S], F32R, BIG + 16 * KB)
        OH = at("OH", [P, KT, S], F32R, BIG + 32 * KB)
        OL = at("OL", [P, KT, S], F32R, BIG + 48 * KB)
        KH, KL, QH, QL = [at(n, [P, S], F32R, BIG + (64 + 2 * k) * KB) for k, n in enumerate(("KH", "KL", "QH", "QL"))]
        VH = at("VH", [P, TB, P], F32R, BIG + 72 * KB)
        VL = at("VL", [P, TB, P], F32R, BIG + 74 * KB)
        PTH = [at(f"PTH{k}", [P, S], F32R, BIG + (76 + 2 * k) * KB) for k in range(2)]
        PTL = [at(f"PTL{k}", [P, S], F32R, BIG + (80 + 2 * k) * KB) for k in range(2)]
        PQ = at("PQ", [P, 6 * P], F32, BIG + 84 * KB)
        CT = at("CT", [P, TB, HEADS], F32, BIG + 87 * KB)
        PROB = [PQ[:, 0:128], PQ[:, 128:384], PQ[:, 384:768], W[7][:, 0:S]]

        YGH = at("YGH", [P, KT, S], F32R, BIG)
        YGL = at("YGL", [P, KT, S], F32R, BIG + 16 * KB)
        BC = at("BC", [P, 2 * GH, S], F32, BIG + 32 * KB)
        QDH0, QDL0, KIH, KIL, KTH, KTL = [at(n, [P, S], F32R, BIG + (48 + 2 * k) * KB)
                                          for k, n in enumerate(("QDH0", "QDL0", "KIH", "KIL", "KTH", "KTL"))]
        QDH = [QDH0, at("QDH1", [P, S], F32R, ring_at[3])]
        QDL = [QDL0, at("QDL1", [P, S], F32R, ring_at[3] + 2 * KB)]
        T0, T1 = [at(f"T{k}", [P, S], F32, ring_at[3] + (4 + 2 * k) * KB) for k in range(2)]
        E = [at(f"E{k}", [P, S], F32, raw_at[3] + 2 * k * KB) for k in range(2)]
        VGH = at("VGH", [P, TB, 2 * P], F32R, BIG + 60 * KB)
        VGL = at("VGL", [P, TB, 2 * P], F32R, BIG + 64 * KB)
        SH = at("SH", [P, NCH - 1, 2 * P], F32R, BIG + 68 * KB)
        SL = at("SL", [P, NCH - 1, 2 * P], F32R, BIG + 75 * KB)
        ST = [at(f"ST{k}", [P, 2 * P], F32, BIG + (82 + k) * KB) for k in range(2)]
        SCH = at("SCH", [P, S], F32R, BIG + 84 * KB)
        SCL = at("SCL", [P, S], F32R, BIG + 86 * KB)
        SC0 = at("SC0", [P, S], F32, BIG + 86 * KB)
        UP = at("UP", [2 * GATE_RANK, 2 * GH * GDK], F32, BIG + 68 * KB)
        GMASK = [W[9][:, 0:P], W[9][:, P:2 * P]]
        EBL = [W[9][:, 2 * P + d * NCH:2 * P + (d + 1) * NCH] for d in range(2)]
        YSH = at("YSH", [P, KT, S], F32R, BIG + 32 * KB)
        YSL = at("YSL", [P, KT, S], F32R, BIG + 48 * KB)
        SKH, SKL = [at(n, [P, S], F32R, BIG + (64 + 2 * k) * KB) for k, n in enumerate(("SKH", "SKL"))]
        SVH, SVL = [at(n, [P, TB, P], F32R, BIG + (68 + 2 * k) * KB) for k, n in enumerate(("SVH", "SVL"))]
        SQH = [at(f"SQH{t}", [P, S], F32R, BIG + (72 + 4 * t) * KB) for t in range(SWA_Q)]
        SQL = [at(f"SQL{t}", [P, S], F32R, BIG + (74 + 4 * t) * KB) for t in range(SWA_Q)]
        SPH = [at("SPH0", [P, S], F32R, W_at[1]), at("SPH1", [P, S], F32R, raw_at[3])]
        SPL = [at("SPL0", [P, S], F32R, W_at[5]), at("SPL1", [P, S], F32R, raw_at[3] + 2 * KB)]
        SPROB = [[W[k][:, 0:3 * P] for k in (2, 3, 4, 6)],
                 [at(f"SPROB{t}", [P, 3 * P], F32, ring_at[3] + 2 * t * KB) for t in range(SWA_Q)]]
        MGH = at("MGH", [P, KT, S], F32R, BIG + 64 * KB)
        MGL = at("MGL", [P, KT, S], F32R, ring_at[2])

        WIN = [list(range(max(0, q - 1), min(TB - 1, q + 1) + 1)) for q in range(TB)]
        SEEN = [sum(len(w) for w in WIN[:q]) for q in range(TB + 1)]

        def chunk_order(d):
            return [n if d == 0 else NCH - 1 - n for n in range(NCH - 1)]

        def kv_place(n):
            bank = (0, 1)[n % 2] if n // 2 < 2 else (4, 5)[n % 2]
            return bank, slice(n // 2 % 2 * 2 * P, (n // 2 % 2 + 1) * 2 * P)

        PS = ctx.enter_context(nc.psum_tensor("PS", [P, 8, S], F32))
        cums = nc.dram_tensor("cums", (HEADS, S), F32, kind="Internal").ap()

        stream = {"units": 0, "owner": [None] * 4, "loads": [0] * 4}

        def rows(w):
            return w.rearrange("(k p) n -> p k n", p=P)

        def wphase(ring, iters, units):
            return WeightPhase(stream, ring, iters, units)

        def col(base, step=P):
            return lambda i: i * step + base

        a_in, a_out = rows(T["a_w_in"][0]), rows(T["a_w_out"][0])
        up = [rows(T["ffn_w_up"][l]) for l in range(2)] + [rows(T["w_ffn_in_2"][0])]
        down = [rows(T["ffn_w_down"][l]) for l in range(2)] + [rows(T["w_ffn_out_2"][0])]
        kvf, qg, b_out = rows(T["w_kvf"]), rows(T["b_w_qg"][0]), rows(T["b_w_out"][0])
        w_in, w_og, w_os, w_out = [rows(T[n][0]) for n in ("w_in_2", "w_o_gla_2", "w_o_swa_2", "w_out_2")]

        def square_units(w, n=4):
            return [(w, 0, KT, col(j * P, n * P)) for j in range(n)]

        def ffn_phases(l):
            u = []
            for p in range(2):
                u += [(up[l], 0, KT, col(p * P, 2 * P)), (up[l], 0, KT, col(FF + p * P, 2 * P))]
            d = []
            for p in range(2):
                d += [(down[l], k0, min(KT, FT - k0), col(p * P, 2 * P)) for k0 in (0, 8, 16)]
            return wphase(4, FT // 2, u), wphase(3, KT // 2, d)

        ph = {}
        ph["mix"] = wphase(3, KT, [(a_in, 0, KT, col(D)), (a_in, 0, KT, col(2 * D)), (a_in, 0, KT, col(0))])
        ph["mix_out"] = wphase(4, 2, square_units(a_out))
        if stop > 1:
            ph["up0"], ph["down0"] = ffn_phases(0)
        if stop > 2:
            ph["forget"] = wphase(4, 1, [(kvf, 0, KT, lambda i: 2 * D + HEADS - P)])
            ph["attn"] = wphase(4, PAIRS, [(kvf, 0, KT, col(0)), (kvf, 0, KT, col(D)),
                                           (qg, 0, KT, col(0)), (qg, 0, KT, col(D))])
            ph["attn_out"] = wphase(4, 2, square_units(b_out))
        if stop > 3:
            ph["up1"], ph["down1"] = ffn_phases(1)
        if stop > 4:
            ph["lr"] = wphase(4, 1, [(w_in, 0, KT, lambda i: G_LR)])
            ph["gla"] = wphase(3, GH, [(w_in, 0, KT, col(G_Q)), (w_in, 0, KT, col(G_K)),
                                       (w_in, 0, KT, col(G_V, 256)), (w_in, 0, KT, col(G_V + P, 256)),
                                       (w_in, 0, KT, col(G_R, 256)), (w_in, 0, KT, col(G_R + P, 256))])
            ph["swa"] = wphase(3, SWA_GROUPS, [(w_in, 0, KT, col(S_K))] +
                               [(w_in, 0, KT, col(S_Q + t * P, SWA_Q * P)) for t in range(SWA_Q)] +
                               [(w_in, 0, KT, col(S_V))])
            ph["merge"] = wphase(2, KT, [(w_in, 0, KT, col(GA)), (w_in, 0, KT, col(GB)),
                                         (w_og, 0, KT, col(0)), (w_os, 0, KT, col(0))])
            ph["out2"] = wphase(2, 2, square_units(w_out))
            stream["owner"][2] = stream["owner"][3] = stream["units"] - 1
        if stop > 5:
            ph["up2"], ph["down2"] = ffn_phases(2)

        loaded = [sem(f"weights_loaded{s}") for s in range(4)]
        high_done, split_done, unit_done = sem("weights_high"), sem("weights_split"), sem("unit_done")

        def tile(t, m):
            return t[:, m, :] if isinstance(m, int) else t[:, bass.ds(m, 1), :].rearrange("p a n -> p (a n)")

        def window_out(t, i, q):
            c = slice(q * P, (q + 1) * P)
            return t[:, i * SWA_Q:(i + 1) * SWA_Q, c] if isinstance(i, int) else t[:, bass.ds(i * SWA_Q, SWA_Q), c]

        def column(t, m):
            return t[:, m:m + 1] if isinstance(m, int) else t[:, bass.ds(m, 1)]

        ORDER = {"_x": 0, 0: 1, 1: 2, 2: 3, 3: 4, 4: 5, 5: 6}

        def tiles(n):
            return ORDER[n] * KT

        last_resid = min(stop, 6) - 1

        block = ctx.enter_context(nc.Block())

        @block.sync
        def _(sp):
            for t in range(TB):
                sp.dma_start(XIN[:, t, :], T["x"][0, t * P:(t + 1) * P, :]).then_inc(sem("x_loaded"), 16)
            for p in ph.values():
                def body(i, p=p):
                    for j, (w, k0, nk, c) in enumerate(p.units):
                        free = p.before(i, j)
                        if free is not None:
                            sp.wait_ge(split_done, free)
                            if not isinstance(i, int):
                                sp.sem_inc(sem("sync_step"), 1)
                        sp.dma_start(RAW[p.slot(j)][:, 0:nk, :], w[:, k0:k0 + nk, bass.ds(c(i), P)]).then_inc(
                            loaded[p.slot(j)], 16)
                loop(sp, p.iters, body)
            for t in range(TB):
                sp.wait_ge(sem("out_rows"), 2 * (t + 1))
                sp.dma_start(out[0, t * P:(t + 1) * P, :], XIN[:, t, :]).then_inc(sem("stored"), 16)
            sp.wait_ge(sem("stored"), 16 * TB)

        @block.gpsimd
        def _(pool):
            pool.wait_ge(sem("zeroed"), 1)
            for p in ph.values():
                def body(i, p=p):
                    for j, (w, k0, nk, c) in enumerate(p.units):
                        s = p.slot(j)
                        free = p.before(i, j)
                        if free is not None:
                            pool.wait_ge(unit_done, free)
                        pool.wait_ge(loaded[s], p.load_count(i, j) * 16)
                        if not isinstance(i, int):
                            pool.tensor_tensor(TICK, ONEC, ONEC, ALU.mult)
                        pool.tensor_scalar(WH[s][:, 0:nk, :], RAW[s][:, 0:nk, :], 1.0, 1.0, ALU.mult, ALU.mult).then_inc(high_done, 1)
                        pool.wait_ge(high_done, p.unit(i, j) + 1)
                        pool.tensor_tensor(WL[s][:, 0:nk, :], RAW[s][:, 0:nk, :], WH[s][:, 0:nk, :].bitcast(F32),
                                           ALU.subtract).then_inc(split_done, 1)
                loop(pool, p.iters, body)

        @block.tensor
        def _(pe):
            def unit(p, i, j, bank, xh, xl, first=True, last=True, ready=None):
                pe.wait_ge(split_done, p.unit(i, j) + 1)
                s, (_, k0, nk, _) = p.slot(j), p.units[j]
                for k in range(nk):
                    if ready:
                        pe.wait_ge(ready[0], ready[2] + ready[1] * (k0 + k + 1))
                    o = PS[:, bank, :]
                    pe.matmul(o, WH[s][:, k, :], xh[:, k0 + k, :], start=first and k == 0, stop=False)
                    pe.matmul(o, WH[s][:, k, :], xl[:, k0 + k, :], start=False, stop=False)
                    mm = pe.matmul(o, WL[s][:, k, :], xh[:, k0 + k, :], start=False, stop=last and k == nk - 1)
                mm.then_inc(unit_done, 1)

            def product(o, ah, al, bh, bl, start=True, stop=True, loose=False):
                pe.matmul(o, ah, bh, start=start, stop=False, skip_group_check=loose)
                pe.matmul(o, ah, bl, start=False, stop=False, skip_group_check=loose)
                return pe.matmul(o, al, bh, start=False, stop=stop, skip_group_check=loose)

            def row_sums(n):
                pe.wait_ge(sem("acc"), tiles(n) + KT)
                pe.matmul(PS[:, 7, :], ONE[:, :], W[1][:, 0:S], start=True, stop=True).then_inc(sem("nsum"), 1)

            def residual(p, n, groups, xh, xl, ready, banks_read):
                tpi = p.U // groups
                def body(i):
                    for t in range(tpi):
                        m = i * tpi + t
                        if t >= 2 or not isinstance(i, int) or i > 0:
                            pe.wait_ge(sem("resid"), tiles(n) + m - 1)
                        else:
                            pe.wait_ge(*banks_read[t])
                        for g in range(groups):
                            unit(p, i, t * groups + g, t % 2, xh, xl, g == 0, g == groups - 1,
                                 ready if isinstance(i, int) and i == 0 and t == 0 else None)
                loop(pe, p.iters, body)

            def ffn(l, n):
                pu, pd = ph[f"up{l}"], ph[f"down{l}"]
                def body(i):
                    for q in range(2):
                        m = 2 * i + q
                        for k in range(2):
                            if not isinstance(i, int) or i > 0:
                                pe.wait_ge(sem(f"ffn_{'ag'[k]}"), m + (l * FT - 1))
                            elif q == 0:
                                pe.wait_ge(sem("resid"), tiles(n) + KT - 1 + k)
                            unit(pu, i, 2 * q + k, 2 * q + k, XH, XL,
                                 ready=(sem("xld"), 1, tiles(n)) if isinstance(i, int) and i == 0 and q == k == 0 else None)
                            if isinstance(i, int) and i == 0 and q == k == 0:
                                row_sums(n)
                loop(pe, pu.iters, body)
                residual(pd, n + 1, 3, HH, HL, (sem("ffn_low"), 1, l * FT),
                         [(sem("ffn_a"), (l + 1) * FT), (sem("ffn_g"), (l + 1) * FT)])

            def scores(b, h):
                H, r = 2 * b + h, slice(HD * h, HD * h + HD)
                if h == 0:
                    pe.wait_ge(sem("hn_low"), 2 * b + 2)
                if not isinstance(b, int) or H > 0:
                    pe.wait_ge(sem("pt_low"), H * TB)
                for q in range(TB):
                    n = (q + 1) * P
                    product(PS[:, 4 + q, 0:n], QH[r, q * P:n], QL[r, q * P:n], KH[r, 0:n], KL[r, 0:n],
                            stop=False, loose=True)
                    pe.matmul(PS[:, 4 + q, q * P:n], IDB[:, :], MCAUSAL[:, :], start=False, stop=True,
                              skip_group_check=True).then_inc(sem("scores"), 1)

            def weigh(b, h):
                H = 2 * b + h
                pe.wait_ge(sem("prob"), H * TB + TB)
                for j in range(TB):
                    for q in range(j, TB):
                        tr = pe.transpose(PS[:, 4 + j, (q - j) * P:(q - j + 1) * P],
                                          PROB[q][:, j * P:(j + 1) * P], IDF[:, :])
                    tr.then_inc(sem("prob_t"), 1)
                if h == 0:
                    pe.wait_ge(sem("v_low"), b + 1)
                if not isinstance(b, int) or H > 0:
                    pe.wait_ge(sem("o_read"), H * 1)
                for j in range(TB):
                    pe.wait_ge(sem("pt_low"), H * TB + (j + 1))
                    n = (TB - j) * P
                    product(PS[:, 2, j * P:S], VH[:, j, :], VL[:, j, :], PTH[j % 2][:, 0:n], PTL[j % 2][:, 0:n],
                            start=j == 0, stop=j == TB - 1, loose=True).then_inc(sem("weighed"), 1)

            def head_sums(n):
                pe.wait_ge(sem("hn_sq"), n + 1)
                pe.matmul(PS[:, 3, :], ONE64[:, :], W[2][:, 0:S], start=True, stop=True).then_inc(sem("hn_sum"), 1)

            def attention():
                pe.wait_ge(sem("resid"), tiles(1) + KT)
                pe.wait_ge(sem("xld"), tiles(1) + KT)
                unit(ph["forget"], 0, 0, 0, X2H, X2L, ready=(sem("x2_low"), 1, 0))
                row_sums(1)
                pe.wait_ge(sem("fg_c"), 1)
                for t in range(TB):
                    tr = pe.transpose(PS[:, 1, t * P:(t + 1) * P], W[4][:, t * P:(t + 1) * P], IDF[:, :])
                tr.then_inc(sem("fg_t"), 1)
                p = ph["attn"]
                def body(i):
                    first = isinstance(i, int) and i == 0
                    if first:
                        pe.wait_ge(sem("fg_z"), 1)
                    else:
                        pe.wait_ge(sem("kq_read"), i * 2)
                    unit(p, i, 0, 0, X2H, X2L)
                    if not first:
                        scores(i - 1, 0)
                    if first:
                        pe.wait_ge(sem("fg_ct"), 1)
                    else:
                        pe.wait_ge(sem("vg_read"), i * 2)
                    unit(p, i, 1, 1, X2H, X2L)
                    if not first:
                        weigh(i - 1, 0)
                        scores(i - 1, 1)
                        pe.wait_ge(sem("v_low"), i * 1)
                    head_sums(i * 2)
                    pe.wait_ge(sem("kq_read"), i * 2 + 1)
                    unit(p, i, 2, 0, XH, XL)
                    if not first:
                        weigh(i - 1, 1)
                    pe.wait_ge(sem("hn_v"), i * 2 + 1)
                    head_sums(i * 2 + 1)
                    pe.wait_ge(sem("vg_read"), i * 2 + 1)
                    unit(p, i, 3, 1, XH, XL)
                    pe.wait_ge(sem("hn_v"), i * 2 + 2)
                    for t in range(TB):
                        tr = pe.transpose(PS[:, 3, t * P:(t + 1) * P], W[5][:, t * P:(t + 1) * P], IDF[:, :])
                    tr.then_inc(sem("v_t"), 1)
                body(0)
                loop(pe, PAIRS, body, start=1)
                for h in range(2):
                    scores(PAIRS - 1, h)
                    weigh(PAIRS - 1, h)
                residual(ph["attn_out"], 2, 1, OH, OL, (sem("o_low"), 1, 0),
                         [(sem("kq_read"), 2 * PAIRS), (sem("vg_read"), 2 * PAIRS)])

            def gates():
                pe.wait_ge(sem("resid"), tiles(3) + KT)
                unit(ph["lr"], 0, 0, 0, XH, XL, ready=(sem("xld"), 1, tiles(3)))
                row_sums(3)
                pe.wait_ge(sem("up_loaded"), 32)
                pe.wait_ge(sem("lr"), 1)
                for t in range(2 * GH):
                    if t >= 2:
                        pe.wait_ge(sem("z_read"), t - 1)
                    pe.matmul(PS[:, 1 + t % 2, :], UP[:, t * P:(t + 1) * P], W[1][0:2 * GATE_RANK, 0:S],
                              start=True, stop=True).then_inc(sem("z"), 1)

            def gla_inter(i, d):
                n = 2 * i + d
                for s, c in enumerate(chunk_order(d)):
                    to = c + 1 if d == 0 else c - 1
                    t = slice(to * CH, (to + 1) * CH)
                    pe.wait_ge(sem("g_state_low"), n * (NCH - 1) + (s + 1))
                    for u in range(2):
                        v = slice(u * P, (u + 1) * P)
                        mm = product(PS[:, 6 + u, t], SH[:, s, v], SL[:, s, v], QDH[d][:, t], QDL[d][:, t],
                                     start=d == 0 and s == 0, stop=d == 1 and s == NCH - 2, loose=True)
                mm.then_inc(sem("g_inter"), 1)

            def gla_sum(i):
                pe.wait_ge(sem("g_sq"), i * 2 + 2)
                pe.matmul(PS[:, 3, :], ONE[:, :], E[0][:, :], start=True, stop=False)
                pe.matmul(PS[:, 3, :], ONE[:, :], E[1][:, :], start=False, stop=True).then_inc(sem("g_sum"), 1)

            def gla(i):
                p = ph["gla"]
                later = not isinstance(i, int) or i > 0
                if later:
                    pe.wait_ge(sem("g_sc"), i * 1)
                else:
                    pe.wait_ge(sem("z_read"), 2 * GH)
                unit(p, i, 0, 2, XH, XL)
                if later:
                    gla_inter(i - 1, 1)
                unit(p, i, 1, 4, XH, XL)
                if later:
                    gla_sum(i - 1)
                unit(p, i, 2, 0, XH, XL)
                unit(p, i, 3, 1, XH, XL)
                def scores(d):
                    n = 2 * i + d
                    pe.wait_ge(sem("gd_low"), n * 3 + 2)
                    if d == 1:
                        pe.wait_ge(sem("g_sc0"), i + 1)
                    for b in range(TB):
                        c = slice(b * P, (b + 1) * P)
                        mm = product(PS[:, 2, c], KIH[:, c], KIL[:, c], QDH[d][:, c], QDL[d][:, c])
                    mm.then_inc(sem("g_scores"), 1)
                    pe.wait_ge(sem("g_kt"), n + 1)
                    for t in range(TB):
                        tr = pe.transpose(PS[:, 3, t * P:(t + 1) * P], W[8][:, t * P:(t + 1) * P], IDF[:, :])
                    tr.then_inc(sem("g_kt_t"), 1)
                def keys_values(d):
                    n = 2 * i + d
                    pe.wait_ge(sem("gd_low"), n * 3 + 3)
                    for c in chunk_order(d):
                        r, b = slice(c % 2 * CH, c % 2 * CH + CH), c // 2
                        bank, cols = kv_place(c)
                        product(PS[:, bank, cols], KTH[r, b * P:(b + 1) * P], KTL[r, b * P:(b + 1) * P],
                                VGH[r, b, :], VGL[r, b, :]).then_inc(sem("g_kv"), 1)
                scores(0)
                pe.wait_ge(sem("g_read"), i * 6 + 4)
                for t in range(TB):
                    for u in range(2):
                        tr = pe.transpose(PS[:, 4 + t // 2, (t % 2 * 2 + u) * P:(t % 2 * 2 + u + 1) * P],
                                          W[3 + u][:, t * P:(t + 1) * P], IDF[:, :])
                tr.then_inc(sem("gv_t"), 1)
                unit(p, i, 4, 6, XH, XL)
                pe.wait_ge(sem("gv_low"), i * 2 + 2)
                keys_values(0)
                unit(p, i, 5, 7, XH, XL)
                scores(1)
                pe.wait_ge(sem("g_read"), i * 6 + 6)
                gla_inter(i, 0)
                keys_values(1)
                pe.wait_ge(sem("g_sc_low"), i + 1)
                for u in range(2):
                    for b in range(TB):
                        c = slice(b * P, (b + 1) * P)
                        product(PS[:, 6 + u, c], VGH[:, b, u * P:(u + 1) * P], VGL[:, b, u * P:(u + 1) * P],
                                SCH[:, c], SCL[:, c], start=False, stop=False, loose=True)

            def swa(i):
                p = ph["swa"]
                later = not isinstance(i, int) or i > 0
                def head_sum(n):
                    pe.wait_ge(sem("sw_sq"), i * 5 + (n + 1))
                    if n >= 2:
                        pe.wait_ge(sem("sw_v"), i * 5 + (n - 1))
                    pe.matmul(PS[:, 4 + n % 2, :], ONE[:, :], E[n % 2][:, :], start=True, stop=True).then_inc(sem("sw_sum"), 1)
                for j in range(6):
                    if j == 3 and later:
                        pe.wait_ge(sem("sw_out"), i * TB)
                    unit(p, i, j, j % 4, XH, XL)
                    if j > 0:
                        head_sum(j - 1)
                pe.wait_ge(sem("sw_read"), i * 6 + 6)
                for t in range(TB):
                    tr = pe.transpose(PS[:, 6, t * P:(t + 1) * P], W[9][:, t * P:(t + 1) * P], IDF[:, :])
                tr.then_inc(sem("sv_t"), 1)
                pe.wait_ge(sem("sv_low"), i + 1)
                pe.wait_ge(sem("sw_low"), i * 5 + 5)
                def scores(q):
                    win, n = WIN[q], i * 4 * TB + 4 * q
                    if q > 0:
                        pe.wait_ge(sem("sw_exp"), n)
                    for t in range(SWA_Q):
                        c = slice(q * P, (q + 1) * P)
                        k = slice(win[0] * P, (win[-1] + 1) * P)
                        product(PS[:, 4 + t, 0:len(win) * P], SQH[t][:, c], SQL[t][:, c], SKH[:, k], SKL[:, k],
                                stop=False, loose=True)
                        if q > 0:
                            mm = pe.matmul(PS[:, 4 + t, 0:P], IDB[:, :], MUPPER[:, :], start=False,
                                           stop=q == TB - 1, skip_group_check=True)
                        if q < TB - 1:
                            mm = pe.matmul(PS[:, 4 + t, (len(win) - 1) * P:len(win) * P], IDB[:, :], MCAUSAL[:, :],
                                           start=False, stop=True, skip_group_check=True)
                        mm.then_inc(sem("sw_scores"), 1)
                scores(0)
                for q in range(TB):
                    win, n = WIN[q], i * 4 * TB + 4 * q
                    if q < TB - 1:
                        scores(q + 1)
                    pe.wait_ge(sem("sw_prob"), n + 4)
                    for jj in range(len(win)):
                        if q > 0 and jj == 0:
                            pe.wait_ge(sem("sw_plow"), i * SEEN[TB] + SEEN[q])
                        for t in range(SWA_Q):
                            tr = pe.transpose(PS[:, jj, t * P:(t + 1) * P], SPROB[q % 2][t][:, jj * P:(jj + 1) * P], IDF[:, :])
                        tr.then_inc(sem("sw_pt"), 1)
                    if q > 0:
                        pe.wait_ge(sem("sw_out"), i * TB + q)
                    for jj, j in enumerate(win):
                        k = SEEN[q] + jj
                        pe.wait_ge(sem("sw_plow"), i * SEEN[TB] + (k + 1))
                        product(PS[:, 3, :], SVH[:, j, :], SVL[:, j, :], SPH[k % 2][:, :], SPL[k % 2][:, :], start=jj == 0,
                                stop=jj == len(win) - 1).then_inc(sem("sw_pv"), 1)

            def merge(i):
                p = ph["merge"]
                for j, (xh, xl) in enumerate(((XH, XL), (XH, XL), (YGH, YGL), (YSH, YSL))):
                    if isinstance(i, int) and i == 0:
                        if j == 3:
                            pe.wait_ge(sem("sw_out"), SWA_GROUPS * TB)
                    else:
                        pe.wait_ge(sem("mg_read"), i * 4 + (j - 3))
                    unit(p, i, j, j, xh, xl)

            pe.wait_ge(sem("consts"), 16)
            pe.wait_ge(sem("params"), 16 * N_PARAM_DMAS)
            pe.wait_ge(sem("zeroed"), 1)
            pe.transpose(PS[:, 2, 0:P], PROW[:, 0, :], CST[:, C_ID:C_ID + P])
            for l in range(2):
                tr = pe.transpose(PS[:, 2, P * (l + 1):P * (l + 1) + P], PROW[:, 1 + l, :], CST[:, C_ID:C_ID + P])
            tr.then_inc(sem("prm_t"), 1)
            pe.wait_ge(sem("x_loaded"), 16 * TB)
            for m in range(KT):
                if m >= 2:
                    pe.wait_ge(sem("resid"), tiles("_x") + m - 1)
                for t in range(TB):
                    tr = pe.transpose(PS[:, m % 2, t * P:(t + 1) * P], XIN[:, t, m * P:(m + 1) * P], CST[:, C_ID:C_ID + P])
                tr.then_inc(sem("xt"), 1)
            p = ph["mix"]
            pe.wait_ge(sem("resid"), tiles("_x") + KT)
            def mix(i):
                for j in range(3):
                    if not isinstance(i, int) or i > 0:
                        pe.wait_ge(sem(f"mix_{'chb'[j]}"), i * 1)
                    unit(p, i, j, j, XH, XL, ready=(sem("xld"), 1, tiles("_x")) if isinstance(i, int) and i == 0 and j == 0 else None)
                    if isinstance(i, int) and i == 0 and j == 0:
                        row_sums("_x")
            loop(pe, KT, mix)
            residual(ph["mix_out"], 0, 1, BUH, BUL, (sem("mix_low"), 1, 0),
                     [(sem("mix_c"), KT), (sem("mix_h"), KT)])
            if stop > 1:
                ffn(0, 0)
            if stop > 2:
                attention()
            if stop > 3:
                ffn(1, 2)
            if stop > 4:
                gates()
                gla(0)
                loop(pe, GH, gla, start=1)
                gla_inter(GH - 1, 1)
                gla_sum(GH - 1)
                loop(pe, SWA_GROUPS, swa)
                loop(pe, KT, merge)
                residual(ph["out2"], 4, 1, MGH, MGL, (sem("mg_low"), 1, 0),
                         [(sem("mg_read"), 4 * KT), (sem("mg_read"), 4 * KT)])
            if stop > 5:
                ffn(2, 4)
            pe.wait_ge(sem("resid"), tiles(last_resid) + KT)
            for t in range(TB):
                for h in range(2):
                    n = 2 * t + h
                    if n >= 2:
                        pe.wait_ge(sem("out_rows"), n - 1)
                    for m in range(4):
                        tr = pe.transpose(PS[:, 2 + n % 2, m * P:(m + 1) * P],
                                          XT[:, 4 * h + m, t * P:(t + 1) * P], IDF[:, :])
                    tr.then_inc(sem("out_t"), 1)

        @block.scalar
        def _(act):
            steps = Steps(act, sem("act_step"))
            link = steps.link

            def rsqrt(v, r, rr, ready, value, done):
                act.wait_ge(ready, value)
                link(act.activation(r, v, ACT.Ln))
                link(act.activation(r, r, ACT.Exp, scale=-0.5))
                act.activation(rr, r, ACT.Square).then_inc(done, 1)

            def norm(n):
                rsqrt(W[4][:, 0:S], W[5][:, 0:S], W[6][:, 0:S], sem("nv"), ORDER[n] + 1, sem("nrr"))

            def residual(n, iters, tpi, gains):
                def body(i):
                    for t in range(tpi):
                        m = i * tpi + t
                        if gains and (t >= 2 or not isinstance(i, int) or i > 0):
                            act.wait_ge(sem("acc"), tiles(n) + m - 1)
                        act.wait_ge(sem("resid"), tiles(n) + m + 1)
                        if not gains:
                            continue
                        act.wait_ge(sem("prm_ready"), 3)
                        act.activation(W[2 + t % 2][:, 0:S], tile(XT, m), ACT.Square).then_inc(sem("sq"), 1)
                        for xh, _, row in gains:
                            act.activation(tile(xh, m), tile(XT, m), ACT.Copy,
                                           scale=column(PRM, m + row)).then_inc(sem("xhd"), 1)
                if gains:
                    loop(act, iters, body, steps)

            def ffn(l, n, conv, gains):
                norm(n)
                def body(i):
                    for q in range(2):
                        m = 2 * i + q
                        u, g = W[3 + q][:, 0:S], W[5 + q]
                        act.wait_ge(sem("ffn_u" if conv else "ffn_a"), m + (l * FT + 1))
                        act.activation(u, u, ACT.Silu).then_inc(sem("ffn_silu"), 1)
                        act.wait_ge(sem("ffn_h"), m + l * FT + 1)
                        act.wait_ge(sem("prm_ready"), 3)
                        act.copy(tile(HH, m), g[:, 0:S]).then_inc(sem("ffn_high"), 1)
                loop(act, FT // 2, body, steps)
                residual(n + 1, KT // 2, 2, gains)

            def softmax(b, h):
                H = 2 * b + h
                for q in range(TB):
                    act.wait_ge(sem("score_max"), H * TB + (q + 1))
                    pr = PROB[q][:, 0:(q + 1) * P]
                    act.activation(pr, pr, ACT.Exp, bias=NEGM[:, q:q + 1],
                                   accum_out=RS[:, q:q + 1]).then_inc(sem("exp"), 1)
                for q in range(TB):
                    act.wait_ge(sem("rinv"), H * TB + (q + 1))
                    pr = PROB[q][:, 0:(q + 1) * P]
                    act.activation(pr, pr, ACT.Copy, scale=RINV[:, q:q + 1]).then_inc(sem("prob"), 1)

            def high_probs(b, h):
                H = 2 * b + h
                for j in range(TB):
                    act.wait_ge(sem("prob_t"), H * TB + (j + 1))
                    if not isinstance(b, int) or H > 0 or j >= 2:
                        act.wait_ge(sem("weighed"), H * TB + (j - 1))
                    act.copy(PTH[j % 2][:, 0:(TB - j) * P], PS[:, 4 + j, 0:(TB - j) * P]).then_inc(sem("pt_high"), 1)

            def high_out(b):
                act.wait_ge(sem("o_read"), 2 * b + 2)
                act.wait_ge(sem("prm_ready"), 3)
                act.copy(tile(OH, b), W[6][:, 0:S]).then_inc(sem("o_high"), 1)

            def load_cums(b):
                for h in range(2):
                    row = cums[2 * b + h, :] if isinstance(b, int) else \
                        cums[bass.ds(2 * b + h, 1), :].rearrange("a n -> (a n)")
                    act.dma_start(W[8 + h][:, 0:S], row.partition_broadcast(P)).then_inc(sem("cums_loaded"), 16)

            def head_norm(n, to):
                rsqrt(W[3][:, 0:S], W[2][:, 0:S], W[4][:, 0:S], sem("hn_v"), n + 1, sem("hn_rr"))
                act.wait_ge(sem("hn_x"), n + 1)
                act.copy(to[:, :], W[1][:, 0:S]).then_inc(sem("hn_high"), 1)

            def square(n):
                act.wait_ge(sem("kq_read"), n + 1)
                act.activation(W[2][:, 0:S], W[1][:, 0:S], ACT.Square).then_inc(sem("hn_sq"), 1)

            def attention():
                act.wait_ge(sem("resid"), tiles(1) + KT)
                for m in range(KT):
                    act.activation(X2H[:, m, :], XT[:, m, :], ACT.Copy,
                                   scale=PRM[:, R_KV + m:R_KV + m + 1]).then_inc(sem("x2_high"), 1)
                norm(1)
                act.wait_ge(sem("fg_z"), 1)
                link(act.activation(W[2][:, 0:S], W[1][:, 0:S], ACT.Abs))
                link(act.activation(W[2][:, 0:S], W[2][:, 0:S], ACT.Exp, scale=-1.0))
                act.activation(W[2][:, 0:S], W[2][:, 0:S], ACT.Ln, bias=ONEC).then_inc(sem("fg_sp"), 1)
                act.wait_ge(sem("fg_c"), 1)
                act.dma_start(cums[:, :], W[4][P - HEADS:P, 0:S]).then_inc(sem("cums_stored"), 16)
                act.wait_ge(sem("cums_stored"), 16)
                def body(i):
                    first = isinstance(i, int) and i == 0
                    square(i * 2)
                    if not first:
                        softmax(i - 1, 0)
                        high_probs(i - 1, 0)
                        softmax(i - 1, 1)
                    load_cums(i)
                    if not first:
                        act.wait_ge(sem("scores"), i * 2 * TB)
                    head_norm(i * 2, KH)
                    square(i * 2 + 1)
                    if not first:
                        high_probs(i - 1, 1)
                        high_out(i - 1)
                    head_norm(i * 2 + 1, QH)
                    act.wait_ge(sem("vg_read"), i * 2 + 2)
                    act.activation(W[6][:, 0:S], W[6][:, 0:S], ACT.Exp, scale=-1.0).then_inc(sem("g_exp"), 1)
                    act.wait_ge(sem("v_t"), i + 1)
                    act.copy(VH[:, :, :], PS[:, 3, :].rearrange("p (t c) -> p t c", t=TB)).then_inc(sem("v_high"), 1)
                body(0)
                loop(act, PAIRS, body, steps, start=1)
                for h in range(2):
                    softmax(PAIRS - 1, h)
                    high_probs(PAIRS - 1, h)
                high_out(PAIRS - 1)

            def gates():
                act.wait_ge(sem("up_zeroed"), 1)
                for d, name in enumerate(("gla_gate_up_fwd_2", "gla_gate_up_bwd_2")):
                    act.dma_start(UP[d * GATE_RANK:(d + 1) * GATE_RANK, d * GH * GDK:(d + 1) * GH * GDK],
                                  T[name][0]).then_inc(sem("up_loaded"), 16)
                norm(3)
                act.dma_start(W[9][:, 0:2 * P], T["consts"][:, C_GF:C_GF + 2 * P]).then_inc(sem("g_masks"), 16)
                for t in range(2 * GH):
                    z, sp = W[2 + t % 2][:, 0:S], W[4 + t % 2][:, 0:S]
                    act.wait_ge(sem("z_read"), t + 1)
                    link(act.activation(sp, z, ACT.Abs))
                    link(act.activation(sp, sp, ACT.Exp, scale=-1.0))
                    act.activation(sp, sp, ACT.Ln, bias=ONEC).then_inc(sem("z_sp"), 1)

            def gla_square(i):
                act.wait_ge(sem("g_silu"), i + 1)
                act.wait_ge(sem("g_inter"), i * 2 + 2)
                for u in range(2):
                    act.activation(E[u][:, :], PS[:, 6 + u, :], ACT.Square).then_inc(sem("g_sq"), 1)

            def gla_norm(i):
                rsqrt(T0[:, :], T1[:, :], E[0][:, :], sem("g_nv"), i + 1, sem("g_nrr"))
                for u in range(2):
                    act.wait_ge(sem("g_y"), i * 2 + (u + 1))
                    act.wait_ge(sem("prm_ready"), 3)
                    act.copy(tile(YGH, i * 2 + u), W[3 + u][:, 0:S]).then_inc(sem("g_yhigh"), 1)

            def gla(i):
                later = not isinstance(i, int) or i > 0
                def decays(d):
                    act.wait_ge(sem("prm_ready"), 3)
                    act.activation(W[7][:, 0:S], tile(BC, i + GH * d), ACT.Exp).then_inc(sem("g_e"), 1)
                    act.activation(W[8][:, 0:S], tile(BC, i + GH * d), ACT.Exp, scale=-1.0).then_inc(sem("g_e"), 1)
                def high_qk(d):
                    n = 2 * i + d
                    act.wait_ge(sem("g_qk"), n * 2 + 1)
                    act.copy(QDH[d][:, :], W[7][:, 0:S]).then_inc(sem("gd_high"), 1)
                    if d == 1:
                        act.wait_ge(sem("g_scores"), i * 2 + 1)
                    act.wait_ge(sem("g_qk"), n * 2 + 2)
                    act.copy(KIH[:, :], W[8][:, 0:S]).then_inc(sem("gd_high"), 1)
                def high_tail_keys(d):
                    act.wait_ge(sem("g_kt_t"), 2 * i + (d + 1))
                    act.copy(KTH[:, :], PS[:, 3, :]).then_inc(sem("gd_high"), 1)
                def high_states(d):
                    n = 2 * i + d
                    if d == 1 or later:
                        act.wait_ge(sem("g_inter"), n * 1)
                    for s in range(NCH - 1):
                        act.wait_ge(sem("g_st"), n * (NCH - 1) + (s + 1))
                        act.copy(SH[:, s, :], ST[s % 2][:, :]).then_inc(sem("g_state_high"), 1)
                if later:
                    act.wait_ge(sem("g_sc_low"), i * 1)
                else:
                    act.wait_ge(sem("g_cum"), 2 * GH)
                decays(0)
                if later:
                    gla_square(i - 1)
                    gla_norm(i - 1)
                high_qk(0)
                high_tail_keys(0)
                act.wait_ge(sem("gv_t"), i + 1)
                for b in range(2):
                    act.copy(VGH[:, 2 * b:2 * b + 2, :], PS[:, 4 + b, :].rearrange("p (t c) -> p t c", t=2)).then_inc(sem("gv_high"), 1)
                act.wait_ge(sem("gd_low"), i * 6 + 2)
                decays(1)
                high_qk(1)
                high_states(0)
                high_tail_keys(1)
                act.wait_ge(sem("g_sc"), i + 1)
                act.copy(SCH[:, :], W[7][:, 0:S]).then_inc(sem("g_sc_high"), 1)
                for u in range(2):
                    act.wait_ge(sem("g_read"), i * 6 + (5 + u))
                    act.activation(E[u][:, :], W[5 + u][:, 0:S], ACT.Exp, scale=-1.0).then_inc(sem("g_rexp"), 1)
                high_states(1)

            def swa(i):
                if isinstance(i, int) and i == 0:
                    act.wait_ge(sem("g_ylow"), 2 * GH)
                    for k in range(2):
                        act.dma_start(W[7 + k][:, 0:S], T["consts"][:, C_COS + k * S:C_COS + (k + 1) * S]).then_inc(sem("rope"), 16)
                def square(n):
                    act.wait_ge(sem("sw_read"), i * 6 + (n + 1))
                    act.activation(E[n % 2][:, :], W[(1, 9)[n % 2]][:, 0:S], ACT.Square).then_inc(sem("sw_sq"), 1)
                def finish(n, to):
                    rsqrt(W[3][:, 0:S], W[2][:, 0:S], W[4][:, 0:S], sem("sw_v"), i * 5 + (n + 1), sem("sw_rr"))
                    act.wait_ge(sem("sw_x"), i * 5 + (n + 1))
                    act.copy(to[:, :], W[(1, 9)[n % 2]][:, 0:S]).then_inc(sem("sw_high"), 1)
                square(0)
                square(1)
                for n in range(5):
                    finish(n, SKH if n == 0 else SQH[n - 1])
                    if n < 3:
                        square(n + 2)
                act.wait_ge(sem("sv_t"), i + 1)
                act.copy(SVH[:, :, :], PS[:, 6, :].rearrange("p (t c) -> p t c", t=TB)).then_inc(sem("sv_high"), 1)
                later = not isinstance(i, int) or i > 0
                def exps(q):
                    win, n = WIN[q], i * 4 * TB + 4 * q
                    if q >= 2:
                        act.wait_ge(sem("sw_pt"), i * SEEN[TB] + SEEN[q - 1])
                    elif later:
                        act.wait_ge(sem("sw_pt"), i * SEEN[TB])
                    for t in range(SWA_Q):
                        act.wait_ge(sem("sw_max"), n + (t + 1))
                        act.wait_ge(sem("prm_ready"), 3)
                        act.activation(SESK[q % 2][:, t:t + 1], column(SINK, i * SWA_Q + t), ACT.Exp,
                                       bias=SNEG[q % 2][:, t:t + 1]).then_inc(sem("sw_sink"), 1)
                        act.activation(SPROB[q % 2][t][:, 0:len(win) * P], PS[:, 4 + t, 0:len(win) * P], ACT.Exp,
                                       bias=SNEG[q % 2][:, t:t + 1], accum_out=SRS[q % 2][:, t:t + 1]).then_inc(sem("sw_exp"), 1)
                def scale(q):
                    act.wait_ge(sem("sw_rinv"), i * TB + (q + 1))
                    for t in range(SWA_Q):
                        pr = SPROB[q % 2][t][:, 0:len(WIN[q]) * P]
                        act.activation(pr, pr, ACT.Copy, scale=SINV[q % 2][:, t:t + 1]).then_inc(sem("sw_prob"), 1)
                exps(0)
                scale(0)
                for q in range(TB):
                    if q < TB - 1:
                        exps(q + 1)
                    for jj in range(len(WIN[q])):
                        k = SEEN[q] + jj
                        act.wait_ge(sem("sw_pt"), i * SEEN[TB] + (k + 1))
                        if later or k >= 2:
                            act.wait_ge(sem("sw_pv"), i * SEEN[TB] + (k - 1))
                        act.copy(SPH[k % 2][:, :], PS[:, jj, :]).then_inc(sem("sw_phigh"), 1)
                    if q < TB - 1:
                        scale(q + 1)
                    act.wait_ge(sem("sw_pv"), i * SEEN[TB] + SEEN[q + 1])
                    act.wait_ge(sem("prm_ready"), 3)
                    act.copy(window_out(YSH, i, q), PS[:, 3, :].rearrange("p (t c) -> p t c", t=SWA_Q)).then_inc(sem("sw_ohigh"), 1)

            def merge(i):
                for k in range(2):
                    act.wait_ge(sem("mg_read"), i * 4 + (k + 1))
                    act.activation(W[1 + k][:, 0:S], W[1 + k][:, 0:S], ACT.Sigmoid).then_inc(sem("mg_sig"), 1)
                act.wait_ge(sem("mg"), i + 1)
                act.wait_ge(sem("prm_ready"), 3)
                act.copy(tile(MGH, i), W[3][:, 0:S]).then_inc(sem("mg_high"), 1)

            act.dma_start(CST[:, :], T["consts"][:, 0:C_GF]).then_inc(sem("consts"), 16)
            act.wait_ge(sem("zeroed"), 1)
            for to, src in PARAM_DMAS(PROW, T):
                act.dma_start(to, src).then_inc(sem("params"), 16)
            if stop > 4:
              act.dma_start(SINK[:, :], T["swa_sinks_2"][0].partition_broadcast(P)).then_inc(sem("sinks"), 16)
            residual("_x", 1, KT, [(XH, XL, R_ATTN)])
            norm("_x")
            def mix(i):
                act.wait_ge(sem("mix_bu"), i + 1)
                act.wait_ge(sem("prm_ready"), 3)
                act.copy(tile(BUH, i), W[4][:, 0:S]).then_inc(sem("mix_high"), 1)
            loop(act, KT, mix, steps)
            residual(0, 2, 4, [(XH, XL, R_FFN)] if stop > 1 else [])
            if stop > 1:
                ffn(0, 0, True, [(XH, XL, R_ATTN + KT)] if stop > 2 else [])
            if stop > 2:
                attention()
                residual(2, 2, 4, [(XH, XL, R_FFN + KT)] if stop > 3 else [])
            if stop > 3:
                ffn(1, 2, True, [(XH, XL, R_MIX)] if stop > 4 else [])
            if stop > 4:
                gates()
                gla(0)
                loop(act, GH, gla, steps, start=1)
                gla_square(GH - 1)
                gla_norm(GH - 1)
                loop(act, SWA_GROUPS, swa, steps)
                loop(act, KT, merge, steps)
                residual(4, 2, 4, [(XH, XL, R_FFN2)] if stop > 5 else [])
            if stop > 5:
                ffn(2, 4, False, [])

        @block.vector
        def _(dve):
            steps = Steps(dve, sem("dve_step"))
            link = steps.link

            def newton(v, r, rr, ready, value, out_, signal=None):
                dve.wait_ge(ready, value)
                link(dve.tensor_tensor(v, v, rr, ALU.mult))
                link(dve.tensor_scalar(v, v, -0.5, 1.5, ALU.mult, ALU.add))
                ins = dve.tensor_tensor(out_, r, v, ALU.mult)
                if signal is None:
                    link(ins)
                else:
                    ins.then_inc(signal, 1)

            def norm(n):
                dve.wait_ge(sem("nsum"), ORDER[n] + 1)
                dve.tensor_scalar(W[4][:, 0:S], PS[:, 7, :], 1.0 / D, EPS, ALU.mult, ALU.add).then_inc(sem("nv"), 1)
                newton(W[4][:, 0:S], W[5][:, 0:S], W[6][:, 0:S], sem("nrr"), ORDER[n] + 1, W[0][:, 0:S])

            def residual(n, iters, tpi, gains, take):
                def body(i):
                    for t in range(tpi):
                        m = i * tpi + t
                        take(i, t, m).then_inc(sem("resid"), 1)
                        if not gains:
                            continue
                        dve.wait_ge(sem("sq"), tiles(n) + m + 1)
                        sq, acc = W[2 + t % 2][:, 0:S], W[1][:, 0:S]
                        if isinstance(m, int) and m == 0:
                            dve.tensor_copy(acc, sq).then_inc(sem("acc"), 1)
                        else:
                            dve.wait_ge(sem("acc"), tiles(n) + m)
                            dve.tensor_tensor(acc, acc, sq, ALU.add).then_inc(sem("acc"), 1)
                        for g, (xh, xl, row) in enumerate(gains):
                            dve.wait_ge(sem("xhd"), tiles(n) + m + 1)
                            dve.scalar_tensor_tensor(tile(xl, m), tile(XT, m), column(PRM, m + row),
                                                     tile(xh, m).bitcast(F32), ALU.mult,
                                                     ALU.subtract).then_inc(sem("xld"), 1)
                loop(dve, iters, body, steps)

            def add_products(p, groups):
                def take(i, t, m):
                    dve.wait_ge(unit_done, p.unit(i, t * groups + groups - 1) + 1)
                    return dve.tensor_tensor(tile(XT, m), PS[:, t % 2, :], tile(XT, m), ALU.add)
                return take

            def conv(x, o, w):
                link(dve.tensor_scalar(o, x[:, 0:S], w[0], None, ALU.mult))
                link(dve.scalar_tensor_tensor(o, x[:, 1:S + 1], w[1], o, ALU.mult, ALU.add))
                return dve.scalar_tensor_tensor(o, x[:, 2:S + 2], w[2], o, ALU.mult, ALU.add)

            def ffn(l, n, with_conv, gains):
                pu, pd = ph[f"up{l}"], ph[f"down{l}"]
                norm(n)
                for q in range(2):
                    dve.memset(W[1 + q][:, 0:2], 0.0)
                link(dve.memset(W[7][:, 0:2], 0.0))
                def body(i):
                    for q in range(2):
                        m = 2 * i + q
                        a, u, g = W[1 + q], W[3 + q][:, 0:S], W[5 + q][:, 0:S]
                        dve.wait_ge(unit_done, pu.unit(i, 2 * q) + 1)
                        dve.tensor_tensor(a[:, 2:S + 2] if with_conv else u, PS[:, 2 * q, :], W[0][:, 0:S],
                                          ALU.mult).then_inc(sem("ffn_a"), 1)
                        if with_conv:
                            dve.wait_ge(sem("ffn_a"), m + l * FT + 1)
                            conv(a, u, [column(FC, m + (l * 3 + k) * FT) for k in range(3)]).then_inc(sem("ffn_u"), 1)
                        dve.wait_ge(unit_done, pu.unit(i, 2 * q + 1) + 1)
                        dve.tensor_tensor(g, PS[:, 2 * q + 1, :], W[0][:, 0:S], ALU.mult).then_inc(sem("ffn_g"), 1)
                        dve.wait_ge(sem("ffn_g"), m + l * FT + 1)
                        dve.wait_ge(sem("ffn_silu"), m + l * FT + 1)
                        dve.tensor_tensor(g, g, u, ALU.mult).then_inc(sem("ffn_h"), 1)
                        dve.wait_ge(sem("ffn_high"), m + l * FT + 1)
                        dve.tensor_tensor(tile(HL, m), g, tile(HH, m).bitcast(F32), ALU.subtract).then_inc(sem("ffn_low"), 1)
                loop(dve, FT // 2, body, steps)
                residual(n + 1, KT // 2, 2, gains, add_products(pd, 3))

            def softmax(b, h):
                H = 2 * b + h
                if h == 0:
                    dve.wait_ge(sem("cums_loaded"), 32 * b + 32)
                if not isinstance(b, int) or H > 0:
                    dve.wait_ge(sem("prob_t"), H * TB)
                for q in range(TB):
                    n = (q + 1) * P
                    pr = PROB[q][:, 0:n]
                    dve.wait_ge(sem("scores"), H * TB + (q + 1))
                    ci = CT[:, q, H:H + 1] if isinstance(b, int) else CT[:, q, bass.ds(H, 1)]
                    dve.scalar_tensor_tensor(pr, PS[:, 4 + q, 0:n], ci, W[8 + h][:, 0:n], ALU.add,
                                             ALU.subtract).then_inc(sem("scores_read"), 1)
                    dve.wait_ge(sem("scores_read"), H * TB + (q + 1))
                    dve.tensor_reduce(NEGM[:, q:q + 1], pr, AX.X, ALU.max, negate=True).then_inc(sem("score_max"), 1)
                for q in range(TB):
                    dve.wait_ge(sem("exp"), H * TB + (q + 1))
                    dve.reciprocal(RINV[:, q:q + 1], RS[:, q:q + 1]).then_inc(sem("rinv"), 1)

            def low_probs(b, h):
                H = 2 * b + h
                for j in range(TB):
                    n = (TB - j) * P
                    dve.wait_ge(sem("pt_high"), H * TB + (j + 1))
                    dve.tensor_tensor(PTL[j % 2][:, 0:n], PS[:, 4 + j, 0:n], PTH[j % 2][:, 0:n].bitcast(F32),
                                      ALU.subtract).then_inc(sem("pt_low"), 1)
                r = slice(HD * h, HD * h + HD)
                dve.wait_ge(sem("weighed"), H * TB + TB)
                dve.tensor_tensor(W[6][r, 0:S], PS[r, 2, :], W[6][r, 0:S], ALU.mult).then_inc(sem("o_read"), 1)

            def low_out(b):
                dve.wait_ge(sem("o_high"), b + 1)
                dve.tensor_tensor(tile(OL, b), W[6][:, 0:S], tile(OH, b).bitcast(F32), ALU.subtract).then_inc(sem("o_low"), 1)

            def head_norm(n, gain, high, low):
                dve.wait_ge(sem("hn_sum"), n + 1)
                dve.tensor_scalar(W[3][:, 0:S], PS[:, 3, :], 1.0 / HD, EPS, ALU.mult, ALU.add).then_inc(sem("hn_v"), 1)
                newton(W[3][:, 0:S], W[2][:, 0:S], W[4][:, 0:S], sem("hn_rr"), n + 1, W[4][:, 0:S])
                dve.scalar_tensor_tensor(W[1][:, 0:S], W[1][:, 0:S], PRM[:, gain:gain + 1], W[4][:, 0:S],
                                         ALU.mult, ALU.mult).then_inc(sem("hn_x"), 1)
                dve.wait_ge(sem("hn_high"), n + 1)
                dve.tensor_tensor(low[:, :], W[1][:, 0:S], high[:, :].bitcast(F32), ALU.subtract).then_inc(sem("hn_low"), 1)

            def attention():
                for m in range(KT):
                    dve.wait_ge(sem("x2_high"), m + 1)
                    dve.scalar_tensor_tensor(X2L[:, m, :], XT[:, m, :], PRM[:, R_KV + m:R_KV + m + 1],
                                             X2H[:, m, :].bitcast(F32), ALU.mult, ALU.subtract).then_inc(sem("x2_low"), 1)
                norm(1)
                dve.wait_ge(unit_done, ph["forget"].unit(0, 0) + 1)
                link(dve.tensor_tensor(W[1][:, 0:S], PS[:, 0, :], W[0][:, 0:S], ALU.mult))
                dve.tensor_scalar(W[1][:, 0:S], W[1][:, 0:S], PRM[:, R_BF:R_BF + 1], None, ALU.add).then_inc(sem("fg_z"), 1)
                link(dve.memset(W[5][:, 0:S], 1.0))
                dve.wait_ge(sem("fg_sp"), 1)
                link(dve.scalar_tensor_tensor(W[3][:, 0:S], W[1][:, 0:S], 0.0, W[2][:, 0:S], ALU.min, ALU.subtract))
                dve.tensor_tensor_scan(W[4][:, 0:S], W[5][:, 0:S], W[3][:, 0:S], 0.0, ALU.mult, ALU.add).then_inc(sem("fg_c"), 1)
                dve.wait_ge(sem("fg_t"), 1)
                dve.tensor_copy(CT[:, :, :], PS[:, 1, :].rearrange("p (t c) -> p t c", t=TB)[:, :, P - HEADS:P]).then_inc(sem("fg_ct"), 1)
                dve.wait_ge(sem("fg_ct"), 1)
                p = ph["attn"]
                def read(i, j, w, name, n):
                    dve.wait_ge(unit_done, p.unit(i, j) + 1)
                    if j == 2 or (j == 0 and not (isinstance(i, int) and i == 0)):
                        dve.wait_ge(sem("hn_low"), i * 2 + j // 2)
                    if j == 3 and not (isinstance(i, int) and i == 0):
                        dve.wait_ge(sem("o_low"), i * 1)
                    dve.tensor_tensor(W[w][:, 0:S], PS[:, j % 2, :], W[0][:, 0:S], ALU.mult).then_inc(sem(name), 1)
                def body(i):
                    first = isinstance(i, int) and i == 0
                    if first:
                        dve.wait_ge(sem("cums_stored"), 16)
                    read(i, 0, 1, "kq_read", i * 2)
                    if not first:
                        softmax(i - 1, 0)
                    read(i, 1, 5, "vg_read", i * 2)
                    if not first:
                        low_probs(i - 1, 0)
                        softmax(i - 1, 1)
                    head_norm(i * 2, R_KN, KH, KL)
                    read(i, 2, 1, "kq_read", i * 2 + 1)
                    if not first:
                        low_probs(i - 1, 1)
                        low_out(i - 1)
                    head_norm(i * 2 + 1, R_QN, QH, QL)
                    read(i, 3, 6, "vg_read", i * 2 + 1)
                    dve.wait_ge(sem("g_exp"), i + 1)
                    link(dve.tensor_scalar(W[6][:, 0:S], W[6][:, 0:S], 1.0, None, ALU.add))
                    link(dve.reciprocal(W[6][:, 0:S], W[6][:, 0:S]))
                    dve.wait_ge(sem("v_high"), i + 1)
                    dve.tensor_tensor(VL[:, :, :], PS[:, 3, :].rearrange("p (t c) -> p t c", t=TB),
                                      VH[:, :, :].bitcast(F32), ALU.subtract).then_inc(sem("v_low"), 1)
                body(0)
                loop(dve, PAIRS, body, steps, start=1)
                for h in range(2):
                    softmax(PAIRS - 1, h)
                    low_probs(PAIRS - 1, h)
                low_out(PAIRS - 1)

            def gates():
                dve.memset(UP[:, :], 0.0).then_inc(sem("up_zeroed"), 1)
                norm(3)
                dve.wait_ge(unit_done, ph["lr"].unit(0, 0) + 1)
                r = slice(0, 2 * GATE_RANK)
                dve.tensor_tensor(W[1][r, 0:S], PS[r, 0, :], W[0][r, 0:S], ALU.mult).then_inc(sem("lr"), 1)
                link(dve.memset(W[7][:, 0:S], 1.0))
                link(dve.memset(W[7][:, 0:S:CH], 0.0))
                def cumulate(t):
                    z, sp, lg = W[2 + t % 2][:, 0:S], W[4 + t % 2][:, 0:S], W[6][:, 0:S]
                    dve.wait_ge(sem("z_sp"), t + 1)
                    link(dve.scalar_tensor_tensor(lg, z, 0.0, sp, ALU.min, ALU.subtract))
                    link(dve.tensor_scalar(lg, lg, 1.0 / 16.0, -0.5, ALU.mult, ALU.max))
                    o = BC[:, t, :]
                    if t >= GH:
                        lg, o = lg[:, ::-1], o[:, ::-1]
                    dve.tensor_tensor_scan(o, W[7][:, 0:S], lg, 0.0, ALU.mult, ALU.add).then_inc(sem("g_cum"), 1)
                    dve.wait_ge(sem("g_cum"), t + 1)
                for t in range(2 * GH):
                    dve.wait_ge(sem("z"), t + 1)
                    dve.tensor_scalar(W[2 + t % 2][:, 0:S], PS[:, 1 + t % 2, :], PRM[:, R_GBF + t:R_GBF + t + 1], None,
                                      ALU.add).then_inc(sem("z_read"), 1)
                    if t > 0:
                        cumulate(t - 1)
                cumulate(2 * GH - 1)
                dve.wait_ge(sem("g_masks"), 16)

            def gla_norm(i):
                dve.wait_ge(sem("g_sum"), i + 1)
                dve.tensor_scalar(T0[:, :], PS[:, 3, :], 1.0 / (2 * P), EPS, ALU.mult, ALU.add).then_inc(sem("g_nv"), 1)
                newton(T0[:, :], T1[:, :], E[0][:, :], sem("g_nrr"), i + 1, E[0][:, :])
                for u in range(2):
                    o = W[3 + u][:, 0:S]
                    link(dve.scalar_tensor_tensor(o, PS[:, 6 + u, :], PRM[:, R_OUTG + u:R_OUTG + u + 1], E[0][:, :],
                                                  ALU.mult, ALU.mult))
                    dve.tensor_tensor(o, o, W[5 + u][:, 0:S], ALU.mult).then_inc(sem("g_y"), 1)
                for u in range(2):
                    dve.wait_ge(sem("g_yhigh"), i * 2 + (u + 1))
                    dve.tensor_tensor(tile(YGL, i * 2 + u), W[3 + u][:, 0:S], tile(YGH, i * 2 + u).bitcast(F32),
                                      ALU.subtract).then_inc(sem("g_ylow"), 1)

            def gla(i):
                p = ph["gla"]
                later = not isinstance(i, int) or i > 0
                w7, w8 = W[7][:, 0:S], W[8][:, 0:S]
                def read(j):
                    dve.wait_ge(unit_done, p.unit(i, j) + 1)
                    bank = PS[:, (2, 4, 0, 1, 6, 7)[j], :]
                    if j == 0:
                        ins = dve.scalar_tensor_tensor(W[1][:, 0:S], bank, GDK ** -0.5, W[0][:, 0:S], ALU.mult, ALU.mult)
                    else:
                        ins = dve.tensor_tensor(W[1 + j][:, 0:S], bank, W[0][:, 0:S], ALU.mult)
                    ins.then_inc(sem("g_read"), 1)
                def decay(d):
                    n = 2 * i + d
                    dve.wait_ge(sem("g_e"), n * 2 + 2)
                    link(dve.tensor_copy(EBL[d], W[7][:, CH - 1:S:CH] if d == 0 else W[7][:, 0:S:CH]))
                    dve.wait_ge(sem("g_read"), i * 6 + 2)
                    dve.tensor_tensor(w7, W[1][:, 0:S], w7, ALU.mult).then_inc(sem("g_qk"), 1)
                    dve.tensor_tensor(w8, W[2][:, 0:S], w8, ALU.mult).then_inc(sem("g_qk"), 1)
                    dve.wait_ge(sem("gd_high"), n * 3 + 1)
                    dve.tensor_tensor(QDL[d][:, :], w7, QDH[d][:, :].bitcast(F32), ALU.subtract).then_inc(sem("gd_low"), 1)
                    dve.wait_ge(sem("gd_high"), n * 3 + 2)
                    dve.tensor_tensor(KIL[:, :], w8, KIH[:, :].bitcast(F32), ALU.subtract).then_inc(sem("gd_low"), 1)
                    dve.wait_ge(sem("gd_low"), n * 3 + 2)
                    dve.tensor_tensor(w8.rearrange("p (n c) -> p n c", n=NCH), w8.rearrange("p (n c) -> p n c", n=NCH),
                                      EBL[d].unsqueeze(2).to_broadcast([P, NCH, CH]), ALU.mult).then_inc(sem("g_kt"), 1)
                def masked_scores(d, to):
                    dve.wait_ge(sem("g_scores"), i * 2 + (d + 1))
                    return dve.tensor_tensor(to.rearrange("p (t c) -> p t c", t=TB),
                                             PS[:, 2, :].rearrange("p (t c) -> p t c", t=TB),
                                             GMASK[d].unsqueeze(1).to_broadcast([P, TB, P]), ALU.mult)
                def low_tail_keys(d):
                    dve.wait_ge(sem("gd_high"), (2 * i + d) * 3 + 3)
                    dve.tensor_tensor(KTL[:, :], PS[:, 3, :], KTH[:, :].bitcast(F32), ALU.subtract).then_inc(sem("gd_low"), 1)
                def states(d):
                    n = 2 * i + d
                    def low_state(s):
                        dve.wait_ge(sem("g_state_high"), n * (NCH - 1) + (s + 1))
                        dve.tensor_tensor(SL[:, s, :], ST[s % 2][:, :], SH[:, s, :].bitcast(F32),
                                          ALU.subtract).then_inc(sem("g_state_low"), 1)
                    for s, c in enumerate(chunk_order(d)):
                        bank, cols = kv_place(c)
                        dve.wait_ge(sem("g_kv"), n * (NCH - 1) + (4 if s < 4 else NCH - 1))
                        if s >= 2:
                            dve.wait_ge(sem("g_state_low"), n * (NCH - 1) + (s - 1))
                        elif d == 1 or later:
                            dve.wait_ge(sem("g_state_low"), n * (NCH - 1))
                        if s == 0:
                            ins = dve.tensor_copy(ST[0][:, :], PS[:, bank, cols])
                        else:
                            dve.wait_ge(sem("g_st"), n * (NCH - 1) + s)
                            ins = dve.scalar_tensor_tensor(ST[s % 2][:, :], ST[(s + 1) % 2][:, :], EBL[d][:, c:c + 1],
                                                           PS[:, bank, cols], ALU.mult, ALU.add)
                        ins.then_inc(sem("g_st"), 1)
                        if s > 0:
                            low_state(s - 1)
                    low_state(NCH - 2)
                if later:
                    gla_norm(i - 1)
                    dve.wait_ge(sem("g_ylow"), i * 2)
                read(0)
                read(1)
                decay(0)
                read(2)
                read(3)
                masked_scores(0, SC0[:, :]).then_inc(sem("g_sc0"), 1)
                low_tail_keys(0)
                for b in range(2):
                    dve.wait_ge(sem("gv_high"), i * 2 + (b + 1))
                    dve.tensor_tensor(VGL[:, 2 * b:2 * b + 2, :], PS[:, 4 + b, :].rearrange("p (t c) -> p t c", t=2),
                                      VGH[:, 2 * b:2 * b + 2, :].bitcast(F32), ALU.subtract).then_inc(sem("gv_low"), 1)
                read(4)
                decay(1)
                states(0)
                read(5)
                link(masked_scores(1, w7))
                dve.wait_ge(sem("g_sc0"), i + 1)
                dve.tensor_tensor(w7, w7, SC0[:, :], ALU.add).then_inc(sem("g_sc"), 1)
                low_tail_keys(1)
                dve.wait_ge(sem("g_sc_high"), i + 1)
                dve.tensor_tensor(SCL[:, :], w7, SCH[:, :].bitcast(F32), ALU.subtract).then_inc(sem("g_sc_low"), 1)
                states(1)
                for u in range(2):
                    r, e = W[5 + u][:, 0:S], E[u][:, :]
                    dve.wait_ge(sem("g_rexp"), i * 2 + (u + 1))
                    link(dve.tensor_scalar(e, e, 1.0, None, ALU.add))
                    link(dve.reciprocal(e, e))
                    ins = dve.tensor_tensor(r, r, e, ALU.mult)
                    if u == 0:
                        link(ins)
                    else:
                        ins.then_inc(sem("g_silu"), 1)

            def swa(i):
                p = ph["swa"]
                if isinstance(i, int) and i == 0:
                    dve.wait_ge(sem("rope"), 32)
                    dve.wait_ge(sem("sinks"), 16)
                later = not isinstance(i, int) or i > 0
                w = [W[k][:, 0:S] for k in range(10)]
                def read(j):
                    dve.wait_ge(unit_done, p.unit(i, j) + 1)
                    if j >= 2:
                        dve.wait_ge(sem("sw_low"), i * 5 + (j - 1))
                    dve.tensor_tensor(w[(1, 9)[j % 2]], PS[:, j % 4, :], w[0], ALU.mult).then_inc(sem("sw_read"), 1)
                def finish(n, gain, high, low):
                    x = w[(1, 9)[n % 2]]
                    dve.wait_ge(sem("sw_sum"), i * 5 + (n + 1))
                    dve.tensor_scalar(w[3], PS[:, 4 + n % 2, :], 1.0 / P, EPS, ALU.mult, ALU.add).then_inc(sem("sw_v"), 1)
                    newton(w[3], w[2], w[4], sem("sw_rr"), i * 5 + (n + 1), w[4])
                    link(dve.scalar_tensor_tensor(w[5], x, PRM[:, gain:gain + 1], w[4], ALU.mult, ALU.mult))
                    dve.tensor_tensor(W[6][64:128, 0:S], W[5][0:64, 0:S], W[8][0:64, 0:S], ALU.mult)
                    link(dve.tensor_tensor(W[6][0:64, 0:S], W[5][64:128, 0:S], W[8][64:128, 0:S], ALU.mult))
                    link(dve.tensor_tensor(w[5], w[5], w[7], ALU.mult))
                    dve.tensor_tensor(x, w[5], w[6], ALU.add).then_inc(sem("sw_x"), 1)
                    dve.wait_ge(sem("sw_high"), i * 5 + (n + 1))
                    dve.tensor_tensor(low[:, :], x, high[:, :].bitcast(F32), ALU.subtract).then_inc(sem("sw_low"), 1)
                read(0)
                read(1)
                for n in range(5):
                    finish(n, R_SQG if n else R_SKG, SQH[n - 1] if n else SKH, SQL[n - 1] if n else SKL)
                    if n < 4:
                        read(n + 2)
                dve.wait_ge(sem("sv_high"), i + 1)
                dve.tensor_tensor(SVL[:, :, :], PS[:, 6, :].rearrange("p (t c) -> p t c", t=TB),
                                  SVH[:, :, :].bitcast(F32), ALU.subtract).then_inc(sem("sv_low"), 1)
                def softmax(q):
                    win, n = WIN[q], i * 4 * TB + 4 * q
                    for t in range(SWA_Q):
                        dve.wait_ge(sem("sw_scores"), n + (t + 1))
                        link(dve.tensor_reduce(SMAX[:, t:t + 1], PS[:, 4 + t, 0:len(win) * P], AX.X, ALU.max))
                        dve.tensor_scalar(SNEG[q % 2][:, t:t + 1], SMAX[:, t:t + 1], column(SINK, i * SWA_Q + t), -1.0,
                                          ALU.max, ALU.mult).then_inc(sem("sw_max"), 1)
                    dve.wait_ge(sem("sw_exp"), n + 4)
                    link(dve.tensor_tensor(SINV[q % 2][:, :], SRS[q % 2][:, :], SESK[q % 2][:, :], ALU.add))
                    dve.reciprocal(SINV[q % 2][:, :], SINV[q % 2][:, :]).then_inc(sem("sw_rinv"), 1)
                softmax(0)
                for q in range(TB):
                    if q < TB - 1:
                        softmax(q + 1)
                    for jj in range(len(WIN[q])):
                        k = SEEN[q] + jj
                        dve.wait_ge(sem("sw_phigh"), i * SEEN[TB] + (k + 1))
                        dve.tensor_tensor(SPL[k % 2][:, :], PS[:, jj, :], SPH[k % 2][:, :].bitcast(F32),
                                          ALU.subtract).then_inc(sem("sw_plow"), 1)
                    dve.wait_ge(sem("sw_ohigh"), i * TB + (q + 1))
                    dve.tensor_tensor(window_out(YSL, i, q), PS[:, 3, :].rearrange("p (t c) -> p t c", t=SWA_Q),
                                      window_out(YSH, i, q).bitcast(F32), ALU.subtract).then_inc(sem("sw_out"), 1)

            def merge(i):
                p = ph["merge"]
                for k in range(2):
                    dve.wait_ge(unit_done, p.unit(i, k) + 1)
                    dve.tensor_tensor(W[1 + k][:, 0:S], PS[:, k, :], W[0][:, 0:S], ALU.mult).then_inc(sem("mg_read"), 1)
                for k in range(2):
                    dve.wait_ge(unit_done, p.unit(i, 2 + k) + 1)
                    dve.wait_ge(sem("mg_sig"), i * 2 + (k + 1))
                    dve.tensor_tensor(W[3 + k][:, 0:S], PS[:, 2 + k, :], W[1 + k][:, 0:S], ALU.mult).then_inc(sem("mg_read"), 1)
                dve.wait_ge(sem("mg_read"), i * 4 + 4)
                dve.tensor_tensor(W[3][:, 0:S], W[3][:, 0:S], W[4][:, 0:S], ALU.add).then_inc(sem("mg"), 1)
                dve.wait_ge(sem("mg_high"), i + 1)
                dve.tensor_tensor(tile(MGL, i), W[3][:, 0:S], tile(MGH, i).bitcast(F32), ALU.subtract).then_inc(sem("mg_low"), 1)

            link(dve.memset(PROW[:, :, :], 0.0))
            dve.memset(EPSC, EPS)
            dve.memset(ONEC, 1.0).then_inc(sem("zeroed"), 1)
            dve.wait_ge(sem("consts"), 16)
            for to, c in ((IDF, C_ID), (ONE, C_ONE), (ONE64, C_ONE64), (IDB, C_ID), (MCAUSAL, C_CAUSAL), (MUPPER, C_UPPER)):
                ins = dve.tensor_copy(to[:, :], CST[:, c:c + P])
            ins.then_inc(sem("prm_ready"), 1)
            dve.wait_ge(sem("prm_t"), 1)
            dve.tensor_copy(PRM[:, :], PS[:, 2, 0:N_PRM])
            link(dve.tensor_copy(FC[:, 0:N_FC], PS[:, 2, P:P + N_FC]))
            dve.tensor_copy(FC[:, N_FC:2 * N_FC], PS[:, 2, 2 * P:2 * P + N_FC]).then_inc(sem("prm_ready"), 1)
            dve.tensor_scalar(PRM[:, R_QN:R_QN + 1], PRM[:, R_QN:R_QN + 1], HD ** -0.5, None, ALU.mult)
            dve.tensor_scalar(PRM[:, R_SQG:R_SQG + 1], PRM[:, R_SQG:R_SQG + 1], 128 ** -0.5, None,
                              ALU.mult).then_inc(sem("prm_ready"), 1)
            dve.wait_ge(sem("prm_ready"), 3)

            def take_x(i, t, m):
                dve.wait_ge(sem("xt"), m + 1)
                return dve.tensor_copy(XT[:, m, :], PS[:, m % 2, :])
            residual("_x", 1, KT, [(XH, XL, R_ATTN)], take_x)
            norm("_x")
            link(dve.memset(W[1][:, 0:2], 0.0))
            p = ph["mix"]
            def mix(i):
                dve.wait_ge(unit_done, p.unit(i, 0) + 1)
                dve.tensor_tensor(W[5][:, 0:S], PS[:, 0, :], W[0][:, 0:S], ALU.mult).then_inc(sem("mix_c"), 1)
                dve.wait_ge(unit_done, p.unit(i, 1) + 1)
                dve.tensor_tensor(W[6][:, 0:S], PS[:, 1, :], W[0][:, 0:S], ALU.mult).then_inc(sem("mix_h"), 1)
                dve.wait_ge(sem("mix_h"), i + 1)
                link(dve.tensor_tensor(W[1][:, 2:S + 2], W[5][:, 0:S], W[6][:, 0:S], ALU.mult))
                link(conv(W[1], W[3][:, 0:S], [column(PRM, i + R_ACONV + k * KT) for k in range(3)]))
                dve.wait_ge(unit_done, p.unit(i, 2) + 1)
                dve.tensor_tensor(W[5][:, 0:S], PS[:, 2, :], W[0][:, 0:S], ALU.mult).then_inc(sem("mix_b"), 1)
                dve.wait_ge(sem("mix_b"), i + 1)
                dve.tensor_tensor(W[4][:, 0:S], W[5][:, 0:S], W[3][:, 0:S], ALU.mult).then_inc(sem("mix_bu"), 1)
                dve.wait_ge(sem("mix_high"), i + 1)
                dve.tensor_tensor(tile(BUL, i), W[4][:, 0:S], tile(BUH, i).bitcast(F32), ALU.subtract).then_inc(sem("mix_low"), 1)
            loop(dve, KT, mix, steps)
            residual(0, 2, 4, [(XH, XL, R_FFN)] if stop > 1 else [], add_products(ph["mix_out"], 1))
            if stop > 1:
                ffn(0, 0, True, [(XH, XL, R_ATTN + KT)] if stop > 2 else [])
            if stop > 2:
                attention()
                residual(2, 2, 4, [(XH, XL, R_FFN + KT)] if stop > 3 else [], add_products(ph["attn_out"], 1))
            if stop > 3:
                ffn(1, 2, True, [(XH, XL, R_MIX)] if stop > 4 else [])
            if stop > 4:
                gates()
                gla(0)
                loop(dve, GH, gla, steps, start=1)
                gla_norm(GH - 1)
                loop(dve, SWA_GROUPS, swa, steps)
                loop(dve, KT, merge, steps)
                residual(4, 2, 4, [(XH, XL, R_FFN2)] if stop > 5 else [], add_products(ph["out2"], 1))
            if stop > 5:
                ffn(2, 4, False, [])
            for t in range(TB):
                for h in range(2):
                    n = 2 * t + h
                    dve.wait_ge(sem("out_t"), n + 1)
                    dve.tensor_copy(XIN[:, t, h * S:(h + 1) * S], PS[:, 2 + n % 2, :]).then_inc(sem("out_rows"), 1)


def PARAM_DMAS(PROW, T):
    def tall(a):
        return a.rearrange("(k p) -> k p", p=P)
    d = []
    for row, a in ((R_ATTN, T["attn_norm"][0]), (R_ATTN + KT, T["attn_norm"][1]), (R_FFN, T["ffn_norm"][0]),
                   (R_FFN + KT, T["ffn_norm"][1]), (R_KV, T["kv_norm"]), (R_MIX, T["norm_mix_g_2"][0]),
                   (R_FFN2, T["norm_ffn_g_2"][0]), (R_ACONV, T["a_conv"][0, 0]), (R_ACONV + KT, T["a_conv"][0, 1]),
                   (R_ACONV + 2 * KT, T["a_conv"][0, 2]), (R_GBF, T["gla_gate_bias_fwd_2"][0]),
                   (R_GBB, T["gla_gate_bias_bwd_2"][0]), (R_OUTG, T["gla_out_norm_g_2"][0]),
                   (R_SQG, T["swa_q_norm_g_2"][0]), (R_SKG, T["swa_k_norm_g_2"][0])):
        n = a.shape[0] // P
        d.append((PROW[row:row + n, 0, :], tall(a)))
    for row, a in ((R_QN, T["q_norm"][0]), (R_KN, T["k_norm"])):
        for h in range(2):
            d.append((PROW[row:row + 1, 0, h * HD:(h + 1) * HD], a.rearrange("(k p) -> k p", p=HD)))
    d.append((PROW[R_BF:R_BF + 1, 0, P - HEADS:P], T["b_f"].rearrange("(k p) -> k p", p=HEADS)))
    for l in range(2):
        for k in range(3):
            d.append((PROW[k * FT:(k + 1) * FT, 1 + l, :], tall(T["ffn_conv"][l, k])))
    return d


N_PARAM_DMAS = 15 + 4 + 1 + 6


def constants():
    c = np.zeros((P, N_CONST), np.float32)
    r = np.arange(P)
    row, column = r[:, None], r[None, :]
    c[:, C_ID:C_ID + P] = np.eye(P)
    c[:, C_ONE:C_ONE + P] = 1.0
    c[:, C_ONE64:C_ONE64 + P] = row // HD == column // HD
    c[:, C_CAUSAL:C_CAUSAL + P] = np.where(column <= row, 0.0, NEG)
    c[:, C_UPPER:C_UPPER + P] = np.where(column >= row, 0.0, NEG)
    same = row // CH == column // CH
    c[:, C_GF:C_GF + P] = same & (row <= column)
    c[:, C_GB:C_GB + P] = same & (row > column)
    half = P // 2
    inv = (np.float32(10000.0) ** (-np.arange(half, dtype=np.float32) / np.float32(half))).astype(np.float32)
    ang = np.concatenate([inv, inv])[:, None] * np.arange(S, dtype=np.float32)[None, :]
    c[:, C_COS:C_COS + S] = np.cos(ang)
    c[:, C_SIN:C_SIN + S] = np.where(row < half, 1.0, -1.0) * np.sin(ang)
    return c


STOP = 6


def kernel(**inputs):
    import concourse.bacc as bacc
    from concourse.bass_utils import run_bass_kernel_spmd as run

    nc = bacc.Bacc("TRN2", target_bir_lowering=False, num_devices=1)
    arrays, T = {}, {}
    for name, a in {**inputs, "consts": constants()}.items():
        a = np.ascontiguousarray(a)
        arrays[f"in_{name}"] = a
        T[name] = nc.dram_tensor(f"in_{name}", a.shape, F32, kind="ExternalInput").ap()
    out = nc.dram_tensor("out", (1, S, D), F32, kind="ExternalOutput").ap()
    build(nc, T, out, STOP)
    r = run(nc, [arrays], core_ids=[0])
    return r.results[0]["out"]
```

```python
from contextlib import ExitStack

import numpy as np

import concourse.bass as bass
from concourse import mybir

F32 = mybir.dt.float32
F32R = mybir.dt.float32r
BF16 = mybir.dt.bfloat16
ACT = mybir.ActivationFunctionType
ALU = mybir.AluOpType
AX = mybir.AxisListType

P = 128
S = 512
D = 1024
KT = D // P
TB = S // P
FF = 2816
FT = FF // P
EPS = 1e-6
NEG = -1e30

HEADS = 16
HD = D // HEADS
PAIRS = HEADS // 2

GH = 4
GDK = 128
CH = 64
NCH = S // CH
GATE_RANK = 16
SWA_GROUPS = 2
SWA_Q = 4
G_Q, G_K, G_V, G_R, G_LR = 0, 512, 1024, 2048, 3072
S_Q, S_K, S_V, GA, GB = 3104, 4128, 4384, 4640, 5664

(R_ATTN, R_FFN, R_KV, R_MIX, R_FFN2, R_ACONV, R_GBF, R_GBB, R_OUTG, R_SQG, R_SKG, R_QN, R_KN,
 R_BF) = (0, 16, 32, 40, 48, 56, 80, 84, 88, 90, 91, 92, 93, 94)
N_PRM = 96
N_FC = 3 * FT
C_ID, C_ONE, C_ONE64, C_CAUSAL, C_UPPER, C_GF, C_GB, C_COS = 0, 128, 256, 384, 512, 640, 768, 896
C_SIN = C_COS + S
N_CONST = C_SIN + S


class WeightPhase:

    def __init__(self, stream, ring, iters, units):
        self.ring, self.iters, self.units, self.U = ring, iters, units, len(units)
        assert iters == 1 or self.U % ring == 0
        self.base = stream["units"]
        self.owner = list(stream["owner"])
        self.loads0 = list(stream["loads"])
        stream["units"] += self.U * iters
        for n in range(self.U * iters):
            s = (n % self.U) % ring
            stream["owner"][s] = self.base + n
            stream["loads"][s] += 1

    def unit(self, i, j):
        return i * self.U + (self.base + j)

    def slot(self, j):
        return j % self.ring

    def load_count(self, i, j):
        return i * (self.U // self.ring if self.iters > 1 else 0) + (self.loads0[self.slot(j)] + j // self.ring + 1)

    def before(self, i, j):
        if j >= self.ring or not isinstance(i, int) or i > 0:
            return i * self.U + (self.base + j - self.ring + 1)
        last = self.owner[self.slot(j)]
        return None if last is None else last + 1


class Steps:

    def __init__(self, engine, sem):
        self.engine, self.sem = engine, sem
        self.base, self.n, self.i, self.stride, self.start = 0, 0, 0, None, 0

    def enter_loop(self, start):
        self.base, self.n, self.i, self.stride, self.start = self.base + self.n, 0, 0, None, start

    def enter(self, i):
        self.i, self.n = i, 0

    def leave_iteration(self):
        if self.stride is None:
            self.stride = self.n
        assert self.stride == self.n

    def leave_loop(self, iters):
        self.base += (self.stride or 0) * iters
        self.i, self.n, self.stride, self.start = 0, 0, None, 0

    def value(self):
        if isinstance(self.i, int):
            return self.base + self.n + (self.i - self.start) * (self.stride or 0)
        return self.i * self.stride + (self.base + self.n - self.start * self.stride)

    def link(self, ins):
        self.n += 1
        ins.then_inc(self.sem, 1)
        self.engine.wait_ge(self.sem, self.value())


def loop(engine, iters, body, steps=None, start=0):
    def one(i):
        if steps:
            steps.enter(i)
        body(i)
        if steps:
            steps.leave_iteration()
    if steps:
        steps.enter_loop(start)
    one(start)
    if iters > start + 1:
        with engine.Fori(start + 1, iters) as i:
            one(i)
    if steps:
        steps.leave_loop(iters - start)


def build(nc, T, out):
    with ExitStack() as ctx:
        sems = {}

        def sem(name):
            if name not in sems:
                sems[name] = ctx.enter_context(nc.semaphore(name))
            return sems[name]

        pos = [(nc.sbuf_base + 31) // 32 * 32]

        def at(name, shape, dt, offset=None):
            size = int(np.prod(shape[1:])) * (2 if dt == BF16 else 4)
            if offset is None:
                offset = pos[0]
                pos[0] += (size + 31) // 32 * 32
            return nc.alloc_sbuf_tensor_at(name, shape, dt, offset=offset)

        XT = at("XT", [P, KT, S], F32)
        XH = at("XH", [P, KT, S], F32R)
        XL = at("XL", [P, KT, S], F32R)
        raw_at, RAW = [], []
        for s in range(4):
            raw_at.append(pos[0])
            RAW.append(at(f"RAW{s}", [P, KT, P], F32))
        ring_at = []
        WH, WL = [], []
        for s in range(4):
            ring_at.append(pos[0])
            WH.append(at(f"WH{s}", [P, KT, P], F32R))
            WL.append(at(f"WL{s}", [P, KT, P], F32R))
        W_at = []
        W = []
        for s in range(10):
            W_at.append(pos[0])
            W.append(at(f"W{s}", [P, S + 8 if s in (1, 2) else S], F32))
        IDF = at("IDF", [P, P], F32)
        ONE = at("ONE", [P, P], F32)
        ONE64 = at("ONE64", [P, P], F32)
        IDB = at("IDB", [P, P], BF16)
        MCAUSAL = at("MCAUSAL", [P, P], BF16)
        MUPPER = at("MUPPER", [P, P], BF16)
        PRM = at("PRM", [P, N_PRM], F32)
        FC = at("FC", [P, 2 * N_FC], F32)
        SINK = at("SINK", [P, 8], F32)
        COL = at("COL", [P, 40], F32)
        EPSC, ONEC, TICK = COL[:, 0:1], COL[:, 1:2], COL[:, 2:3]
        NEGM, RS, RINV = COL[:, 4:8], COL[:, 8:12], COL[:, 12:16]
        SNEG, SRS, SINV, SESK = [[COL[:, c + d:c + d + 4] for d in (0, 16)] for c in (4, 8, 12, 16)]
        SMAX = COL[:, 36:40]
        BIG = pos[0]
        assert BIG + 2 * FT * S * 4 <= nc.sbuf_usable_end, (BIG, nc.sbuf_usable_end)
        KB = 1024
        XIN = at("XIN", [P, TB, D], F32, BIG)
        PROW = at("PROW", [P, 3, P], F32, BIG + 16 * KB)
        CST = at("CST", [P, C_GF], F32, BIG + 18 * KB)
        BUH = at("BUH", [P, KT, S], F32R, BIG + 32 * KB)
        BUL = at("BUL", [P, KT, S], F32R, BIG + 48 * KB)
        HH = at("HH", [P, FT, S], F32R, BIG)
        HL = at("HL", [P, FT, S], F32R, BIG + 44 * KB)
        X2H = at("X2H", [P, KT, S], F32R, BIG)
        X2L = at("X2L", [P, KT, S], F32R, BIG + 16 * KB)
        OH = at("OH", [P, KT, S], F32R, BIG + 32 * KB)
        OL = at("OL", [P, KT, S], F32R, BIG + 48 * KB)
        KH, KL, QH, QL = [at(n, [P, S], F32R, BIG + (64 + 2 * k) * KB) for k, n in enumerate(("KH", "KL", "QH", "QL"))]
        VH = at("VH", [P, TB, P], F32R, BIG + 72 * KB)
        VL = at("VL", [P, TB, P], F32R, BIG + 74 * KB)
        PQ = at("PQ", [P, 6 * P], F32, BIG + 85 * KB)
        PT_at = [0, 2 * KB, 2 * KB + 1536]
        PTH = [at(f"PTH{j}", [P, S - j * P], F32R, BIG + 76 * KB + PT_at[j]) for j in range(3)]
        PTL = [at(f"PTL{j}", [P, S - j * P], F32R, BIG + 76 * KB + 4608 + PT_at[j]) for j in range(3)]
        PTH.append(at("PTH3", [P, P], F32R, BIG + 85 * KB + 512))
        PTL.append(at("PTL3", [P, P], F32R, BIG + 85 * KB + 1024))
        CT = at("CT", [P, TB, HEADS], F32, BIG + 88 * KB)
        assert BIG + 88 * KB + 4 * TB * HEADS <= nc.sbuf_usable_end
        QB = list(range(TB))[::-1]
        PROB = [PQ[:, 0:128], PQ[:, 128:384], PQ[:, 384:768], W[7][:, 0:S]]

        YGH = at("YGH", [P, KT, S], F32R, BIG)
        YGL = at("YGL", [P, KT, S], F32R, BIG + 16 * KB)
        BC = at("BC", [P, 2 * GH, S], F32, BIG + 32 * KB)
        KIH, KIL, KTH, KTL = [at(n, [P, S], F32R, BIG + (52 + 2 * k) * KB)
                              for k, n in enumerate(("KIH", "KIL", "KTH", "KTL"))]
        QDH = [at(f"QDH{d}", [P, NCH, 2 * CH], F32R, ring_at[2 + d]) for d in range(2)]
        QDL = [at(f"QDL{d}", [P, NCH, 2 * CH], F32R, ring_at[2 + d] + 4 * KB) for d in range(2)]
        SQ = [at(f"SQ{k}", [P, 2 * P], F32, raw_at[2] + k * KB) for k in range(TB)]
        E = [at(f"E{k}", [P, S], F32, raw_at[3] + 2 * k * KB) for k in range(2)]
        ON = at("ON", [P, TB, 2 * P], F32, raw_at[3])
        GSS, GR, GRR = COL[:, 4:8], COL[:, 8:12], COL[:, 12:16]
        VGH = at("VGH", [P, TB, 2 * P], F32R, BIG + 60 * KB)
        VGL = at("VGL", [P, TB, 2 * P], F32R, BIG + 64 * KB)
        SH = at("SH", [P, NCH - 1, 2 * P], F32R, BIG + 68 * KB)
        SL = at("SL", [P, NCH - 1, 2 * P], F32R, BIG + 75 * KB)
        ST = [at(f"ST{k}", [P, 2 * P], F32, BIG + (82 + k) * KB) for k in range(2)]
        SCH = at("SCH", [P, S], F32R, BIG + 84 * KB)
        SCL = at("SCL", [P, S], F32R, BIG + 86 * KB)
        SC0 = at("SC0", [P, S], F32, BIG + 86 * KB)
        UP = at("UP", [2 * GATE_RANK, 2 * GH * GDK], F32, BIG + 68 * KB)
        GMASK = [W[9][:, 0:P], W[9][:, P:2 * P]]
        EBL = [W[9][:, 2 * P + d * NCH:2 * P + (d + 1) * NCH] for d in range(2)]
        YSH = at("YSH", [P, KT, S], F32R, BIG + 32 * KB)
        YSL = at("YSL", [P, KT, S], F32R, BIG + 48 * KB)
        SKH, SKL = [at(n, [P, S], F32R, BIG + (64 + 2 * k) * KB) for k, n in enumerate(("SKH", "SKL"))]
        SVH, SVL = [at(n, [P, TB, P], F32R, BIG + (68 + 2 * k) * KB) for k, n in enumerate(("SVH", "SVL"))]
        SQH = [at(f"SQH{t}", [P, S], F32R, BIG + (72 + 4 * t) * KB) for t in range(SWA_Q)]
        SQL = [at(f"SQL{t}", [P, S], F32R, BIG + (74 + 4 * t) * KB) for t in range(SWA_Q)]
        SROT = at("SROT", [P, S], F32, ring_at[3])
        SPH = [at("SPH0", [P, S], F32R, W_at[1]), at("SPH1", [P, S], F32R, raw_at[3])]
        SPL = [at("SPL0", [P, S], F32R, W_at[5]), at("SPL1", [P, S], F32R, raw_at[3] + 2 * KB)]
        SPROB = [[W[k][:, 0:3 * P] for k in (2, 3, 4, 6)],
                 [at(f"SPROB{t}", [P, 3 * P], F32, ring_at[3] + 2 * t * KB) for t in range(SWA_Q)]]
        MGH = at("MGH", [P, KT, S], F32R, BIG + 64 * KB)
        MGL = at("MGL", [P, KT, S], F32R, ring_at[2])

        WIN = [list(range(max(0, q - 1), min(TB - 1, q + 1) + 1)) for q in range(TB)]
        SEEN = [sum(len(w) for w in WIN[:q]) for q in range(TB + 1)]

        def gla_out(b):
            return PS[:, 6 + b // 2, b % 2 * 2 * P:(b % 2 + 1) * 2 * P]

        def chunk_alone(t, c):
            flat = t.rearrange("p n c -> p (n c)")
            start = 2 * c * CH - c % 2 * CH
            return flat[:, start:start + P]

        def chunk_order(d):
            return [n if d == 0 else NCH - 1 - n for n in range(NCH - 1)]

        def kv_place(n):
            bank = (0, 1)[n % 2] if n // 2 < 2 else (4, 5)[n % 2]
            return bank, slice(n // 2 % 2 * 2 * P, (n // 2 % 2 + 1) * 2 * P)

        PS = ctx.enter_context(nc.psum_tensor("PS", [P, 8, S], F32))
        cums = nc.dram_tensor("cums", (HEADS, S), F32, kind="Internal").ap()

        stream = {"units": 0, "owner": [None] * 4, "loads": [0] * 4}

        def rows(w):
            return w.rearrange("(k p) n -> p k n", p=P)

        def wphase(ring, iters, units):
            return WeightPhase(stream, ring, iters, units)

        def col(base, step=P):
            return lambda i: i * step + base

        a_in, a_out = rows(T["a_w_in"][0]), rows(T["a_w_out"][0])
        up = [rows(T["ffn_w_up"][l]) for l in range(2)] + [rows(T["w_ffn_in_2"][0])]
        down = [rows(T["ffn_w_down"][l]) for l in range(2)] + [rows(T["w_ffn_out_2"][0])]
        kvf, qg, b_out = rows(T["w_kvf"]), rows(T["b_w_qg"][0]), rows(T["b_w_out"][0])
        w_in, w_og, w_os, w_out = [rows(T[n][0]) for n in ("w_in_2", "w_o_gla_2", "w_o_swa_2", "w_out_2")]

        def square_units(w, n=4):
            return [(w, 0, KT, col(j * P, n * P)) for j in range(n)]

        def ffn_phases(l):
            u = []
            for p in range(2):
                u += [(up[l], 0, KT, col(p * P, 2 * P)), (up[l], 0, KT, col(FF + p * P, 2 * P))]
            d = []
            for p in range(2):
                d += [(down[l], k0, min(KT, FT - k0), col(p * P, 2 * P)) for k0 in (0, 8, 16)]
            return wphase(4, FT // 2, u), wphase(3, KT // 2, d)

        ph = {}
        ph["mix"] = wphase(3, KT, [(a_in, 0, KT, col(D)), (a_in, 0, KT, col(2 * D)), (a_in, 0, KT, col(0))])
        ph["mix_out"] = wphase(4, 2, square_units(a_out))
        ph["up0"], ph["down0"] = ffn_phases(0)
        ph["forget"] = wphase(4, 1, [(kvf, 0, KT, lambda i: 2 * D + HEADS - P)])
        ph["attn"] = wphase(4, PAIRS, [(kvf, 0, KT, col(0)), (kvf, 0, KT, col(D)),
                                       (qg, 0, KT, col(0)), (qg, 0, KT, col(D))])
        ph["attn_out"] = wphase(4, 2, square_units(b_out))
        ph["up1"], ph["down1"] = ffn_phases(1)
        ph["lr"] = wphase(4, 1, [(w_in, 0, KT, lambda i: G_LR)])
        ph["gla"] = wphase(2, GH, [(w_in, 0, KT, col(G_Q)), (w_in, 0, KT, col(G_K)),
                                   (w_in, 0, KT, col(G_V, 256)), (w_in, 0, KT, col(G_V + P, 256)),
                                   (w_in, 0, KT, col(G_R, 256)), (w_in, 0, KT, col(G_R + P, 256))])
        ph["swa"] = wphase(2, SWA_GROUPS, [(w_in, 0, KT, col(S_K))] +
                           [(w_in, 0, KT, col(S_Q + t * P, SWA_Q * P)) for t in range(SWA_Q)] +
                           [(w_in, 0, KT, col(S_V))])
        ph["merge"] = wphase(2, KT, [(w_in, 0, KT, col(GA)), (w_in, 0, KT, col(GB)),
                                     (w_og, 0, KT, col(0)), (w_os, 0, KT, col(0))])
        ph["out2"] = wphase(2, 2, square_units(w_out))
        stream["owner"][2] = stream["owner"][3] = stream["units"] - 1
        ph["up2"], ph["down2"] = ffn_phases(2)

        loaded = [sem(f"weights_loaded{s}") for s in range(4)]
        high_done, split_done, unit_done = sem("weights_high"), sem("weights_split"), sem("unit_done")

        def tile(t, m):
            return t[:, m, :] if isinstance(m, int) else t[:, bass.ds(m, 1), :].rearrange("p a n -> p (a n)")

        def window_out(t, i, q):
            c = slice(q * P, (q + 1) * P)
            return t[:, i * SWA_Q:(i + 1) * SWA_Q, c] if isinstance(i, int) else t[:, bass.ds(i * SWA_Q, SWA_Q), c]

        def column(t, m):
            return t[:, m:m + 1] if isinstance(m, int) else t[:, bass.ds(m, 1)]

        ORDER = {"_x": 0, 0: 1, 1: 2, 2: 3, 3: 4, 4: 5, 5: 6}

        def tiles(n):
            return ORDER[n] * KT


        block = ctx.enter_context(nc.Block())

        @block.sync
        def _(sp):
            for t in range(TB):
                sp.dma_start(XIN[:, t, :], T["x"][0, t * P:(t + 1) * P, :]).then_inc(sem("x_loaded"), 16)
            for p in ph.values():
                def body(i, p=p):
                    for j, (w, k0, nk, c) in enumerate(p.units):
                        free = p.before(i, j)
                        if free is not None:
                            sp.wait_ge(split_done, free)
                            if not isinstance(i, int):
                                sp.sem_inc(sem("sync_step"), 1)
                        sp.dma_start(RAW[p.slot(j)][:, 0:nk, :], w[:, k0:k0 + nk, bass.ds(c(i), P)]).then_inc(
                            loaded[p.slot(j)], 16)
                loop(sp, p.iters, body)
            for t in range(TB):
                sp.wait_ge(sem("out_rows"), 2 * (t + 1))
                sp.dma_start(out[0, t * P:(t + 1) * P, :], XIN[:, t, :]).then_inc(sem("stored"), 16)
            sp.wait_ge(sem("stored"), 16 * TB)

        @block.gpsimd
        def _(pool):
            pool.wait_ge(sem("zeroed"), 1)
            for p in ph.values():
                def body(i, p=p):
                    for j, (w, k0, nk, c) in enumerate(p.units):
                        s = p.slot(j)
                        free = p.before(i, j)
                        if free is not None:
                            pool.wait_ge(unit_done, free)
                        pool.wait_ge(loaded[s], p.load_count(i, j) * 16)
                        if not isinstance(i, int):
                            pool.tensor_tensor(TICK, ONEC, ONEC, ALU.mult)
                        pool.tensor_scalar(WH[s][:, 0:nk, :], RAW[s][:, 0:nk, :], 1.0, 1.0, ALU.mult, ALU.mult).then_inc(high_done, 1)
                        pool.wait_ge(high_done, p.unit(i, j) + 1)
                        pool.tensor_tensor(WL[s][:, 0:nk, :], RAW[s][:, 0:nk, :], WH[s][:, 0:nk, :].bitcast(F32),
                                           ALU.subtract).then_inc(split_done, 1)
                loop(pool, p.iters, body)

        @block.tensor
        def _(pe):
            def unit(p, i, j, bank, xh, xl, first=True, last=True, ready=None):
                pe.wait_ge(split_done, p.unit(i, j) + 1)
                s, (_, k0, nk, _) = p.slot(j), p.units[j]
                for k in range(nk):
                    if ready:
                        pe.wait_ge(ready[0], ready[2] + ready[1] * (k0 + k + 1))
                    o = PS[:, bank, :]
                    pe.matmul(o, WH[s][:, k, :], xh[:, k0 + k, :], start=first and k == 0, stop=False)
                    pe.matmul(o, WH[s][:, k, :], xl[:, k0 + k, :], start=False, stop=False)
                    mm = pe.matmul(o, WL[s][:, k, :], xh[:, k0 + k, :], start=False, stop=last and k == nk - 1)
                mm.then_inc(unit_done, 1)

            def product(o, ah, al, bh, bl, start=True, stop=True, loose=False):
                pe.matmul(o, ah, bh, start=start, stop=False, skip_group_check=loose)
                pe.matmul(o, ah, bl, start=False, stop=False, skip_group_check=loose)
                return pe.matmul(o, al, bh, start=False, stop=stop, skip_group_check=loose)

            def row_sums(n):
                pe.wait_ge(sem("acc"), tiles(n) + KT)
                pe.matmul(PS[:, 7, :], ONE[:, :], W[1][:, 0:S], start=True, stop=True).then_inc(sem("nsum"), 1)

            def residual(p, n, groups, xh, xl, ready, banks_read):
                tpi = p.U // groups
                def body(i):
                    for t in range(tpi):
                        m = i * tpi + t
                        if t >= 2 or not isinstance(i, int) or i > 0:
                            pe.wait_ge(sem("resid"), tiles(n) + m - 1)
                        else:
                            pe.wait_ge(*banks_read[t])
                        for g in range(groups):
                            unit(p, i, t * groups + g, t % 2, xh, xl, g == 0, g == groups - 1,
                                 ready if isinstance(i, int) and i == 0 and t == 0 else None)
                loop(pe, p.iters, body)

            def ffn(l, n):
                pu, pd = ph[f"up{l}"], ph[f"down{l}"]
                def body(i):
                    for q in range(2):
                        m = 2 * i + q
                        for k in range(2):
                            if not isinstance(i, int) or i > 0:
                                pe.wait_ge(sem(f"ffn_{'ag'[k]}"), m + (l * FT - 1))
                            elif q == 0:
                                pe.wait_ge(sem("resid"), tiles(n) + KT - 1 + k)
                            unit(pu, i, 2 * q + k, 2 * q + k, XH, XL,
                                 ready=(sem("xld"), 1, tiles(n)) if isinstance(i, int) and i == 0 and q == k == 0 else None)
                            if isinstance(i, int) and i == 0 and q == k == 0:
                                row_sums(n)
                loop(pe, pu.iters, body)
                residual(pd, n + 1, 3, HH, HL, (sem("ffn_low"), 1, l * FT),
                         [(sem("ffn_a"), (l + 1) * FT), (sem("ffn_g"), (l + 1) * FT)])

            def scores(b, h):
                H, r = 2 * b + h, slice(HD * h, HD * h + HD)
                if h == 0:
                    pe.wait_ge(sem("hn_low"), 2 * b + 2)
                if not isinstance(b, int) or H > 0:
                    pe.wait_ge(sem("pt_low"), H * TB)
                for q in QB:
                    n = (q + 1) * P
                    product(PS[:, 4 + q, 0:n], QH[r, q * P:n], QL[r, q * P:n], KH[r, 0:n], KL[r, 0:n],
                            stop=False, loose=True)
                    pe.matmul(PS[:, 4 + q, q * P:n], IDB[:, :], MCAUSAL[:, :], start=False, stop=True,
                              skip_group_check=True).then_inc(sem("scores"), 1)

            def turn(b, h):
                H = 2 * b + h
                pe.wait_ge(sem("prob"), H * TB + TB)
                for j in range(TB):
                    for q in range(j, TB):
                        tr = pe.transpose(PS[:, 4 + j, (q - j) * P:(q - j + 1) * P],
                                          PROB[q][:, j * P:(j + 1) * P], IDF[:, :])
                    tr.then_inc(sem("prob_t"), 1)

            def weigh(b, h):
                H = 2 * b + h
                if h == 0:
                    pe.wait_ge(sem("v_low"), b + 1)
                if not isinstance(b, int) or H > 0:
                    pe.wait_ge(sem("o_read"), H * 1)
                for j in range(TB):
                    pe.wait_ge(sem("pt_low"), H * TB + (j + 1))
                    n = (TB - j) * P
                    product(PS[:, 2, j * P:S], VH[:, j, :], VL[:, j, :], PTH[j][:, 0:n], PTL[j][:, 0:n],
                            start=j == 0, stop=j == TB - 1, loose=True).then_inc(sem("weighed"), 1)

            def head_sums(n):
                pe.wait_ge(sem("hn_sq"), n + 1)
                pe.matmul(PS[:, 3, :], ONE64[:, :], W[2][:, 0:S], start=True, stop=True).then_inc(sem("hn_sum"), 1)

            def attention():
                pe.wait_ge(sem("resid"), tiles(1) + KT)
                pe.wait_ge(sem("xld"), tiles(1) + KT)
                row_sums(1)
                unit(ph["forget"], 0, 0, 4, X2H, X2L, ready=(sem("x2_low"), 1, 0))
                p = ph["attn"]
                def body(i):
                    first = isinstance(i, int) and i == 0
                    if not first:
                        pe.wait_ge(sem("kq_read"), i * 2)
                    unit(p, i, 0, 0, X2H, X2L)
                    if not first:
                        scores(i - 1, 0)
                    if first:
                        pe.wait_ge(sem("fg_c"), 1)
                        for t in range(TB):
                            tr = pe.transpose(PS[:, 5, t * P:(t + 1) * P], W[4][:, t * P:(t + 1) * P], IDF[:, :])
                        tr.then_inc(sem("fg_t"), 1)
                    else:
                        pe.wait_ge(sem("vg_read"), i * 2)
                    unit(p, i, 1, 1, X2H, X2L)
                    if not first:
                        pe.wait_ge(sem("v_low"), i * 1)
                    head_sums(i * 2)
                    if not first:
                        turn(i - 1, 0)
                    pe.wait_ge(sem("kq_read"), i * 2 + 1)
                    unit(p, i, 2, 0, XH, XL)
                    if not first:
                        weigh(i - 1, 0)
                        scores(i - 1, 1)
                    pe.wait_ge(sem("vg_read"), i * 2 + 1)
                    unit(p, i, 3, 1, XH, XL)
                    pe.wait_ge(sem("hn_v"), i * 2 + 1)
                    head_sums(i * 2 + 1)
                    if not first:
                        turn(i - 1, 1)
                    pe.wait_ge(sem("hn_v"), i * 2 + 2)
                    for t in range(TB):
                        tr = pe.transpose(PS[:, 3, t * P:(t + 1) * P], W[5][:, t * P:(t + 1) * P], IDF[:, :])
                    tr.then_inc(sem("v_t"), 1)
                    if not first:
                        weigh(i - 1, 1)
                body(0)
                loop(pe, PAIRS, body, start=1)
                for h in range(2):
                    scores(PAIRS - 1, h)
                    turn(PAIRS - 1, h)
                    weigh(PAIRS - 1, h)
                residual(ph["attn_out"], 2, 1, OH, OL, (sem("o_low"), 1, 0),
                         [(sem("kq_read"), 2 * PAIRS), (sem("vg_read"), 2 * PAIRS)])

            def gates():
                pe.wait_ge(sem("resid"), tiles(3) + KT)
                unit(ph["lr"], 0, 0, 0, XH, XL, ready=(sem("xld"), 1, tiles(3)))
                row_sums(3)

            def gate_tiles(which):
                for t in which:
                    if t >= 2:
                        pe.wait_ge(sem("z_read"), t - 1)
                    pe.matmul(PS[:, 6 + t % 2, :], UP[:, t * P:(t + 1) * P], W[1][0:2 * GATE_RANK, 0:S],
                              start=True, stop=True).then_inc(sem("z"), 1)

            def gla_inter(i, d):
                n = 2 * i + d
                for s, c in enumerate(chunk_order(d)):
                    to = c + 1 if d == 0 else c - 1
                    pe.wait_ge(sem("g_state_low"), n * (NCH - 1) + (s + 1))
                    mm = product(gla_out(to // 2), chunk_alone(QDH[d], to), chunk_alone(QDL[d], to), SH[:, s, :], SL[:, s, :],
                                 start=d == 0 and to in (1, NCH // 2), stop=d == 1 and to in (0, NCH // 2), loose=True)
                mm.then_inc(sem("g_inter"), 1)

            def gla_turn(i):
                pe.wait_ge(sem("g_on"), i * TB + TB)
                for u in range(2):
                    for b in range(TB):
                        tr = pe.transpose(PS[:, (3, 5)[u], b * P:(b + 1) * P], ON[:, b, u * P:(u + 1) * P], IDF[:, :])
                tr.then_inc(sem("g_ot"), 1)

            def gla(i):
                p = ph["gla"]
                later = not isinstance(i, int) or i > 0
                if later:
                    pe.wait_ge(sem("g_sc"), i * 1)
                unit(p, i, 0, 2, XH, XL)
                if later:
                    gla_inter(i - 1, 1)
                else:
                    pe.wait_ge(sem("up_loaded"), 32)
                    pe.wait_ge(sem("lr"), 1)
                    gate_tiles((0, 1, 2, 3))
                unit(p, i, 1, 4, XH, XL)
                if not later:
                    gate_tiles((4, 5))
                unit(p, i, 2, 0, XH, XL)
                if later:
                    gla_turn(i - 1)
                else:
                    gate_tiles((6, 7))
                unit(p, i, 3, 1, XH, XL)
                def scores(d):
                    n = 2 * i + d
                    pe.wait_ge(sem("gd_low"), n * 3 + 2)
                    if d == 1:
                        pe.wait_ge(sem("g_sc0"), i + 1)
                    for b in range(TB):
                        c = slice(b * P, (b + 1) * P)
                        q = [t[:, 2 * b:2 * b + 2, 0:CH] for t in (QDH[d], QDL[d])]
                        mm = product(PS[:, 2, c].rearrange("p (n c) -> p n c", n=2), KIH[:, c], KIL[:, c], q[0], q[1])
                    mm.then_inc(sem("g_scores"), 1)
                    pe.wait_ge(sem("g_kt"), n + 1)
                    if d == 0 and later:
                        pe.wait_ge(sem("g_y"), i * 2)
                    for t in range(TB):
                        tr = pe.transpose(PS[:, 3, t * P:(t + 1) * P], W[8][:, t * P:(t + 1) * P], IDF[:, :])
                    tr.then_inc(sem("g_kt_t"), 1)
                def keys_values(d):
                    n = 2 * i + d
                    pe.wait_ge(sem("gd_low"), n * 3 + 3)
                    for c in chunk_order(d):
                        r, b = slice(c % 2 * CH, c % 2 * CH + CH), c // 2
                        bank, cols = kv_place(c)
                        product(PS[:, bank, cols], KTH[r, b * P:(b + 1) * P], KTL[r, b * P:(b + 1) * P],
                                VGH[r, b, :], VGL[r, b, :]).then_inc(sem("g_kv"), 1)
                if not later:
                    pe.wait_ge(sem("z_read"), 2 * GH)
                    unit(p, i, 4, 6, XH, XL)
                scores(0)
                pe.wait_ge(sem("g_read"), i * 6 + 4)
                for t in range(TB):
                    for u in range(2):
                        tr = pe.transpose(PS[:, 4 + t // 2, (t % 2 * 2 + u) * P:(t % 2 * 2 + u + 1) * P],
                                          W[3 + u][:, t * P:(t + 1) * P], IDF[:, :])
                tr.then_inc(sem("gv_t"), 1)
                if later:
                    unit(p, i, 4, 6, XH, XL)
                pe.wait_ge(sem("gv_low"), i * 2 + 2)
                keys_values(0)
                unit(p, i, 5, 7, XH, XL)
                scores(1)
                pe.wait_ge(sem("g_read"), i * 6 + 6)
                gla_inter(i, 0)
                keys_values(1)
                pe.wait_ge(sem("g_sc_low"), i + 1)
                for b in range(TB):
                    c = slice(b * P, (b + 1) * P)
                    product(gla_out(b), SCH[:, c], SCL[:, c], VGH[:, b, :], VGL[:, b, :],
                            start=False, stop=False, loose=True)

            def swa(i):
                p = ph["swa"]
                later = not isinstance(i, int) or i > 0
                def head_sum(n):
                    pe.wait_ge(sem("sw_sq"), i * 5 + (n + 1))
                    if n >= 2:
                        pe.wait_ge(sem("sw_v"), i * 5 + (n - 1))
                    pe.matmul(PS[:, 4 + n % 2, :], ONE[:, :], E[n % 2][:, :], start=True, stop=True).then_inc(sem("sw_sum"), 1)
                for j in range(6):
                    if j == 3 and later:
                        pe.wait_ge(sem("sw_out"), i * TB)
                    unit(p, i, j, j % 4, XH, XL)
                    if j > 0:
                        head_sum(j - 1)
                pe.wait_ge(sem("sw_read"), i * 6 + 6)
                for t in range(TB):
                    tr = pe.transpose(PS[:, 6, t * P:(t + 1) * P], W[9][:, t * P:(t + 1) * P], IDF[:, :])
                tr.then_inc(sem("sv_t"), 1)
                pe.wait_ge(sem("sv_low"), i + 1)
                pe.wait_ge(sem("sw_low"), i * 5 + 5)
                def scores(q):
                    win, n = WIN[q], i * 4 * TB + 4 * q
                    if q > 0:
                        pe.wait_ge(sem("sw_exp"), n)
                    for t in range(SWA_Q):
                        c = slice(q * P, (q + 1) * P)
                        k = slice(win[0] * P, (win[-1] + 1) * P)
                        product(PS[:, 4 + t, 0:len(win) * P], SQH[t][:, c], SQL[t][:, c], SKH[:, k], SKL[:, k],
                                stop=False, loose=True)
                        if q > 0:
                            mm = pe.matmul(PS[:, 4 + t, 0:P], IDB[:, :], MUPPER[:, :], start=False,
                                           stop=q == TB - 1, skip_group_check=True)
                        if q < TB - 1:
                            mm = pe.matmul(PS[:, 4 + t, (len(win) - 1) * P:len(win) * P], IDB[:, :], MCAUSAL[:, :],
                                           start=False, stop=True, skip_group_check=True)
                        mm.then_inc(sem("sw_scores"), 1)
                scores(0)
                for q in range(TB):
                    win, n = WIN[q], i * 4 * TB + 4 * q
                    if q < TB - 1:
                        scores(q + 1)
                    pe.wait_ge(sem("sw_prob"), n + 4)
                    for jj in range(len(win)):
                        if q > 0 and jj == 0:
                            pe.wait_ge(sem("sw_plow"), i * SEEN[TB] + SEEN[q])
                        for t in range(SWA_Q):
                            tr = pe.transpose(PS[:, jj, t * P:(t + 1) * P], SPROB[q % 2][t][:, jj * P:(jj + 1) * P], IDF[:, :])
                        tr.then_inc(sem("sw_pt"), 1)
                    if q > 0:
                        pe.wait_ge(sem("sw_out"), i * TB + q)
                    for jj, j in enumerate(win):
                        k = SEEN[q] + jj
                        pe.wait_ge(sem("sw_plow"), i * SEEN[TB] + (k + 1))
                        product(PS[:, 3, :], SVH[:, j, :], SVL[:, j, :], SPH[k % 2][:, :], SPL[k % 2][:, :], start=jj == 0,
                                stop=jj == len(win) - 1).then_inc(sem("sw_pv"), 1)

            def merge(i):
                p = ph["merge"]
                for j, (xh, xl) in enumerate(((XH, XL), (XH, XL), (YGH, YGL), (YSH, YSL))):
                    if isinstance(i, int) and i == 0:
                        if j == 3:
                            pe.wait_ge(sem("sw_out"), SWA_GROUPS * TB)
                    else:
                        pe.wait_ge(sem("mg_read"), i * 4 + (j - 3))
                    unit(p, i, j, j, xh, xl)

            pe.wait_ge(sem("consts"), 16)
            pe.wait_ge(sem("params"), 16 * N_PARAM_DMAS)
            pe.wait_ge(sem("zeroed"), 1)
            pe.transpose(PS[:, 2, 0:P], PROW[:, 0, :], CST[:, C_ID:C_ID + P])
            for l in range(2):
                tr = pe.transpose(PS[:, 2, P * (l + 1):P * (l + 1) + P], PROW[:, 1 + l, :], CST[:, C_ID:C_ID + P])
            tr.then_inc(sem("prm_t"), 1)
            pe.wait_ge(sem("x_loaded"), 16 * TB)
            for m in range(KT):
                if m >= 2:
                    pe.wait_ge(sem("resid"), tiles("_x") + m - 1)
                for t in range(TB):
                    tr = pe.transpose(PS[:, m % 2, t * P:(t + 1) * P], XIN[:, t, m * P:(m + 1) * P], CST[:, C_ID:C_ID + P])
                tr.then_inc(sem("xt"), 1)
            p = ph["mix"]
            pe.wait_ge(sem("resid"), tiles("_x") + KT)
            def mix(i):
                for j in range(3):
                    if not isinstance(i, int) or i > 0:
                        pe.wait_ge(sem(f"mix_{'chb'[j]}"), i * 1)
                    unit(p, i, j, j, XH, XL, ready=(sem("xld"), 1, tiles("_x")) if isinstance(i, int) and i == 0 and j == 0 else None)
                    if isinstance(i, int) and i == 0 and j == 0:
                        row_sums("_x")
            loop(pe, KT, mix)
            residual(ph["mix_out"], 0, 1, BUH, BUL, (sem("mix_low"), 1, 0),
                     [(sem("mix_c"), KT), (sem("mix_h"), KT)])
            ffn(0, 0)
            attention()
            ffn(1, 2)
            gates()
            gla(0)
            loop(pe, GH, gla, start=1)
            gla_inter(GH - 1, 1)
            gla_turn(GH - 1)
            loop(pe, SWA_GROUPS, swa)
            loop(pe, KT, merge)
            residual(ph["out2"], 4, 1, MGH, MGL, (sem("mg_low"), 1, 0),
                     [(sem("mg_read"), 4 * KT), (sem("mg_read"), 4 * KT)])
            ffn(2, 4)
            pe.wait_ge(sem("resid"), tiles(5) + KT)
            for t in range(TB):
                for h in range(2):
                    n = 2 * t + h
                    if n >= 2:
                        pe.wait_ge(sem("out_rows"), n - 1)
                    for m in range(4):
                        tr = pe.transpose(PS[:, 2 + n % 2, m * P:(m + 1) * P],
                                          XT[:, 4 * h + m, t * P:(t + 1) * P], IDF[:, :])
                    tr.then_inc(sem("out_t"), 1)

        @block.scalar
        def _(act):
            steps = Steps(act, sem("act_step"))
            link = steps.link

            def rsqrt(v, r, rr, ready, value, done):
                act.wait_ge(ready, value)
                link(act.activation(r, v, ACT.Ln))
                link(act.activation(r, r, ACT.Exp, scale=-0.5))
                act.activation(rr, r, ACT.Square).then_inc(done, 1)

            def norm(n):
                rsqrt(W[4][:, 0:S], W[5][:, 0:S], W[6][:, 0:S], sem("nv"), ORDER[n] + 1, sem("nrr"))

            def residual(n, iters, tpi, gains):
                def body(i):
                    for t in range(tpi):
                        m = i * tpi + t
                        if gains and (t >= 2 or not isinstance(i, int) or i > 0):
                            act.wait_ge(sem("acc"), tiles(n) + m - 1)
                        act.wait_ge(sem("resid"), tiles(n) + m + 1)
                        if not gains:
                            continue
                        act.wait_ge(sem("prm_ready"), 3)
                        act.activation(W[2 + t % 2][:, 0:S], tile(XT, m), ACT.Square).then_inc(sem("sq"), 1)
                        for xh, _, row in gains:
                            act.activation(tile(xh, m), tile(XT, m), ACT.Copy,
                                           scale=column(PRM, m + row)).then_inc(sem("xhd"), 1)
                if gains:
                    loop(act, iters, body, steps)

            def ffn(l, n, conv, gains):
                norm(n)
                def body(i):
                    for q in range(2):
                        m = 2 * i + q
                        u, g = W[3 + q][:, 0:S], W[5 + q]
                        act.wait_ge(sem("ffn_u" if conv else "ffn_a"), m + (l * FT + 1))
                        act.activation(u, u, ACT.Silu).then_inc(sem("ffn_silu"), 1)
                        act.wait_ge(sem("ffn_h"), m + l * FT + 1)
                        act.wait_ge(sem("prm_ready"), 3)
                        act.copy(tile(HH, m), g[:, 0:S]).then_inc(sem("ffn_high"), 1)
                loop(act, FT // 2, body, steps)
                residual(n + 1, KT // 2, 2, gains)

            def softmax(b, h):
                H = 2 * b + h
                for k, q in enumerate(QB):
                    act.wait_ge(sem("score_max"), H * TB + (k + 1))
                    pr = PROB[q][:, 0:(q + 1) * P]
                    act.activation(pr, pr, ACT.Exp, bias=NEGM[:, q:q + 1],
                                   accum_out=RS[:, q:q + 1]).then_inc(sem("exp"), 1)
                for k, q in enumerate(QB):
                    act.wait_ge(sem("rinv"), H * TB + (k + 1))
                    pr = PROB[q][:, 0:(q + 1) * P]
                    act.activation(pr, pr, ACT.Copy, scale=RINV[:, q:q + 1]).then_inc(sem("prob"), 1)

            def high_probs(b, h):
                H = 2 * b + h
                for j in range(TB):
                    act.wait_ge(sem("prob_t"), H * TB + (j + 1))
                    act.copy(PTH[j][:, 0:(TB - j) * P], PS[:, 4 + j, 0:(TB - j) * P]).then_inc(sem("pt_high"), 1)

            def high_out(b):
                act.wait_ge(sem("o_read"), 2 * b + 2)
                act.wait_ge(sem("prm_ready"), 3)
                act.copy(tile(OH, b), W[6][:, 0:S]).then_inc(sem("o_high"), 1)

            def load_cums(b):
                for h in range(2):
                    row = cums[2 * b + h, :] if isinstance(b, int) else \
                        cums[bass.ds(2 * b + h, 1), :].rearrange("a n -> (a n)")
                    act.dma_start(W[8 + h][:, 0:S], row.partition_broadcast(P)).then_inc(sem("cums_loaded"), 16)

            def head_rsqrt(n):
                rsqrt(W[3][:, 0:S], W[2][:, 0:S], W[4][:, 0:S], sem("hn_v"), n + 1, sem("hn_rr"))

            def head_high(n, to):
                act.wait_ge(sem("hn_x"), n + 1)
                act.copy(to[:, :], W[1][:, 0:S]).then_inc(sem("hn_high"), 1)

            def square(n):
                act.wait_ge(sem("kq_read"), n + 1)
                act.activation(W[2][:, 0:S], W[1][:, 0:S], ACT.Square).then_inc(sem("hn_sq"), 1)

            def attention():
                act.wait_ge(sem("resid"), tiles(1) + KT)
                for m in range(KT):
                    act.activation(X2H[:, m, :], XT[:, m, :], ACT.Copy,
                                   scale=PRM[:, R_KV + m:R_KV + m + 1]).then_inc(sem("x2_high"), 1)
                norm(1)
                act.wait_ge(sem("fg_z"), 1)
                link(act.activation(W[2][:, 0:S], W[1][:, 0:S], ACT.Abs))
                link(act.activation(W[2][:, 0:S], W[2][:, 0:S], ACT.Exp, scale=-1.0))
                act.activation(W[2][:, 0:S], W[2][:, 0:S], ACT.Ln, bias=ONEC).then_inc(sem("fg_sp"), 1)
                act.wait_ge(sem("fg_c"), 1)
                act.dma_start(cums[:, :], W[4][P - HEADS:P, 0:S]).then_inc(sem("cums_stored"), 16)
                act.wait_ge(sem("cums_stored"), 16)
                def body(i):
                    first = isinstance(i, int) and i == 0
                    square(i * 2)
                    if not first:
                        softmax(i - 1, 0)
                        high_probs(i - 1, 0)
                    head_rsqrt(i * 2)
                    if not first:
                        softmax(i - 1, 1)
                    load_cums(i)
                    if not first:
                        act.wait_ge(sem("scores"), i * 2 * TB)
                    head_high(i * 2, KH)
                    square(i * 2 + 1)
                    if not first:
                        high_probs(i - 1, 1)
                    head_rsqrt(i * 2 + 1)
                    if not first:
                        high_out(i - 1)
                    head_high(i * 2 + 1, QH)
                    act.wait_ge(sem("vg_read"), i * 2 + 2)
                    act.activation(W[6][:, 0:S], W[6][:, 0:S], ACT.Exp, scale=-1.0).then_inc(sem("g_exp"), 1)
                    act.wait_ge(sem("v_t"), i + 1)
                    if not first:
                        act.wait_ge(sem("weighed"), i * 2 * TB)
                    act.copy(VH[:, :, :], PS[:, 3, :].rearrange("p (t c) -> p t c", t=TB)).then_inc(sem("v_high"), 1)
                body(0)
                loop(act, PAIRS, body, steps, start=1)
                for h in range(2):
                    softmax(PAIRS - 1, h)
                    high_probs(PAIRS - 1, h)
                high_out(PAIRS - 1)

            def gates():
                act.wait_ge(sem("up_zeroed"), 1)
                for d, name in enumerate(("gla_gate_up_fwd_2", "gla_gate_up_bwd_2")):
                    act.dma_start(UP[d * GATE_RANK:(d + 1) * GATE_RANK, d * GH * GDK:(d + 1) * GH * GDK],
                                  T[name][0]).then_inc(sem("up_loaded"), 16)
                norm(3)
                act.dma_start(W[9][:, 0:2 * P], T["consts"][:, C_GF:C_GF + 2 * P]).then_inc(sem("g_masks"), 16)
                for t in range(2 * GH):
                    z, sp = W[2 + t % 2][:, 0:S], W[4 + t % 2][:, 0:S]
                    act.wait_ge(sem("z_read"), t + 1)
                    link(act.activation(sp, z, ACT.Abs))
                    link(act.activation(sp, sp, ACT.Exp, scale=-1.0))
                    act.activation(sp, sp, ACT.Ln, bias=ONEC).then_inc(sem("z_sp"), 1)

            def gla_square(i):
                act.wait_ge(sem("g_inter"), i * 2 + 2)
                for b in range(TB):
                    act.activation(SQ[b][:, :], gla_out(b), ACT.Square, accum_out=GSS[:, b:b + 1]).then_inc(sem("g_sq"), 1)
                rsqrt(GSS[:, :], GR[:, :], GRR[:, :], sem("g_nv"), i + 1, sem("g_nrr"))

            def gla_high(i):
                for u in range(2):
                    act.wait_ge(sem("g_y"), i * 2 + (u + 1))
                    act.wait_ge(sem("prm_ready"), 3)
                    act.copy(tile(YGH, i * 2 + u), W[3 + u][:, 0:S]).then_inc(sem("g_yhigh"), 1)

            def gla(i):
                later = not isinstance(i, int) or i > 0
                def decays(d):
                    act.wait_ge(sem("prm_ready"), 3)
                    act.activation(W[7][:, 0:S], tile(BC, i + GH * d), ACT.Exp).then_inc(sem("g_e"), 1)
                    act.activation(W[8][:, 0:S], tile(BC, i + GH * d), ACT.Exp, scale=-1.0).then_inc(sem("g_e"), 1)
                def high_qk(d):
                    n = 2 * i + d
                    act.wait_ge(sem("g_qk"), n * 2 + 1)
                    act.copy(QDH[d][:, :, 0:CH], W[7][:, 0:S].rearrange("p (n c) -> p n c", n=NCH)).then_inc(sem("gd_high"), 1)
                    if d == 1:
                        act.wait_ge(sem("g_scores"), i * 2 + 1)
                    act.wait_ge(sem("g_qk"), n * 2 + 2)
                    act.copy(KIH[:, :], W[8][:, 0:S]).then_inc(sem("gd_high"), 1)
                def high_tail_keys(d):
                    act.wait_ge(sem("g_kt_t"), 2 * i + (d + 1))
                    act.copy(KTH[:, :], PS[:, 3, :]).then_inc(sem("gd_high"), 1)
                def high_states(d):
                    n = 2 * i + d
                    if d == 1 or later:
                        act.wait_ge(sem("g_inter"), n * 1)
                    for s in range(NCH - 1):
                        act.wait_ge(sem("g_st"), n * (NCH - 1) + (s + 1))
                        act.copy(SH[:, s, :], ST[s % 2][:, :]).then_inc(sem("g_state_high"), 1)
                if later:
                    act.wait_ge(sem("g_sc_low"), i * 1)
                else:
                    act.wait_ge(sem("g_cum"), 2 * GH)
                decays(0)
                if later:
                    gla_square(i - 1)
                high_qk(0)
                if later:
                    gla_high(i - 1)
                high_tail_keys(0)
                act.wait_ge(sem("gv_t"), i + 1)
                for b in range(2):
                    act.copy(VGH[:, 2 * b:2 * b + 2, :], PS[:, 4 + b, :].rearrange("p (t c) -> p t c", t=2)).then_inc(sem("gv_high"), 1)
                act.wait_ge(sem("gd_low"), i * 6 + 2)
                decays(1)
                high_qk(1)
                high_states(0)
                high_tail_keys(1)
                act.wait_ge(sem("g_sc"), i + 1)
                act.copy(SCH[:, :], W[7][:, 0:S]).then_inc(sem("g_sc_high"), 1)
                for u in range(2):
                    act.wait_ge(sem("g_read"), i * 6 + (5 + u))
                    act.activation(E[u][:, :], W[5 + u][:, 0:S], ACT.Exp, scale=-1.0).then_inc(sem("g_rexp"), 1)
                high_states(1)

            def swa(i):
                if isinstance(i, int) and i == 0:
                    act.wait_ge(sem("g_ylow"), 2 * GH)
                    for k in range(2):
                        act.dma_start(W[7 + k][:, 0:S], T["consts"][:, C_COS + k * S:C_COS + (k + 1) * S]).then_inc(sem("rope"), 16)
                def square(n):
                    act.wait_ge(sem("sw_read"), i * 6 + (n + 1))
                    act.activation(E[n % 2][:, :], W[(1, 9)[n % 2]][:, 0:S], ACT.Square).then_inc(sem("sw_sq"), 1)
                def head_rsqrt(n):
                    rsqrt(W[3][:, 0:S], W[2][:, 0:S], W[4][:, 0:S], sem("sw_v"), i * 5 + (n + 1), sem("sw_rr"))
                square(0)
                square(1)
                head_rsqrt(0)
                for n in range(5):
                    act.wait_ge(sem("sw_x"), i * 5 + (n + 1))
                    act.copy((SQH[n - 1] if n else SKH)[:, :], W[(1, 9)[n % 2]][:, 0:S]).then_inc(sem("sw_high"), 1)
                    if n < 4:
                        head_rsqrt(n + 1)
                    if n < 3:
                        square(n + 2)
                act.wait_ge(sem("sv_t"), i + 1)
                act.copy(SVH[:, :, :], PS[:, 6, :].rearrange("p (t c) -> p t c", t=TB)).then_inc(sem("sv_high"), 1)
                later = not isinstance(i, int) or i > 0
                def exps(q):
                    win, n = WIN[q], i * 4 * TB + 4 * q
                    if q >= 2:
                        act.wait_ge(sem("sw_pt"), i * SEEN[TB] + SEEN[q - 1])
                    elif later:
                        act.wait_ge(sem("sw_pt"), i * SEEN[TB])
                    for t in range(SWA_Q):
                        act.wait_ge(sem("sw_max"), n + (t + 1))
                        act.wait_ge(sem("prm_ready"), 3)
                        act.activation(SESK[q % 2][:, t:t + 1], column(SINK, i * SWA_Q + t), ACT.Exp,
                                       bias=SNEG[q % 2][:, t:t + 1]).then_inc(sem("sw_sink"), 1)
                        act.activation(SPROB[q % 2][t][:, 0:len(win) * P], PS[:, 4 + t, 0:len(win) * P], ACT.Exp,
                                       bias=SNEG[q % 2][:, t:t + 1], accum_out=SRS[q % 2][:, t:t + 1]).then_inc(sem("sw_exp"), 1)
                def scale(q):
                    act.wait_ge(sem("sw_rinv"), i * TB + (q + 1))
                    for t in range(SWA_Q):
                        pr = SPROB[q % 2][t][:, 0:len(WIN[q]) * P]
                        act.activation(pr, pr, ACT.Copy, scale=SINV[q % 2][:, t:t + 1]).then_inc(sem("sw_prob"), 1)
                exps(0)
                scale(0)
                for q in range(TB):
                    if q < TB - 1:
                        exps(q + 1)
                    for jj in range(len(WIN[q])):
                        k = SEEN[q] + jj
                        act.wait_ge(sem("sw_pt"), i * SEEN[TB] + (k + 1))
                        if later or k >= 2:
                            act.wait_ge(sem("sw_pv"), i * SEEN[TB] + (k - 1))
                        act.copy(SPH[k % 2][:, :], PS[:, jj, :]).then_inc(sem("sw_phigh"), 1)
                    if q < TB - 1:
                        scale(q + 1)
                    act.wait_ge(sem("sw_pv"), i * SEEN[TB] + SEEN[q + 1])
                    act.wait_ge(sem("prm_ready"), 3)
                    act.copy(window_out(YSH, i, q), PS[:, 3, :].rearrange("p (t c) -> p t c", t=SWA_Q)).then_inc(sem("sw_ohigh"), 1)

            def merge(i):
                for k in range(2):
                    act.wait_ge(sem("mg_read"), i * 4 + (k + 1))
                    act.activation(W[1 + k][:, 0:S], W[1 + k][:, 0:S], ACT.Sigmoid).then_inc(sem("mg_sig"), 1)
                act.wait_ge(sem("mg"), i + 1)
                act.wait_ge(sem("prm_ready"), 3)
                act.copy(tile(MGH, i), W[3][:, 0:S]).then_inc(sem("mg_high"), 1)

            act.dma_start(CST[:, :], T["consts"][:, 0:C_GF]).then_inc(sem("consts"), 16)
            act.wait_ge(sem("zeroed"), 1)
            for to, src in PARAM_DMAS(PROW, T):
                act.dma_start(to, src).then_inc(sem("params"), 16)
            act.dma_start(SINK[:, :], T["swa_sinks_2"][0].partition_broadcast(P)).then_inc(sem("sinks"), 16)
            residual("_x", 1, KT, [(XH, XL, R_ATTN)])
            norm("_x")
            def mix(i):
                act.wait_ge(sem("mix_bu"), i + 1)
                act.wait_ge(sem("prm_ready"), 3)
                act.copy(tile(BUH, i), W[4][:, 0:S]).then_inc(sem("mix_high"), 1)
            loop(act, KT, mix, steps)
            residual(0, 2, 4, [(XH, XL, R_FFN)])
            ffn(0, 0, True, [(XH, XL, R_ATTN + KT)])
            attention()
            residual(2, 2, 4, [(XH, XL, R_FFN + KT)])
            ffn(1, 2, True, [(XH, XL, R_MIX)])
            gates()
            gla(0)
            loop(act, GH, gla, steps, start=1)
            gla_square(GH - 1)
            gla_high(GH - 1)
            loop(act, SWA_GROUPS, swa, steps)
            loop(act, KT, merge, steps)
            residual(4, 2, 4, [(XH, XL, R_FFN2)])
            ffn(2, 4, False, [])

        @block.vector
        def _(dve):
            steps = Steps(dve, sem("dve_step"))
            link = steps.link

            def newton(v, r, rr, ready, value, out_, signal=None):
                dve.wait_ge(ready, value)
                link(dve.tensor_tensor(v, v, rr, ALU.mult))
                link(dve.tensor_scalar(v, v, -0.5, 1.5, ALU.mult, ALU.add))
                ins = dve.tensor_tensor(out_, r, v, ALU.mult)
                if signal is None:
                    link(ins)
                else:
                    ins.then_inc(signal, 1)

            def norm(n):
                dve.wait_ge(sem("nsum"), ORDER[n] + 1)
                dve.tensor_scalar(W[4][:, 0:S], PS[:, 7, :], 1.0 / D, EPS, ALU.mult, ALU.add).then_inc(sem("nv"), 1)
                newton(W[4][:, 0:S], W[5][:, 0:S], W[6][:, 0:S], sem("nrr"), ORDER[n] + 1, W[0][:, 0:S])

            def residual(n, iters, tpi, gains, take, ahead=False):
                def body(i):
                    for t in range(tpi):
                        m = i * tpi + t
                        if ahead and t == 0:
                            take(i, 0, 0).then_inc(sem("resid"), 1)
                        if ahead and t + 1 < tpi:
                            take(i, t + 1, m + 1).then_inc(sem("resid"), 1)
                        if not ahead:
                            take(i, t, m).then_inc(sem("resid"), 1)
                        if not gains:
                            continue
                        dve.wait_ge(sem("sq"), tiles(n) + m + 1)
                        sq, acc = W[2 + t % 2][:, 0:S], W[1][:, 0:S]
                        if isinstance(m, int) and m == 0:
                            dve.tensor_copy(acc, sq).then_inc(sem("acc"), 1)
                        else:
                            dve.wait_ge(sem("acc"), tiles(n) + m)
                            dve.tensor_tensor(acc, acc, sq, ALU.add).then_inc(sem("acc"), 1)
                        for g, (xh, xl, row) in enumerate(gains):
                            dve.wait_ge(sem("xhd"), tiles(n) + m + 1)
                            dve.scalar_tensor_tensor(tile(xl, m), tile(XT, m), column(PRM, m + row),
                                                     tile(xh, m).bitcast(F32), ALU.mult,
                                                     ALU.subtract).then_inc(sem("xld"), 1)
                loop(dve, iters, body, steps)

            def add_products(p, groups):
                def take(i, t, m):
                    dve.wait_ge(unit_done, p.unit(i, t * groups + groups - 1) + 1)
                    return dve.tensor_tensor(tile(XT, m), PS[:, t % 2, :], tile(XT, m), ALU.add)
                return take

            def conv(x, o, w):
                link(dve.tensor_scalar(o, x[:, 0:S], w[0], None, ALU.mult))
                link(dve.scalar_tensor_tensor(o, x[:, 1:S + 1], w[1], o, ALU.mult, ALU.add))
                return dve.scalar_tensor_tensor(o, x[:, 2:S + 2], w[2], o, ALU.mult, ALU.add)

            def ffn(l, n, with_conv, gains):
                pu, pd = ph[f"up{l}"], ph[f"down{l}"]
                norm(n)
                for q in range(2):
                    link(dve.memset(W[1 + q][:, 0:2], 0.0))
                def body(i):
                    for q in range(2):
                        m = 2 * i + q
                        a, u, g = W[1 + q], W[3 + q][:, 0:S], W[5 + q][:, 0:S]
                        dve.wait_ge(unit_done, pu.unit(i, 2 * q) + 1)
                        dve.tensor_tensor(a[:, 2:S + 2] if with_conv else u, PS[:, 2 * q, :], W[0][:, 0:S],
                                          ALU.mult).then_inc(sem("ffn_a"), 1)
                        if with_conv:
                            dve.wait_ge(sem("ffn_a"), m + l * FT + 1)
                            conv(a, u, [column(FC, m + (l * 3 + k) * FT) for k in range(3)]).then_inc(sem("ffn_u"), 1)
                        dve.wait_ge(unit_done, pu.unit(i, 2 * q + 1) + 1)
                        dve.tensor_tensor(g, PS[:, 2 * q + 1, :], W[0][:, 0:S], ALU.mult).then_inc(sem("ffn_g"), 1)
                        dve.wait_ge(sem("ffn_g"), m + l * FT + 1)
                        dve.wait_ge(sem("ffn_silu"), m + l * FT + 1)
                        dve.tensor_tensor(g, g, u, ALU.mult).then_inc(sem("ffn_h"), 1)
                        dve.wait_ge(sem("ffn_high"), m + l * FT + 1)
                        dve.tensor_tensor(tile(HL, m), g, tile(HH, m).bitcast(F32), ALU.subtract).then_inc(sem("ffn_low"), 1)
                loop(dve, FT // 2, body, steps)
                residual(n + 1, KT // 2, 2, gains, add_products(pd, 3))

            def softmax(b, h):
                H = 2 * b + h
                if h == 0:
                    dve.wait_ge(sem("cums_loaded"), 32 * b + 32)
                if not isinstance(b, int) or H > 0:
                    dve.wait_ge(sem("prob_t"), H * TB)
                for k, q in enumerate(QB):
                    n = (q + 1) * P
                    pr = PROB[q][:, 0:n]
                    dve.wait_ge(sem("scores"), H * TB + (k + 1))
                    ci = CT[:, q, H:H + 1] if isinstance(b, int) else CT[:, q, bass.ds(H, 1)]
                    dve.scalar_tensor_tensor(pr, PS[:, 4 + q, 0:n], ci, W[8 + h][:, 0:n], ALU.add,
                                             ALU.subtract).then_inc(sem("scores_read"), 1)
                    dve.wait_ge(sem("scores_read"), H * TB + (k + 1))
                    dve.tensor_reduce(NEGM[:, q:q + 1], pr, AX.X, ALU.max, negate=True).then_inc(sem("score_max"), 1)
                for k, q in enumerate(QB):
                    dve.wait_ge(sem("exp"), H * TB + (k + 1))
                    dve.reciprocal(RINV[:, q:q + 1], RS[:, q:q + 1]).then_inc(sem("rinv"), 1)

            def low_probs(b, h):
                H = 2 * b + h
                for j in range(TB):
                    n = (TB - j) * P
                    dve.wait_ge(sem("pt_high"), H * TB + (j + 1))
                    dve.tensor_tensor(PTL[j][:, 0:n], PS[:, 4 + j, 0:n], PTH[j][:, 0:n].bitcast(F32),
                                      ALU.subtract).then_inc(sem("pt_low"), 1)

            def take_out(b, h):
                H = 2 * b + h
                r = slice(HD * h, HD * h + HD)
                dve.wait_ge(sem("weighed"), H * TB + TB)
                dve.tensor_tensor(W[6][r, 0:S], PS[r, 2, :], W[6][r, 0:S], ALU.mult).then_inc(sem("o_read"), 1)

            def low_out(b):
                dve.wait_ge(sem("o_high"), b + 1)
                dve.tensor_tensor(tile(OL, b), W[6][:, 0:S], tile(OH, b).bitcast(F32), ALU.subtract).then_inc(sem("o_low"), 1)

            def head_var(n):
                dve.wait_ge(sem("hn_sum"), n + 1)
                dve.tensor_scalar(W[3][:, 0:S], PS[:, 3, :], 1.0 / HD, EPS, ALU.mult, ALU.add).then_inc(sem("hn_v"), 1)

            def head_norm(n, gain):
                newton(W[3][:, 0:S], W[2][:, 0:S], W[4][:, 0:S], sem("hn_rr"), n + 1, W[4][:, 0:S])
                dve.scalar_tensor_tensor(W[1][:, 0:S], W[1][:, 0:S], PRM[:, gain:gain + 1], W[4][:, 0:S],
                                         ALU.mult, ALU.mult).then_inc(sem("hn_x"), 1)

            def head_low(n, high, low):
                dve.wait_ge(sem("hn_high"), n + 1)
                dve.tensor_tensor(low[:, :], W[1][:, 0:S], high[:, :].bitcast(F32), ALU.subtract).then_inc(sem("hn_low"), 1)

            def attention():
                for m in range(KT):
                    dve.wait_ge(sem("x2_high"), m + 1)
                    dve.scalar_tensor_tensor(X2L[:, m, :], XT[:, m, :], PRM[:, R_KV + m:R_KV + m + 1],
                                             X2H[:, m, :].bitcast(F32), ALU.mult, ALU.subtract).then_inc(sem("x2_low"), 1)
                norm(1)
                dve.wait_ge(unit_done, ph["forget"].unit(0, 0) + 1)
                link(dve.tensor_tensor(W[1][:, 0:S], PS[:, 4, :], W[0][:, 0:S], ALU.mult))
                dve.tensor_scalar(W[1][:, 0:S], W[1][:, 0:S], PRM[:, R_BF:R_BF + 1], None, ALU.add).then_inc(sem("fg_z"), 1)
                link(dve.memset(W[5][:, 0:S], 1.0))
                dve.wait_ge(sem("fg_sp"), 1)
                link(dve.scalar_tensor_tensor(W[3][:, 0:S], W[1][:, 0:S], 0.0, W[2][:, 0:S], ALU.min, ALU.subtract))
                dve.tensor_tensor_scan(W[4][:, 0:S], W[5][:, 0:S], W[3][:, 0:S], 0.0, ALU.mult, ALU.add).then_inc(sem("fg_c"), 1)
                dve.wait_ge(sem("fg_t"), 1)
                dve.tensor_copy(CT[:, :, :], PS[:, 5, :].rearrange("p (t c) -> p t c", t=TB)[:, :, P - HEADS:P]).then_inc(sem("fg_ct"), 1)
                dve.wait_ge(sem("fg_ct"), 1)
                p = ph["attn"]
                def read(i, j, w, name, n):
                    dve.wait_ge(unit_done, p.unit(i, j) + 1)
                    if j == 2 or (j == 0 and not (isinstance(i, int) and i == 0)):
                        dve.wait_ge(sem("hn_low"), i * 2 + j // 2)
                    if j == 3 and not (isinstance(i, int) and i == 0):
                        dve.wait_ge(sem("o_low"), i * 1)
                    dve.tensor_tensor(W[w][:, 0:S], PS[:, j % 2, :], W[0][:, 0:S], ALU.mult).then_inc(sem(name), 1)
                def body(i):
                    first = isinstance(i, int) and i == 0
                    if first:
                        dve.wait_ge(sem("cums_stored"), 16)
                    read(i, 0, 1, "kq_read", i * 2)
                    if not first:
                        softmax(i - 1, 0)
                    read(i, 1, 5, "vg_read", i * 2)
                    head_var(i * 2)
                    if not first:
                        low_probs(i - 1, 0)
                    head_norm(i * 2, R_KN)
                    if not first:
                        take_out(i - 1, 0)
                        softmax(i - 1, 1)
                    head_low(i * 2, KH, KL)
                    read(i, 2, 1, "kq_read", i * 2 + 1)
                    head_var(i * 2 + 1)
                    if not first:
                        low_probs(i - 1, 1)
                    head_norm(i * 2 + 1, R_QN)
                    if not first:
                        take_out(i - 1, 1)
                        low_out(i - 1)
                    head_low(i * 2 + 1, QH, QL)
                    read(i, 3, 6, "vg_read", i * 2 + 1)
                    dve.wait_ge(sem("g_exp"), i + 1)
                    link(dve.tensor_scalar(W[6][:, 0:S], W[6][:, 0:S], 1.0, None, ALU.add))
                    link(dve.reciprocal(W[6][:, 0:S], W[6][:, 0:S]))
                    dve.wait_ge(sem("v_high"), i + 1)
                    dve.tensor_tensor(VL[:, :, :], PS[:, 3, :].rearrange("p (t c) -> p t c", t=TB),
                                      VH[:, :, :].bitcast(F32), ALU.subtract).then_inc(sem("v_low"), 1)
                body(0)
                loop(dve, PAIRS, body, steps, start=1)
                for h in range(2):
                    softmax(PAIRS - 1, h)
                    low_probs(PAIRS - 1, h)
                    take_out(PAIRS - 1, h)
                low_out(PAIRS - 1)

            def gates():
                dve.memset(UP[:, :], 0.0).then_inc(sem("up_zeroed"), 1)
                for d in range(2):
                    dve.memset(QDH[d][:, :, CH:2 * CH].bitcast(F32), 0.0)
                    link(dve.memset(QDL[d][:, :, CH:2 * CH].bitcast(F32), 0.0))
                norm(3)
                dve.wait_ge(unit_done, ph["lr"].unit(0, 0) + 1)
                r = slice(0, 2 * GATE_RANK)
                dve.tensor_tensor(W[1][r, 0:S], PS[r, 0, :], W[0][r, 0:S], ALU.mult).then_inc(sem("lr"), 1)
                link(dve.memset(W[7][:, 0:S], 1.0))
                link(dve.memset(W[7][:, 0:S:CH], 0.0))
                def cumulate(t):
                    z, sp, lg = W[2 + t % 2][:, 0:S], W[4 + t % 2][:, 0:S], W[6][:, 0:S]
                    dve.wait_ge(sem("z_sp"), t + 1)
                    link(dve.scalar_tensor_tensor(lg, z, 0.0, sp, ALU.min, ALU.subtract))
                    link(dve.tensor_scalar(lg, lg, 1.0 / 16.0, -0.5, ALU.mult, ALU.max))
                    o = BC[:, t, :]
                    if t >= GH:
                        lg, o = lg[:, ::-1], o[:, ::-1]
                    dve.tensor_tensor_scan(o, W[7][:, 0:S], lg, 0.0, ALU.mult, ALU.add).then_inc(sem("g_cum"), 1)
                    dve.wait_ge(sem("g_cum"), t + 1)
                for t in range(2 * GH):
                    dve.wait_ge(sem("z"), t + 1)
                    dve.tensor_scalar(W[2 + t % 2][:, 0:S], PS[:, 6 + t % 2, :], PRM[:, R_GBF + t:R_GBF + t + 1], None,
                                      ALU.add).then_inc(sem("z_read"), 1)
                    if t > 0:
                        cumulate(t - 1)
                cumulate(2 * GH - 1)
                dve.wait_ge(sem("g_masks"), 16)

            def gla_norm(i):
                dve.wait_ge(sem("g_sq"), i * TB + TB)
                dve.tensor_scalar(GSS[:, :], GSS[:, :], 1.0 / (2 * P), EPS, ALU.mult, ALU.add).then_inc(sem("g_nv"), 1)
                newton(GSS[:, :], GR[:, :], GRR[:, :], sem("g_nrr"), i + 1, GRR[:, :])
                dve.wait_ge(sem("g_silu"), i + 1)
                for b in range(TB):
                    dve.tensor_scalar(ON[:, b, :], gla_out(b), GRR[:, b:b + 1], None, ALU.mult).then_inc(sem("g_on"), 1)

            def gla_gate(i):
                dve.wait_ge(sem("g_ot"), i + 1)
                for u in range(2):
                    dve.scalar_tensor_tensor(W[3 + u][:, 0:S], PS[:, (3, 5)[u], :], PRM[:, R_OUTG + u:R_OUTG + u + 1],
                                             W[5 + u][:, 0:S], ALU.mult, ALU.mult).then_inc(sem("g_y"), 1)
                for u in range(2):
                    dve.wait_ge(sem("g_yhigh"), i * 2 + (u + 1))
                    dve.tensor_tensor(tile(YGL, i * 2 + u), W[3 + u][:, 0:S], tile(YGH, i * 2 + u).bitcast(F32),
                                      ALU.subtract).then_inc(sem("g_ylow"), 1)

            def gla(i):
                p = ph["gla"]
                later = not isinstance(i, int) or i > 0
                w7, w8 = W[7][:, 0:S], W[8][:, 0:S]
                def read(j):
                    dve.wait_ge(unit_done, p.unit(i, j) + 1)
                    bank = PS[:, (2, 4, 0, 1, 6, 7)[j], :]
                    if j == 0:
                        ins = dve.scalar_tensor_tensor(W[1][:, 0:S], bank, GDK ** -0.5, W[0][:, 0:S], ALU.mult, ALU.mult)
                    else:
                        ins = dve.tensor_tensor(W[1 + j][:, 0:S], bank, W[0][:, 0:S], ALU.mult)
                    ins.then_inc(sem("g_read"), 1)
                def decay(d):
                    n = 2 * i + d
                    dve.wait_ge(sem("g_e"), n * 2 + 2)
                    link(dve.tensor_copy(EBL[d], W[7][:, CH - 1:S:CH] if d == 0 else W[7][:, 0:S:CH]))
                    dve.wait_ge(sem("g_read"), i * 6 + 2)
                    dve.tensor_tensor(w7, W[1][:, 0:S], w7, ALU.mult).then_inc(sem("g_qk"), 1)
                    dve.tensor_tensor(w8, W[2][:, 0:S], w8, ALU.mult).then_inc(sem("g_qk"), 1)
                    dve.wait_ge(sem("gd_high"), n * 3 + 1)
                    dve.tensor_tensor(QDL[d][:, :, 0:CH], w7.rearrange("p (n c) -> p n c", n=NCH),
                                      QDH[d][:, :, 0:CH].bitcast(F32), ALU.subtract).then_inc(sem("gd_low"), 1)
                    dve.wait_ge(sem("gd_high"), n * 3 + 2)
                    dve.tensor_tensor(KIL[:, :], w8, KIH[:, :].bitcast(F32), ALU.subtract).then_inc(sem("gd_low"), 1)
                    dve.wait_ge(sem("gd_low"), n * 3 + 2)
                    dve.tensor_tensor(w8.rearrange("p (n c) -> p n c", n=NCH), w8.rearrange("p (n c) -> p n c", n=NCH),
                                      EBL[d].unsqueeze(2).to_broadcast([P, NCH, CH]), ALU.mult).then_inc(sem("g_kt"), 1)
                def masked_scores(d, to):
                    dve.wait_ge(sem("g_scores"), i * 2 + (d + 1))
                    return dve.tensor_tensor(to.rearrange("p (t c) -> p t c", t=TB),
                                             PS[:, 2, :].rearrange("p (t c) -> p t c", t=TB),
                                             GMASK[d].unsqueeze(1).to_broadcast([P, TB, P]), ALU.mult)
                def low_tail_keys(d):
                    dve.wait_ge(sem("gd_high"), (2 * i + d) * 3 + 3)
                    dve.tensor_tensor(KTL[:, :], PS[:, 3, :], KTH[:, :].bitcast(F32), ALU.subtract).then_inc(sem("gd_low"), 1)
                def states(d):
                    n = 2 * i + d
                    def low_state(s):
                        dve.wait_ge(sem("g_state_high"), n * (NCH - 1) + (s + 1))
                        dve.tensor_tensor(SL[:, s, :], ST[s % 2][:, :], SH[:, s, :].bitcast(F32),
                                          ALU.subtract).then_inc(sem("g_state_low"), 1)
                    for s, c in enumerate(chunk_order(d)):
                        bank, cols = kv_place(c)
                        dve.wait_ge(sem("g_kv"), n * (NCH - 1) + (4 if s < 4 else NCH - 1))
                        if s >= 2:
                            dve.wait_ge(sem("g_state_low"), n * (NCH - 1) + (s - 1))
                        elif d == 1 or later:
                            dve.wait_ge(sem("g_state_low"), n * (NCH - 1))
                        if s == 0:
                            ins = dve.tensor_copy(ST[0][:, :], PS[:, bank, cols])
                        else:
                            dve.wait_ge(sem("g_st"), n * (NCH - 1) + s)
                            ins = dve.scalar_tensor_tensor(ST[s % 2][:, :], ST[(s + 1) % 2][:, :], EBL[d][:, c:c + 1],
                                                           PS[:, bank, cols], ALU.mult, ALU.add)
                        ins.then_inc(sem("g_st"), 1)
                        if s > 0:
                            low_state(s - 1)
                    low_state(NCH - 2)
                if later:
                    gla_norm(i - 1)
                read(0)
                read(1)
                decay(0)
                if later:
                    gla_gate(i - 1)
                    dve.wait_ge(sem("g_ylow"), i * 2)
                read(2)
                read(3)
                masked_scores(0, SC0[:, :]).then_inc(sem("g_sc0"), 1)
                low_tail_keys(0)
                for b in range(2):
                    dve.wait_ge(sem("gv_high"), i * 2 + (b + 1))
                    dve.tensor_tensor(VGL[:, 2 * b:2 * b + 2, :], PS[:, 4 + b, :].rearrange("p (t c) -> p t c", t=2),
                                      VGH[:, 2 * b:2 * b + 2, :].bitcast(F32), ALU.subtract).then_inc(sem("gv_low"), 1)
                read(4)
                decay(1)
                states(0)
                read(5)
                link(masked_scores(1, w7))
                dve.wait_ge(sem("g_sc0"), i + 1)
                dve.tensor_tensor(w7, w7, SC0[:, :], ALU.add).then_inc(sem("g_sc"), 1)
                low_tail_keys(1)
                dve.wait_ge(sem("g_sc_high"), i + 1)
                dve.tensor_tensor(SCL[:, :], w7, SCH[:, :].bitcast(F32), ALU.subtract).then_inc(sem("g_sc_low"), 1)
                states(1)
                for u in range(2):
                    r, e = W[5 + u][:, 0:S], E[u][:, :]
                    dve.wait_ge(sem("g_rexp"), i * 2 + (u + 1))
                    link(dve.tensor_scalar(e, e, 1.0, None, ALU.add))
                    link(dve.reciprocal(e, e))
                    ins = dve.tensor_tensor(r, r, e, ALU.mult)
                    if u == 0:
                        link(ins)
                    else:
                        ins.then_inc(sem("g_silu"), 1)

            def swa(i):
                p = ph["swa"]
                if isinstance(i, int) and i == 0:
                    dve.wait_ge(sem("rope"), 32)
                    dve.wait_ge(sem("sinks"), 16)
                later = not isinstance(i, int) or i > 0
                w = [W[k][:, 0:S] for k in range(10)]
                def read(j):
                    dve.wait_ge(unit_done, p.unit(i, j) + 1)
                    if j >= 2:
                        dve.wait_ge(sem("sw_low"), i * 5 + (j - 1))
                    dve.tensor_tensor(w[(1, 9)[j % 2]], PS[:, j % 4, :], w[0], ALU.mult).then_inc(sem("sw_read"), 1)
                def rotate(n):
                    x, y = W[(1, 9)[n % 2]], W[(5, 6)[n % 2]]
                    gain = R_SQG if n else R_SKG
                    dve.wait_ge(sem("sw_read"), i * 6 + (n + 1))
                    dve.scalar_tensor_tensor(y[:, 0:S], x[:, 0:S], PRM[:, gain:gain + 1], w[7], ALU.mult, ALU.mult)
                    for a, b in ((slice(0, 64), slice(64, 128)), (slice(64, 128), slice(0, 64))):
                        ins = dve.scalar_tensor_tensor(SROT[b, :], x[a, 0:S], PRM[a, gain:gain + 1], W[8][a, 0:S],
                                                       ALU.mult, ALU.mult)
                    link(ins)
                    link(dve.tensor_tensor(y[:, 0:S], y[:, 0:S], SROT[:, :], ALU.add))
                def variance(n):
                    dve.wait_ge(sem("sw_sum"), i * 5 + (n + 1))
                    dve.tensor_scalar(w[3], PS[:, 4 + n % 2, :], 1.0 / P, EPS, ALU.mult, ALU.add).then_inc(sem("sw_v"), 1)
                read(0)
                rotate(0)
                read(1)
                variance(0)
                for n in range(5):
                    if n < 4:
                        rotate(n + 1)
                    x, y = w[(1, 9)[n % 2]], w[(5, 6)[n % 2]]
                    newton(w[3], w[2], w[4], sem("sw_rr"), i * 5 + (n + 1), w[4])
                    dve.tensor_tensor(x, y, w[4], ALU.mult).then_inc(sem("sw_x"), 1)
                    if n < 4:
                        variance(n + 1)
                    dve.wait_ge(sem("sw_high"), i * 5 + (n + 1))
                    high, low = (SQH[n - 1], SQL[n - 1]) if n else (SKH, SKL)
                    dve.tensor_tensor(low[:, :], x, high[:, :].bitcast(F32), ALU.subtract).then_inc(sem("sw_low"), 1)
                    if n < 4:
                        read(n + 2)
                dve.wait_ge(sem("sv_high"), i + 1)
                dve.tensor_tensor(SVL[:, :, :], PS[:, 6, :].rearrange("p (t c) -> p t c", t=TB),
                                  SVH[:, :, :].bitcast(F32), ALU.subtract).then_inc(sem("sv_low"), 1)
                def softmax(q):
                    win, n = WIN[q], i * 4 * TB + 4 * q
                    for t in range(SWA_Q):
                        dve.wait_ge(sem("sw_scores"), n + (t + 1))
                        link(dve.tensor_reduce(SMAX[:, t:t + 1], PS[:, 4 + t, 0:len(win) * P], AX.X, ALU.max))
                        dve.tensor_scalar(SNEG[q % 2][:, t:t + 1], SMAX[:, t:t + 1], column(SINK, i * SWA_Q + t), -1.0,
                                          ALU.max, ALU.mult).then_inc(sem("sw_max"), 1)
                    dve.wait_ge(sem("sw_exp"), n + 4)
                    link(dve.tensor_tensor(SINV[q % 2][:, :], SRS[q % 2][:, :], SESK[q % 2][:, :], ALU.add))
                    dve.reciprocal(SINV[q % 2][:, :], SINV[q % 2][:, :]).then_inc(sem("sw_rinv"), 1)
                softmax(0)
                for q in range(TB):
                    if q < TB - 1:
                        softmax(q + 1)
                    for jj in range(len(WIN[q])):
                        k = SEEN[q] + jj
                        dve.wait_ge(sem("sw_phigh"), i * SEEN[TB] + (k + 1))
                        dve.tensor_tensor(SPL[k % 2][:, :], PS[:, jj, :], SPH[k % 2][:, :].bitcast(F32),
                                          ALU.subtract).then_inc(sem("sw_plow"), 1)
                    dve.wait_ge(sem("sw_ohigh"), i * TB + (q + 1))
                    dve.tensor_tensor(window_out(YSL, i, q), PS[:, 3, :].rearrange("p (t c) -> p t c", t=SWA_Q),
                                      window_out(YSH, i, q).bitcast(F32), ALU.subtract).then_inc(sem("sw_out"), 1)

            def merge(i):
                p = ph["merge"]
                for k in range(2):
                    dve.wait_ge(unit_done, p.unit(i, k) + 1)
                    dve.tensor_tensor(W[1 + k][:, 0:S], PS[:, k, :], W[0][:, 0:S], ALU.mult).then_inc(sem("mg_read"), 1)
                for k in range(2):
                    dve.wait_ge(unit_done, p.unit(i, 2 + k) + 1)
                    dve.wait_ge(sem("mg_sig"), i * 2 + (k + 1))
                    dve.tensor_tensor(W[3 + k][:, 0:S], PS[:, 2 + k, :], W[1 + k][:, 0:S], ALU.mult).then_inc(sem("mg_read"), 1)
                dve.wait_ge(sem("mg_read"), i * 4 + 4)
                dve.tensor_tensor(W[3][:, 0:S], W[3][:, 0:S], W[4][:, 0:S], ALU.add).then_inc(sem("mg"), 1)
                dve.wait_ge(sem("mg_high"), i + 1)
                dve.tensor_tensor(tile(MGL, i), W[3][:, 0:S], tile(MGH, i).bitcast(F32), ALU.subtract).then_inc(sem("mg_low"), 1)

            link(dve.memset(PROW[:, :, :], 0.0))
            dve.memset(EPSC, EPS)
            dve.memset(ONEC, 1.0).then_inc(sem("zeroed"), 1)
            dve.wait_ge(sem("consts"), 16)
            for to, c in ((IDF, C_ID), (ONE, C_ONE), (ONE64, C_ONE64), (IDB, C_ID), (MCAUSAL, C_CAUSAL), (MUPPER, C_UPPER)):
                ins = dve.tensor_copy(to[:, :], CST[:, c:c + P])
            ins.then_inc(sem("prm_ready"), 1)
            dve.wait_ge(sem("prm_t"), 1)
            dve.tensor_copy(PRM[:, :], PS[:, 2, 0:N_PRM])
            link(dve.tensor_copy(FC[:, 0:N_FC], PS[:, 2, P:P + N_FC]))
            dve.tensor_copy(FC[:, N_FC:2 * N_FC], PS[:, 2, 2 * P:2 * P + N_FC]).then_inc(sem("prm_ready"), 1)
            dve.tensor_scalar(PRM[:, R_QN:R_QN + 1], PRM[:, R_QN:R_QN + 1], HD ** -0.5, None, ALU.mult)
            dve.tensor_scalar(PRM[:, R_SQG:R_SQG + 1], PRM[:, R_SQG:R_SQG + 1], 128 ** -0.5, None,
                              ALU.mult).then_inc(sem("prm_ready"), 1)
            dve.wait_ge(sem("prm_ready"), 3)

            def take_x(i, t, m):
                dve.wait_ge(sem("xt"), m + 1)
                return dve.tensor_copy(XT[:, m, :], PS[:, m % 2, :])
            residual("_x", 1, KT, [(XH, XL, R_ATTN)], take_x, ahead=True)
            norm("_x")
            link(dve.memset(W[1][:, 0:2], 0.0))
            p = ph["mix"]
            def mix(i):
                dve.wait_ge(unit_done, p.unit(i, 0) + 1)
                dve.tensor_tensor(W[5][:, 0:S], PS[:, 0, :], W[0][:, 0:S], ALU.mult).then_inc(sem("mix_c"), 1)
                dve.wait_ge(unit_done, p.unit(i, 1) + 1)
                dve.tensor_tensor(W[6][:, 0:S], PS[:, 1, :], W[0][:, 0:S], ALU.mult).then_inc(sem("mix_h"), 1)
                dve.wait_ge(sem("mix_h"), i + 1)
                link(dve.tensor_tensor(W[1][:, 2:S + 2], W[5][:, 0:S], W[6][:, 0:S], ALU.mult))
                link(conv(W[1], W[3][:, 0:S], [column(PRM, i + R_ACONV + k * KT) for k in range(3)]))
                dve.wait_ge(unit_done, p.unit(i, 2) + 1)
                dve.tensor_tensor(W[5][:, 0:S], PS[:, 2, :], W[0][:, 0:S], ALU.mult).then_inc(sem("mix_b"), 1)
                dve.wait_ge(sem("mix_b"), i + 1)
                dve.tensor_tensor(W[4][:, 0:S], W[5][:, 0:S], W[3][:, 0:S], ALU.mult).then_inc(sem("mix_bu"), 1)
                dve.wait_ge(sem("mix_high"), i + 1)
                dve.tensor_tensor(tile(BUL, i), W[4][:, 0:S], tile(BUH, i).bitcast(F32), ALU.subtract).then_inc(sem("mix_low"), 1)
            loop(dve, KT, mix, steps)
            residual(0, 2, 4, [(XH, XL, R_FFN)], add_products(ph["mix_out"], 1))
            ffn(0, 0, True, [(XH, XL, R_ATTN + KT)])
            attention()
            residual(2, 2, 4, [(XH, XL, R_FFN + KT)], add_products(ph["attn_out"], 1))
            ffn(1, 2, True, [(XH, XL, R_MIX)])
            gates()
            gla(0)
            loop(dve, GH, gla, steps, start=1)
            gla_norm(GH - 1)
            gla_gate(GH - 1)
            loop(dve, SWA_GROUPS, swa, steps)
            loop(dve, KT, merge, steps)
            residual(4, 2, 4, [(XH, XL, R_FFN2)], add_products(ph["out2"], 1))
            ffn(2, 4, False, [])
            for t in range(TB):
                for h in range(2):
                    n = 2 * t + h
                    dve.wait_ge(sem("out_t"), n + 1)
                    dve.tensor_copy(XIN[:, t, h * S:(h + 1) * S], PS[:, 2 + n % 2, :]).then_inc(sem("out_rows"), 1)


def PARAM_DMAS(PROW, T):
    def tall(a):
        return a.rearrange("(k p) -> k p", p=P)

    def all_tall(a):
        return a.rearrange("l (k p) -> (l k) p", p=P)
    d = []
    for row, a in ((R_ATTN, T["attn_norm"]), (R_FFN, T["ffn_norm"]), (R_ACONV, T["a_conv"][0])):
        n = a.shape[0] * a.shape[1] // P
        d.append((PROW[row:row + n, 0, :], all_tall(a)))
    for row, a in ((R_KV, T["kv_norm"]), (R_MIX, T["norm_mix_g_2"][0]),
                   (R_FFN2, T["norm_ffn_g_2"][0]), (R_GBF, T["gla_gate_bias_fwd_2"][0]),
                   (R_GBB, T["gla_gate_bias_bwd_2"][0]), (R_OUTG, T["gla_out_norm_g_2"][0]),
                   (R_SQG, T["swa_q_norm_g_2"][0]), (R_SKG, T["swa_k_norm_g_2"][0])):
        n = a.shape[0] // P
        d.append((PROW[row:row + n, 0, :], tall(a)))
    for row, a in ((R_QN, T["q_norm"][0]), (R_KN, T["k_norm"])):
        for h in range(2):
            d.append((PROW[row:row + 1, 0, h * HD:(h + 1) * HD], a.rearrange("(k p) -> k p", p=HD)))
    d.append((PROW[R_BF:R_BF + 1, 0, P - HEADS:P], T["b_f"].rearrange("(k p) -> k p", p=HEADS)))
    for l in range(2):
        d.append((PROW[0:3 * FT, 1 + l, :], all_tall(T["ffn_conv"][l])))
    return d


N_PARAM_DMAS = 3 + 8 + 4 + 1 + 2


def constants():
    c = np.zeros((P, N_CONST), np.float32)
    r = np.arange(P)
    row, column = r[:, None], r[None, :]
    c[:, C_ID:C_ID + P] = np.eye(P)
    c[:, C_ONE:C_ONE + P] = 1.0
    c[:, C_ONE64:C_ONE64 + P] = row // HD == column // HD
    c[:, C_CAUSAL:C_CAUSAL + P] = np.where(column <= row, 0.0, NEG)
    c[:, C_UPPER:C_UPPER + P] = np.where(column >= row, 0.0, NEG)
    same = row // CH == column // CH
    c[:, C_GF:C_GF + P] = same & (row <= column)
    c[:, C_GB:C_GB + P] = same & (row > column)
    half = P // 2
    inv = (np.float32(10000.0) ** (-np.arange(half, dtype=np.float32) / np.float32(half))).astype(np.float32)
    ang = np.concatenate([inv, inv])[:, None] * np.arange(S, dtype=np.float32)[None, :]
    c[:, C_COS:C_COS + S] = np.cos(ang)
    c[:, C_SIN:C_SIN + S] = np.where(row < half, 1.0, -1.0) * np.sin(ang)
    return c


def kernel(**inputs):
    import concourse.bacc as bacc
    from concourse.bass_utils import run_bass_kernel_spmd as run

    nc = bacc.Bacc("TRN2", target_bir_lowering=False, num_devices=1)
    arrays, T = {}, {}
    for name, a in {**inputs, "consts": constants()}.items():
        a = np.ascontiguousarray(a)
        arrays[f"in_{name}"] = a
        T[name] = nc.dram_tensor(f"in_{name}", a.shape, F32, kind="ExternalInput").ap()
    out = nc.dram_tensor("out", (1, S, D), F32, kind="ExternalOutput").ap()
    build(nc, T, out)
    r = run(nc, [arrays], core_ids=[0])
    return r.results[0]["out"]
```
